# Optimizing a Trainium2 kernel written in Bass

```python
import math
import jax, jax.numpy as jnp
from jax import lax
import numpy as np

D_MODEL = 2048
BATCH = 1
SEQ = 256
DEPTH = 2

N_A = DEPTH // 2
N_B = DEPTH - N_A

POOL_WINDOWS = (2, 4, 8, 16)
N_POOL_GROUPS = len(POOL_WINDOWS)
POOL_GROUP = D_MODEL // N_POOL_GROUPS

N_HEADS = 16
QK_NOPE_DIM = 128
QK_ROPE_DIM = 64
QK_DIM = QK_NOPE_DIM + QK_ROPE_DIM
V_DIM = 128
Q_LORA_RANK = 512
KV_LORA_RANK = 512
ROPE_BASE = 10000.0
ATTN_SCALE = 1.0 / math.sqrt(QK_DIM)
Q_BLOCK = 128

FFN_MULT = 256
D_FF = ((8 * D_MODEL + 3 * FFN_MULT - 1) // (3 * FFN_MULT)) * FFN_MULT

NORM_EPS = 1e-6
POS_OFFSET_MAX = 4096

kernel_name = "yoco_pool_mla_hybrid"

def rms_norm(x, g):
    xf = x.astype(jnp.float32)
    y = xf * lax.rsqrt(jnp.mean(xf * xf, axis=-1, keepdims=True) + NORM_EPS)
    return (y * g.astype(jnp.float32)).astype(x.dtype)

def swiglu(h, w_gate, w_up, w_down):
    return (jax.nn.silu(h @ w_gate) * (h @ w_up)) @ w_down

def rope_tables(positions):
    half = QK_ROPE_DIM // 2
    inv_freq = ROPE_BASE ** (-jnp.arange(half, dtype=jnp.float32) / half)
    ang = positions.astype(jnp.float32)[..., None] * inv_freq
    return jnp.cos(ang), jnp.sin(ang)

def apply_rope(x, cos, sin):
    half = QK_ROPE_DIM // 2
    xf = x.astype(jnp.float32)
    x1, x2 = xf[..., :half], xf[..., half:]
    out = jnp.concatenate([x1 * cos - x2 * sin, x2 * cos + x1 * sin], axis=-1)
    return out.astype(x.dtype)

def multiscale_pool_mixer(h, pool_w, pool_scale):
    S = h.shape[1]
    hf = h.astype(jnp.float32)
    cs = jnp.cumsum(hf, axis=1)
    t = jnp.arange(S)
    outs = []
    for g, w in enumerate(POOL_WINDOWS):
        sl = slice(g * POOL_GROUP, (g + 1) * POOL_GROUP)
        c = cs[..., sl]
        c_prev = jnp.pad(c, ((0, 0), (w, 0), (0, 0)))[:, :S]
        count = jnp.minimum(t + 1, w).astype(jnp.float32)[None, :, None]
        diff = (c - c_prev) / count - hf[..., sl]
        outs.append(jnp.einsum('bsc,cd->bsd', diff.astype(h.dtype), pool_w[g]))
    return jnp.concatenate(outs, axis=-1) * pool_scale

def shared_mla_kv(h, w_kv_a, kv_latent_norm, w_kv_b, cos, sin):
    B, S, _ = h.shape
    kv = h @ w_kv_a
    c_kv = rms_norm(kv[..., :KV_LORA_RANK], kv_latent_norm)
    k_pe = apply_rope(kv[..., KV_LORA_RANK:], cos, sin)
    kv_up = (c_kv @ w_kv_b).reshape(B, S, N_HEADS, QK_NOPE_DIM + V_DIM)
    return kv_up[..., :QK_NOPE_DIM], k_pe, kv_up[..., QK_NOPE_DIM:]

def causal_mla_attention(q_nope, q_pe, k_nope, k_pe, v):
    S = q_nope.shape[1]
    outs = []
    for i in range(S // Q_BLOCK):
        s0, e = i * Q_BLOCK, (i + 1) * Q_BLOCK
        sc = (jnp.einsum('bqhd,bkhd->bhqk', q_nope[:, s0:e], k_nope[:, :e])
              + jnp.einsum('bqhr,bkr->bhqk', q_pe[:, s0:e], k_pe[:, :e]))
        sc = sc.astype(jnp.float32) * ATTN_SCALE
        mask = jnp.arange(e)[None, :] <= (s0 + jnp.arange(Q_BLOCK))[:, None]
        sc = jnp.where(mask, sc, -jnp.inf)
        p = jax.nn.softmax(sc, axis=-1).astype(v.dtype)
        outs.append(jnp.einsum('bhqk,bkhd->bqhd', p, v[:, :e]))
    return jnp.concatenate(outs, axis=1)

def mla_layer_mixer(h, w_q_a, q_latent_norm, w_q_b, w_o, k_nope, k_pe, v, cos, sin):
    B, S, _ = h.shape
    q = (rms_norm(h @ w_q_a, q_latent_norm) @ w_q_b).reshape(B, S, N_HEADS, QK_DIM)
    q_nope = q[..., :QK_NOPE_DIM]
    q_pe = apply_rope(q[..., QK_NOPE_DIM:], cos[:, :, None, :], sin[:, :, None, :])
    o = causal_mla_attention(q_nope, q_pe, k_nope, k_pe, v)
    return o.reshape(B, S, N_HEADS * V_DIM) @ w_o

def setup_inputs(seed: int = 0) -> dict:
    key = jax.random.key(seed)
    ks = jax.random.split(key, 24)
    f32 = jnp.float32

    def dense(k, shape, fan_in):
        return jax.random.normal(k, shape, f32) * (fan_in ** -0.5)

    def gain(k, shape):
        return 1.0 + 0.05 * jax.random.normal(k, shape, f32)

    x = jax.random.normal(ks[0], (BATCH, SEQ, D_MODEL), f32)
    positions = (jax.random.randint(ks[1], (BATCH, 1), 0, POS_OFFSET_MAX, dtype=jnp.int32)
                 + jnp.arange(SEQ, dtype=jnp.int32)[None, :])
    return {
        "x": x,
        "positions": positions,
        "pool_norm": gain(ks[2], (N_A, D_MODEL)),
        "pool_w": dense(ks[3], (N_A, N_POOL_GROUPS, POOL_GROUP, POOL_GROUP), POOL_GROUP),
        "pool_scale": gain(ks[4], (N_A, D_MODEL)),
        "kv_in_norm": gain(ks[5], (D_MODEL,)),
        "w_kv_a": dense(ks[6], (D_MODEL, KV_LORA_RANK + QK_ROPE_DIM), D_MODEL),
        "kv_latent_norm": gain(ks[7], (KV_LORA_RANK,)),
        "w_kv_b": dense(ks[8], (KV_LORA_RANK, N_HEADS * (QK_NOPE_DIM + V_DIM)), KV_LORA_RANK),
        "attn_norm": gain(ks[9], (N_B, D_MODEL)),
        "w_q_a": dense(ks[10], (N_B, D_MODEL, Q_LORA_RANK), D_MODEL),
        "q_latent_norm": gain(ks[11], (N_B, Q_LORA_RANK)),
        "w_q_b": dense(ks[12], (N_B, Q_LORA_RANK, N_HEADS * QK_DIM), Q_LORA_RANK),
        "w_o": dense(ks[13], (N_B, N_HEADS * V_DIM, D_MODEL), N_HEADS * V_DIM),
        "ffn_norm": gain(ks[14], (DEPTH, D_MODEL)),
        "w_gate": dense(ks[15], (DEPTH, D_MODEL, D_FF), D_MODEL),
        "w_up": dense(ks[16], (DEPTH, D_MODEL, D_FF), D_MODEL),
        "w_down": dense(ks[17], (DEPTH, D_FF, D_MODEL), D_FF),
        "final_norm": gain(ks[18], (D_MODEL,)),
    }

def reference(x, positions, pool_norm, pool_w, pool_scale, kv_in_norm, w_kv_a,
              kv_latent_norm, w_kv_b, attn_norm, w_q_a, q_latent_norm, w_q_b, w_o,
              ffn_norm, w_gate, w_up, w_down, final_norm):
    cos, sin = rope_tables(positions)
    k_nope = k_pe = v = None
    for l in range(DEPTH):
        if l == N_A:
            k_nope, k_pe, v = shared_mla_kv(rms_norm(x, kv_in_norm), w_kv_a,
                                            kv_latent_norm, w_kv_b, cos, sin)
        if l < N_A:
            x = x + multiscale_pool_mixer(rms_norm(x, pool_norm[l]), pool_w[l], pool_scale[l])
        else:
            b = l - N_A
            x = x + mla_layer_mixer(rms_norm(x, attn_norm[b]), w_q_a[b], q_latent_norm[b],
                                    w_q_b[b], w_o[b], k_nope, k_pe, v, cos, sin)
        x = x + swiglu(rms_norm(x, ffn_norm[l]), w_gate[l], w_up[l], w_down[l])
    return rms_norm(x, final_norm)


_drawn_inputs = setup_inputs


def setup_inputs(seed=0):
    import zlib

    import numpy as np

    out = dict(_drawn_inputs(seed))
    spreads = {}
    factors = {'kv_in_norm': 5.579, 'kv_latent_norm': 5.946, 'attn_norm': 8.0, 'q_latent_norm': 8.0}
    for name, (base, spread) in spreads.items():
        noise = np.random.default_rng([zlib.crc32(name.encode()), seed]).standard_normal(out[name].shape)
        drawn = base * np.exp(spread * noise) if base else spread * noise
        out[name] = __import__('jax').numpy.asarray(drawn.astype(out[name].dtype))
    for name, factor in factors.items():
        out[name] = (out[name] * factor).astype(out[name].dtype)
    return out
```

```python
from contextlib import ExitStack

import numpy as np
import concourse.bass as bass
from concourse import mybir

F32 = mybir.dt.float32
F32R = mybir.dt.float32r
I32 = mybir.dt.int32
ALU = mybir.AluOpType
ACT = mybir.ActivationFunctionType

P = 128
SEQ = 256
D_MODEL = 2048
D_FF = 5632
WINDOWS = (2, 4, 8, 16)
HEADS = 16
NOPE, ROPE, V_DIM = 128, 64, 128
LATENT = 512
ATTN_SCALE = 1.0 / float(np.sqrt(NOPE + ROPE))
EPS = 1e-6

DT = D_MODEL // P
LT = LATENT // P
FH = D_FF // P // 2
GROUPS = len(WINDOWS)
GT = DT // GROUPS
PAD = max(WINDOWS)
HG = HEADS // 2

WEIGHT_SLOTS = 8
SPLIT_SLOTS = 4
TILES = 8
DTILES = FH // 2
BODY = WEIGHT_SLOTS

C_IDENT = 0
C_MASK = C_IDENT + P
C_CORR = C_MASK + 2 * P
C_FREQ = C_CORR + GROUPS * PAD
C_SIGN = C_FREQ + 1
C_COLS = C_SIGN + 1

G_POOL, G_SCALE, G_KV, G_ATTN, G_FFN0, G_FFN1, G_FINAL, G_LKV, G_LQ, G_COLS = (
    0, DT, 2 * DT, 3 * DT, 4 * DT, 5 * DT, 6 * DT, 7 * DT, 7 * DT + LT, 7 * DT + 2 * LT)


def chunk_plan():
    chunks, tiles, c, t = {}, {}, 0, 0
    for name, nc_, nt in (
        ("pool", DT * GT // TILES, DT),
        ("up0", 4 * FH, 2 * FH), ("down0", 2 * DT, DT), ("up1", 4 * FH, 2 * FH), ("down1", 2 * DT, DT),
        ("kva", 2 * LT, LT), ("kpe", 2, 2), ("qa", 2 * LT, LT),
        ("heads", 4 * HG, 8 * HG), ("wo", 2 * DT, DT),
        ("up2", 4 * FH, 2 * FH), ("down2", 2 * DT, DT), ("up3", 4 * FH, 2 * FH), ("down3", 2 * DT, DT),
    ):
        chunks[name], tiles[name] = c, t
        c, t = c + nc_, t + nt
    chunks["end"] = c
    return chunks, tiles


CHUNK, TILE = chunk_plan()

SQUARED = (DT, DT, LT, LT, DT, DT)


def squares_before(k):
    return sum(SQUARED[:k - 1])


def chunk_elems(n):
    for ph in ("down0", "down1", "down2", "down3"):
        if CHUNK[ph] <= n < CHUNK[ph] + 2 * DT:
            return DTILES * P
    if CHUNK["heads"] <= n < CHUNK["wo"] and (n - CHUNK["heads"]) % 4 == 2:
        return TILES * P // 2
    return TILES * P


def plus(n, i, per):
    return n if i is None else i * per + n


def trunk(nc, xT, positions, consts, gains, pool_w, w_kv_a, w_k_pe, w_q_a, w_kv_k, w_kv_v, w_q_nope, w_q_pe,
          w_o, w_gate, w_up, w_down, out):
    with ExitStack() as ctx:
        def sem(name):
            return ctx.enter_context(nc.semaphore(name))

        def sb(name, shape, dt=F32):
            return ctx.enter_context(nc.sbuf_tensor(name, shape, dt))

        x = sb("x", [P, DT, SEQ])
        raw = sb("raw", [P, WEIGHT_SLOTS, DTILES * P])
        w_hi = sb("w_hi", [P, SPLIT_SLOTS, DTILES * P], F32R)
        w_lo = sb("w_lo", [P, SPLIT_SLOTS, DTILES * P], F32R)
        const = sb("const", [P, C_COLS])
        gain = sb("gain", [P, G_COLS, 1])
        ones = sb("ones", [P, P])
        eps = sb("eps", [P, 1])
        cos = sb("cos", [P, SEQ])
        sin = sb("sin", [P, SEQ])
        root = sb("root", [P, SEQ])
        rstd = sb("rstd", [P, SEQ])
        square = sb("square", [P, SEQ])
        square_sum = sb("square_sum", [P, SEQ])
        cross = sb("cross", [P, 2, SEQ])
        sums = sb("sums", [P, 2, SEQ])
        gate_act = sb("gate_act", [P, SEQ])
        product = sb("product", [P, SEQ])

        KB = 1024
        region_at = nc.sbuf_base
        sb("region", [P, 80 * KB // 4])
        scratch_at = nc.sbuf_base
        sb("scratch", [P, (6 * KB + 64) // 4])

        def at(name, shape, dt, offset):
            return nc.alloc_sbuf_tensor_at(name, shape, dt, offset=offset)

        xg = at("xg", [P, DT, 2 * SEQ], F32R, region_at)
        act = at("act", [P, FH, 2 * SEQ], F32R, region_at + 32 * KB)
        PR = PAD + SEQ
        grp = GT * PR * 4
        pool_at = region_at + 32 * KB
        pooled = at("pooled", [P, 2, GT, 2 * SEQ], F32R, pool_at)
        x_square = at("x_square", [P, DT, SEQ], F32, pool_at)
        normed = at("normed", [P, DT, PR], F32, pool_at + 16 * KB)
        win_v = at("win_v", [P, GT, PR], F32, pool_at + 16 * KB + 4 * grp)
        win_v2 = at("win_v2", [P, GT, PR], F32, pool_at + 16 * KB + 5 * grp)
        win_p = at("win_p", [P, GT, PR], F32, pool_at + 16 * KB + 6 * grp)
        win_p2 = at("win_p2", [P, GT, PR], F32, scratch_at)
        xq = at("xq", [P, DT, 2 * SEQ], F32R, region_at + 32 * KB)
        latent = at("latent", [P, 2, LT, 2 * SEQ], F32R, region_at + 64 * KB)
        lat_raw = at("lat_raw", [P, LT, SEQ], F32, scratch_at)
        k_buf = at("k_buf", [P, 2, 2, 2 * SEQ], F32R, region_at)
        q_buf = at("q_buf", [P, 2, 2, 2 * SEQ], F32R, region_at + 8 * KB)
        v_buf = at("v_buf", [P, 2, 2, 2, 2 * V_DIM], F32R, region_at + 16 * KB)
        qpe_buf = at("qpe_buf", [P, 2, 2 * SEQ], F32R, region_at + 24 * KB)
        kpe_buf = at("kpe_buf", [P, 2, 2 * SEQ], F32R, region_at + 28 * KB)
        heads = at("heads", [P, HEADS, 2 * SEQ], F32R, region_at + 32 * KB)
        prob = at("prob", [P, 2, 3 * P], F32, scratch_at)
        probT = at("probT", [P, 2, 3 * P], F32R, scratch_at + 3 * KB)
        stat = at("stat", [P, 2, 8], F32, scratch_at + 6 * KB)
        y = at("y", [P, DT, SEQ], F32, region_at)
        pos_i = at("pos_i", [P, SEQ], I32, scratch_at + 4 * KB + KB // 2)
        angle = at("angle", [P, SEQ], F32, scratch_at)
        turns = at("turns", [P, SEQ], F32, scratch_at + KB)

        ps = ctx.enter_context(nc.psum_tensor("ps", [P, 8, 512], F32))
        SCORES, PROBT, STATS = 4, 6, 7

        x_landed = [sem(f"x_landed{q}") for q in range(4)]
        const_landed = sem("const_landed")
        landed = [sem(f"landed{s}") for s in range(WEIGHT_SLOTS)]
        hi_ready = sem("hi_ready")
        lo_ready = sem("lo_ready")
        chunks_used = sem("chunks_used")
        evacuated = sem("evacuated")
        xg_hi = sem("xg_hi")
        xg_ready = sem("xg_ready")
        cross_ready = sem("cross_ready")
        sums_ready = sem("sums_ready")
        gate_ready = sem("gate_ready")
        product_ready = sem("product_ready")
        act_hi = sem("act_hi")
        act_ready = sem("act_ready")
        squares_added = sem("squares_added")
        stats_summed = sem("stats_summed")
        root_ready = sem("root_ready")
        rstd_ready = sem("rstd_ready")
        squares_ready = sem("squares_ready")
        init_ready = sem("init_ready")
        windows_ready = sem("windows_ready")
        normed_ready = sem("normed_ready")
        diff_ready = sem("diff_ready")
        pooled_hi = sem("pooled_hi")
        pooled_ready = sem("pooled_ready")
        angle_ready = sem("angle_ready")
        table_ready = sem("table_ready")
        pos_landed = sem("pos_landed")
        lat_sum = sem("lat_sum")
        lat_scaled = sem("lat_scaled")
        lat_hi = sem("lat_hi")
        lat_ready = sem("lat_ready")
        proj_hi = sem("proj_hi")
        rope_sum = sem("rope_sum")
        rope_swapped = sem("rope_swapped")
        rope_done = sem("rope_done")
        k_ready = sem("k_ready")
        q_ready = sem("q_ready")
        qpe_ready = sem("qpe_ready")
        kpe_ready = sem("kpe_ready")
        scores_ready = sem("scores_ready")
        max_ready = sem("max_ready")
        exp_ready = sem("exp_ready")
        prob_ready = sem("prob_ready")
        probT_ready = sem("probT_ready")
        probT_hi = sem("probT_hi")
        probT_split = sem("probT_split")
        head_ready = sem("head_ready")
        head_hi = sem("head_hi")
        head_split = sem("head_split")
        y_gained = sem("y_gained")
        y_done_v = sem("y_done_v")
        y_done_p = sem("y_done_p")
        stored = sem("stored")
        v_step = sem("v_step")
        p_step = sem("p_step")

        block = ctx.enter_context(nc.Block())

        KV, Q = 0, 1
        INIT = 7
        UPS = ("up0", "up1", "up2", "up3")
        DOWNS = ("down0", "down1", "down2", "down3")

        @block.sync
        def _(sp):
            def load(n, src, i=None):
                if n >= WEIGHT_SLOTS:
                    sp.wait_ge(lo_ready, plus(n - WEIGHT_SLOTS + 1, i, BODY))
                sp.dma_start(raw[:, n % WEIGHT_SLOTS, 0:chunk_elems(n)], src).then_inc(landed[n % WEIGHT_SLOTS], 16)

            for q in range(4):
                sp.dma_start(x[:, 4 * q:4 * q + 4, :], xT[:, 4 * q:4 * q + 4, :]).then_inc(x_landed[q], 16)
            sp.dma_start(const[:, :], consts).then_inc(const_landed, 16)
            sp.dma_start(gain[:, :, :], gains).then_inc(const_landed, 16)
            sp.dma_start(pos_i[:, :], positions.partition_broadcast(P)).then_inc(pos_landed, 16)
            for c in range(CHUNK["up0"]):
                load(CHUNK["pool"] + c, pool_w[c])

            def ffn(layer, half):
                up, down = UPS[2 * layer + half], DOWNS[2 * layer + half]
                with sp.Fori(0, FH // 2) as i:
                    for c in range(BODY):
                        w = w_gate if c % 4 < 2 else w_up
                        row = ((layer * 2 + half) * FH + c // 4) * 2 + c % 2
                        load(CHUNK[up] + c, w[plus(row, i, 4)], i)
                with sp.Fori(0, DT // 4) as i:
                    for c in range(BODY):
                        load(CHUNK[down] + c, w_down[plus((layer * 2 + half) * DT * 2 + c, i, BODY)], i)

            ffn(0, 0)
            ffn(0, 1)
            for c in range(2 * LT):
                load(CHUNK["kva"] + c, w_kv_a[c])
            for c in range(2):
                n = CHUNK["kpe"] + c
                sp.wait_ge(lo_ready, n - WEIGHT_SLOTS + 1)
                sp.dma_start(raw[:, n % WEIGHT_SLOTS, 0:TILES * ROPE], w_k_pe[c]).then_inc(
                    landed[n % WEIGHT_SLOTS], 16)
            for c in range(2 * LT):
                load(CHUNK["qa"] + c, w_q_a[c])
            with sp.Fori(0, HG // 2) as i:
                for g in range(2):
                    for c, w in enumerate((w_kv_k, w_kv_v, w_q_pe, w_q_nope)):
                        load(CHUNK["heads"] + 4 * g + c, w[plus(g, i, 2)], i)
            with sp.Fori(0, DT // 4) as i:
                for c in range(BODY):
                    load(CHUNK["wo"] + c, w_o[plus(c, i, BODY)], i)
            ffn(1, 0)
            ffn(1, 1)

            for q in range(4):
                if q < 3:
                    sp.wait_ge(y_done_v, q + 1)
                else:
                    sp.wait_ge(y_done_p, 1)
                sp.dma_start(out[:, 4 * q:4 * q + 4, :], y[:, 4 * q:4 * q + 4, :]).then_inc(stored, 16)
            sp.wait_ge(stored, 64)

        @block.tensor
        def _(pe):
            def product3(n, j, bank, moving, start, stop):
                s = n % SPLIT_SLOTS
                pe.matmul(ps[:, bank, :], w_hi[:, s, j * P:(j + 1) * P], moving, start=start, stop=False)
                return pe.matmul(ps[:, bank, 0:SEQ], w_lo[:, s, j * P:(j + 1) * P], moving[:, 0:SEQ],
                                 start=False, stop=stop)

            def bank_free(t, i=None, per=0):
                if t >= 4:
                    pe.wait_ge(evacuated, plus(t - 3, i, per))

            def long_tile(n, t, operand, kts, i=None, per=0, each=None):
                for c in range(2):
                    pe.wait_ge(lo_ready, plus(n + c + 1, i, BODY))
                    if c == 0:
                        bank_free(t, i, per)
                    for j in range(kts):
                        kt = c * kts + j
                        if each is not None:
                            each(kt)
                        mm = product3(n + c, j, t % 4, operand[:, kt, :], kt == 0, kt == 2 * kts - 1)
                    mm.then_inc(chunks_used, 1)

            def sum_over_partitions(k):
                pe.wait_ge(squares_added, squares_before(k + 1))
                pe.wait_ge(root_ready, k)
                pe.matmul(ps[:, STATS, 0:SEQ], ones[:, :], square_sum[:, :], start=True,
                          stop=True).then_inc(stats_summed, 1)

            pe.wait_ge(init_ready, INIT)
            for t in range(DT):
                if t % 4 == 0:
                    pe.wait_ge(squares_ready, t // 4 + 1)
                mm = pe.matmul(ps[:, STATS, 0:SEQ], ones[:, :], x_square[:, t, :], start=(t == 0),
                               stop=(t == DT - 1))
            mm.then_inc(stats_summed, 1)

            for c in range(CHUNK["up0"]):
                n, g = CHUNK["pool"] + c, c // 2
                if c % 2 == 0:
                    pe.wait_ge(pooled_ready, g + 1)
                pe.wait_ge(lo_ready, n + 1)
                for m in range(2):
                    t = TILE["pool"] + 2 * c + m
                    bank_free(t)
                    for kt in range(GT):
                        mm = product3(n, m * GT + kt, t % 4, pooled[:, g % 2, kt, :], kt == 0, kt == GT - 1)
                mm.then_inc(chunks_used, 1)

            def ffn(layer, half, xg_before, stats):
                p = 2 * layer + half
                n0, t0 = CHUNK[UPS[p]], TILE[UPS[p]]
                peel = 0
                if half == 0:
                    peel = 1
                    long_tile(n0, t0, xg, TILES, each=lambda kt: pe.wait_ge(xg_ready, xg_before + kt + 1))
                    long_tile(n0 + 2, t0 + 1, xg, TILES)
                    sum_over_partitions(stats)
                    long_tile(n0 + 4, t0 + 2, xg, TILES)
                    long_tile(n0 + 6, t0 + 3, xg, TILES)
                with pe.Fori(0, FH // 2 - peel) as i:
                    for f in range(4):
                        long_tile(n0 + BODY * peel + 2 * f, t0 + 4 * peel + f, xg, TILES, i, 4)
                n0, t0 = CHUNK[DOWNS[p]], TILE[DOWNS[p]]
                long_tile(n0, t0, act, DTILES, each=lambda kt: pe.wait_ge(act_ready, p * FH + kt + 1))
                for d in range(1, 4):
                    long_tile(n0 + 2 * d, t0 + d, act, DTILES)
                with pe.Fori(0, DT // 4 - 1) as i:
                    for d in range(4):
                        long_tile(n0 + BODY + 2 * d, t0 + 4 + d, act, DTILES, i, 4)

            ffn(0, 0, 0, 1)
            ffn(0, 1, None, None)

            for m in range(LT):
                long_tile(CHUNK["kva"] + 2 * m, TILE["kva"] + m, xg, TILES,
                          each=(lambda kt: pe.wait_ge(xg_ready, DT + kt + 1)) if m == 0 else None)
                if m == 0:
                    sum_over_partitions(2)
            long_tile(CHUNK["kpe"], TILE["kpe"], xg, TILES)
            for m in range(LT):
                long_tile(CHUNK["qa"] + 2 * m, TILE["qa"] + m, xq, TILES,
                          each=(lambda kt: pe.wait_ge(xg_ready, 2 * DT + kt + 1)) if m == 0 else None)
                if m == 1:
                    sum_over_partitions(3)

            def key_part(g, i=None):
                n, t = CHUNK["heads"] + 4 * g, TILE["heads"] + 8 * g
                pe.wait_ge(lo_ready, plus(n + 1, i, BODY))
                for m in range(2):
                    bank_free(t + m, i, 16)
                    for kt in range(LT):
                        mm = product3(n, m * LT + kt, (t + m) % 4, latent[:, KV, kt, :], kt == 0, kt == LT - 1)
                mm.then_inc(chunks_used, 1)

            def value_part(g, i=None):
                n, t = CHUNK["heads"] + 4 * g + 1, TILE["heads"] + 8 * g + 2
                s = n % SPLIT_SLOTS
                pe.wait_ge(lo_ready, plus(n + 1, i, BODY))
                for m in range(2):
                    bank_free(t + m, i, 16)
                    dst = ps[:, (t + m) % 4, 0:2 * V_DIM]
                    for kt in range(LT):
                        wh = w_hi[:, s, kt * 2 * V_DIM:(kt + 1) * 2 * V_DIM]
                        wl = w_lo[:, s, kt * 2 * V_DIM:(kt + 1) * 2 * V_DIM]
                        c_hi = latent[:, KV, kt, m * P:(m + 1) * P]
                        c_lo = latent[:, KV, kt, SEQ + m * P:SEQ + (m + 1) * P]
                        pe.matmul(dst, c_hi, wh, start=(kt == 0), stop=False)
                        pe.matmul(dst, c_hi, wl, start=False, stop=False)
                        mm = pe.matmul(dst, c_lo, wh, start=False, stop=(kt == LT - 1))
                mm.then_inc(chunks_used, 1)

            def query_rope_part(g, i=None):
                n, t = CHUNK["heads"] + 4 * g + 2, TILE["heads"] + 8 * g + 4
                pe.wait_ge(lo_ready, plus(n + 1, i, BODY))
                bank_free(t, i, 16)
                for kt in range(LT):
                    mm = product3(n, kt, t % 4, latent[:, Q, kt, :], kt == 0, kt == LT - 1)
                mm.then_inc(chunks_used, 1)

            def query_part(g, i=None):
                n, t = CHUNK["heads"] + 4 * g + 3, TILE["heads"] + 8 * g + 6
                pe.wait_ge(lo_ready, plus(n + 1, i, BODY))
                for m in range(2):
                    bank_free(t + m, i, 16)
                    for kt in range(LT):
                        mm = product3(n, m * LT + kt, (t + m) % 4, latent[:, Q, kt, :], kt == 0, kt == LT - 1)
                mm.then_inc(chunks_used, 1)

            def scores(g, hh, i=None):
                b = g % 2
                if hh == 0:
                    pe.wait_ge(k_ready, plus(g + 1, i, 2))
                    pe.wait_ge(qpe_ready, plus(g + 1, i, 2))
                    pe.wait_ge(q_ready, plus(g + 1, i, 2))
                if g >= 1 or i is not None:
                    pe.wait_ge(max_ready, plus(2 * g + hh - 1, i, 4))
                for qt in range(2):
                    nk = (qt + 1) * P
                    dst = ps[:, SCORES + hh, qt * P:qt * P + nk]
                    pairs = ((q_buf[:, b, hh, :], k_buf[:, b, hh, :]), (qpe_buf[:, b, :], kpe_buf[:, hh, :]))
                    for part, (q, k) in enumerate(pairs):
                        q_hi, q_lo = q[:, qt * P:(qt + 1) * P], q[:, SEQ + qt * P:SEQ + (qt + 1) * P]
                        k_hi, k_lo = k[:, 0:nk], k[:, SEQ:SEQ + nk]
                        pe.matmul(dst, q_hi, k_hi, start=(part == 0), stop=False)
                        pe.matmul(dst, q_hi, k_lo, start=False, stop=False)
                        mm = pe.matmul(dst, q_lo, k_hi, start=False, stop=(part == 1))
                mm.then_inc(scores_ready, 1)

            def turn_probs(g, hh, i=None):
                pe.wait_ge(prob_ready, plus(2 * g + hh + 1, i, 4))
                if g >= 1 or hh >= 1 or i is not None:
                    pe.wait_ge(probT_split, plus(2 * g + hh, i, 4))
                for c in range(3):
                    mm = pe.transpose(ps[:, PROBT, c * P:(c + 1) * P], prob[:, hh, c * P:(c + 1) * P],
                                      const[:, C_IDENT:C_IDENT + P])
                mm.then_inc(probT_ready, 1)

            def head_output(g, hh, i=None):
                b = g % 2
                if hh == 0:
                    pe.wait_ge(evacuated, plus(TILE["heads"] + 8 * g + 4, i, 16))
                pe.wait_ge(probT_split, plus(2 * g + hh + 1, i, 4))
                if g >= 1 or hh >= 1 or i is not None:
                    pe.wait_ge(head_split, plus(2 * g + hh, i, 4))
                for kt in range(2):
                    v_hi = v_buf[:, b, kt, 0, hh * V_DIM:(hh + 1) * V_DIM]
                    v_lo = v_buf[:, b, kt, 1, hh * V_DIM:(hh + 1) * V_DIM]
                    cols = slice(0, 2 * P) if kt == 0 else slice(2 * P, 3 * P)
                    dst = ps[:, STATS, 0:SEQ] if kt == 0 else ps[:, STATS, P:SEQ]
                    pe.matmul(dst, v_hi, probT[:, 0, cols], start=(kt == 0), stop=False)
                    pe.matmul(dst, v_hi, probT[:, 1, cols], start=False, stop=False)
                    mm = pe.matmul(dst, v_lo, probT[:, 0, cols], start=False, stop=(kt == 1))
                mm.then_inc(head_ready, 1)

            def slot(g, i=None):
                if g < HG:
                    if g == 0:
                        pe.wait_ge(lat_ready, LT)
                    key_part(g, i)
                if 2 <= g:
                    head_output(g - 2, 0, i)
                    turn_probs(g - 2, 1, i)
                if g < HG:
                    value_part(g, i)
                if 2 <= g:
                    head_output(g - 2, 1, i)
                if 1 <= g <= HG:
                    scores(g - 1, 0, i)
                    scores(g - 1, 1, i)
                if g < HG:
                    if g == 0:
                        sum_over_partitions(4)
                        pe.wait_ge(lat_ready, 2 * LT)
                    query_rope_part(g, i)
                    query_part(g, i)
                if 1 <= g <= HG:
                    turn_probs(g - 1, 0, i)

            slot(0)
            slot(1)
            with pe.Fori(0, HG // 2 - 1) as i:
                slot(2, i)
                slot(3, i)
            slot(HG)
            slot(HG + 1)

            n0, t0 = CHUNK["wo"], TILE["wo"]
            pe.wait_ge(head_split, HEADS)
            with pe.Fori(0, DT // 4) as i:
                for d in range(4):
                    long_tile(n0 + 2 * d, t0 + d, heads, TILES, i, 4)

            ffn(1, 0, 3 * DT, 5)
            ffn(1, 1, None, None)
            sum_over_partitions(6)

        @block.scalar
        def _(sc):
            def split(n, i=None):
                if n >= CHUNK["end"]:
                    return
                e = chunk_elems(n)
                src = raw[:, n % WEIGHT_SLOTS, 0:e]
                if CHUNK["kpe"] <= n < CHUNK["kpe"] + 2:
                    src = raw[:, n % WEIGHT_SLOTS, 0:TILES * ROPE].rearrange("p (k o c) -> p k o c", k=TILES, o=1)
                    src = src.broadcast_to([P, TILES, 2, ROPE])
                sc.wait_ge(landed[n % WEIGHT_SLOTS], plus(16 * (n // WEIGHT_SLOTS + 1), i, 16))
                if n >= SPLIT_SLOTS:
                    sc.wait_ge(chunks_used, plus(n - SPLIT_SLOTS + 1, i, BODY))
                dst = w_hi[:, n % SPLIT_SLOTS, 0:e]
                if CHUNK["kpe"] <= n < CHUNK["kpe"] + 2:
                    dst = dst.rearrange("p (k o c) -> p k o c", k=TILES, o=2)
                nc.scalar.activation(dst, src, ACT.Copy).then_inc(hi_ready, 1)

            def root_of(k, features):
                sc.wait_ge(stats_summed, k)
                if k >= 2:
                    sc.wait_ge(rstd_ready, k - 1)
                nc.scalar.activation(root[:, :], ps[:, STATS, 0:SEQ], ACT.Sqrt, bias=eps[:, :],
                                     scale=1.0 / features).then_inc(root_ready, 1)

            def gained(t, tile_count, col, dst, i=None, per=0):
                sc.wait_ge(evacuated, plus(tile_count, i, per))
                nc.scalar.activation(dst[:, plus(t, i, per), 0:SEQ], x[:, plus(t, i, per), :], ACT.Identity,
                                     scale=gain[:, plus(col + t, i, per), :]).then_inc(xg_hi, 1)

            for q in range(4):
                sc.wait_ge(x_landed[q], 16)
                nc.scalar.activation(x_square[:, 4 * q:4 * q + 4, :], x[:, 4 * q:4 * q + 4, :],
                                     ACT.Square).then_inc(squares_ready, 1)
            sc.wait_ge(init_ready, INIT)
            root_of(1, D_MODEL)
            sc.wait_ge(const_landed, 32)
            for n in range(2):
                split(n)

            def pooled_group(g):
                sc.wait_ge(diff_ready, g + 1)
                diff = (win_v, win_v2)[g % 2]
                if g >= 2:
                    sc.wait_ge(chunks_used, 2 * (g - 2) + 2)
                nc.scalar.activation(pooled[:, g % 2, :, 0:SEQ], diff[:, :, PAD:], ACT.Copy).then_inc(pooled_hi, 1)

            pooled_group(0)
            split(2)
            split(3)
            pooled_group(1)
            for c in range(CHUNK["up0"]):
                for m in range(2):
                    gained(2 * c + m, TILE["pool"] + 2 * c + m + 1, G_FFN0, xg)
                if c in (1, 3):
                    pooled_group(2 + c // 2)
                split(c + SPLIT_SLOTS)

            def ffn_tile(p, f, splits, i=None):
                n, t = CHUNK[UPS[p]] + 4 * f, TILE[UPS[p]] + 2 * f
                bank = t % 4
                sc.wait_ge(chunks_used, plus(n + 4, i, BODY))
                nc.scalar.activation(cross[:, :, :], ps[:, bank:bank + 2, SEQ:], ACT.Copy).then_inc(cross_ready, 1)
                splits[0]()
                sc.wait_ge(sums_ready, plus(p * FH + f + 1, i, 2))
                nc.scalar.activation(gate_act[:, :], sums[:, 0, :], ACT.Silu).then_inc(gate_ready, 1)
                splits[1]()
                sc.wait_ge(product_ready, plus(p * FH + f + 1, i, 2))
                nc.scalar.activation(act[:, plus(f, i, 2), 0:SEQ], product[:, :], ACT.Copy).then_inc(act_hi, 1)
                splits[2]()

            def ffn(layer, half, stats):
                p = 2 * layer + half
                n0 = CHUNK[UPS[p]]
                for w in range(3):
                    split(n0 + w + SPLIT_SLOTS)
                if stats is not None:
                    root_of(stats, D_MODEL)

                def tile(f, i=None):
                    n = n0 + 4 * f + 3 + SPLIT_SLOTS
                    ffn_tile(p, f, (lambda: split(n, i), lambda: split(n + 1, i),
                                    lambda: (split(n + 2, i), split(n + 3, i))), i)

                with sc.Fori(0, FH // 2 - 1) as i:
                    tile(0, i)
                    tile(1, i)
                tile(FH - 2)
                nothing = lambda: None
                ffn_tile(p, FH - 1, (nothing, nothing, lambda: split(n0 + 4 * FH - 1 + SPLIT_SLOTS)))

                n1, t1 = CHUNK[DOWNS[p]], TILE[DOWNS[p]]

                def down(d, i=None):
                    split(n1 + 2 * d + SPLIT_SLOTS, i)
                    if half == 1 and layer == 0:
                        gained(d, t1 + d + 1, G_KV, xg, i, 4)
                    if half == 1 and layer == 1:
                        sc.wait_ge(evacuated, plus(t1 + d + 1, i, 4))
                        nc.scalar.activation(y[:, plus(d, i, 4), :], x[:, plus(d, i, 4), :], ACT.Identity,
                                             scale=gain[:, plus(G_FINAL + d, i, 4), :]).then_inc(y_gained, 1)
                    split(n1 + 2 * d + 1 + SPLIT_SLOTS, i)

                with sc.Fori(0, DT // 4 - 1) as i:
                    for d in range(4):
                        down(d, i)
                for d in range(DT - 4, DT):
                    down(d)

            ffn(0, 0, 2)
            sc.wait_ge(angle_ready, 1)
            nc.scalar.activation(sin[:, :], angle[:, :], ACT.Sin).then_inc(table_ready, 1)
            nc.scalar.activation(cos[:, :], turns[:, :], ACT.Sin).then_inc(table_ready, 1)
            ffn(0, 1, None)

            xq_tiles = iter(range(DT))

            def xq_some(k):
                for _ in range(k):
                    gained(next(xq_tiles), TILE["kva"], G_ATTN, xq)

            def lat_pair(name, m):
                n, t = CHUNK[name] + 2 * m, TILE[name] + m
                sc.wait_ge(chunks_used, n + 4)
                sc.wait_ge(evacuated, t)
                nc.scalar.activation(cross[:, :, :], ps[:, t % 4:t % 4 + 2, SEQ:], ACT.Copy).then_inc(cross_ready, 1)

            def lat_split(which, col):
                sc.wait_ge(lat_scaled, which + 1)
                for t in range(LT):
                    nc.scalar.activation(latent[:, which, t, 0:SEQ], lat_raw[:, t, :], ACT.Identity,
                                         scale=gain[:, col + t, :]).then_inc(lat_hi, 1)

            n0 = CHUNK["kva"]
            for w in range(3):
                split(n0 + w + SPLIT_SLOTS)
                xq_some(2)
                if w == 1:
                    root_of(3, D_MODEL)
            lat_pair("kva", 0)
            for w in range(3, 7):
                split(n0 + w + SPLIT_SLOTS)
                xq_some(2)
            lat_pair("kva", 2)
            split(n0 + 7 + SPLIT_SLOTS)
            xq_some(2)
            split(n0 + 8 + SPLIT_SLOTS)
            sc.wait_ge(chunks_used, CHUNK["kpe"] + 2)
            sc.wait_ge(evacuated, TILE["kpe"])
            b = TILE["kpe"] % 4
            nc.scalar.activation(cross[:, 0, :], ps[:, b, SEQ:], ACT.Copy).then_inc(cross_ready, 1)
            split(n0 + 9 + SPLIT_SLOTS)

            def swap_halves(k, i=None, per=0):
                sc.wait_ge(rope_sum, plus(k, i, per))
                for q in range(4):
                    last = nc.scalar.activation(product[32 * q:32 * q + 32, :],
                                                gate_act[32 * (q ^ 1):32 * (q ^ 1) + 32, :], ACT.Copy)
                    last.then_inc(rope_swapped, 1)

            swap_halves(1)
            sc.wait_ge(rope_done, 1)
            for hh in range(2):
                rows = slice(64 * hh, 64 * hh + 64)
                nc.scalar.activation(kpe_buf[rows, hh, 0:SEQ], gate_act[rows, :], ACT.Copy).then_inc(proj_hi, 1)
            split(n0 + 10 + SPLIT_SLOTS)
            split(n0 + 11 + SPLIT_SLOTS)
            split(n0 + 12 + SPLIT_SLOTS)
            lat_pair("qa", 0)
            split(n0 + 13 + SPLIT_SLOTS)
            root_of(4, LATENT)
            lat_split(0, G_LKV)
            split(n0 + 14 + SPLIT_SLOTS)
            split(n0 + 15 + SPLIT_SLOTS)
            split(n0 + 16 + SPLIT_SLOTS)
            lat_pair("qa", 2)
            split(n0 + 17 + SPLIT_SLOTS)

            def pair_hi(g, part, dst, i):
                n = CHUNK["heads"] + 4 * g + part
                t = TILE["heads"] + 8 * g + 2 * part
                sc.wait_ge(chunks_used, plus(n + 1, i, BODY))
                sc.wait_ge(evacuated, plus(t, i, 16))
                nc.scalar.activation(cross[:, :, :], ps[:, t % 4:t % 4 + 2, SEQ:], ACT.Copy).then_inc(cross_ready, 1)
                sc.wait_ge(evacuated, plus(t + 2, i, 16))
                nc.scalar.activation(dst[:, g % 2, :, 0:SEQ], sums[:, :, :], ACT.Copy).then_inc(proj_hi, 1)

            def value_hi(g, i):
                n, t = CHUNK["heads"] + 4 * g + 1, TILE["heads"] + 8 * g + 2
                sc.wait_ge(chunks_used, plus(n + 1, i, BODY))
                if g >= 2 or i is not None:
                    sc.wait_ge(head_ready, plus(2 * g - 2, i, 4))
                nc.scalar.activation(v_buf[:, g % 2, :, 0, :], ps[:, t % 4:t % 4 + 2, 0:2 * V_DIM],
                                     ACT.Copy).then_inc(proj_hi, 1)

            def rope_hi(g, i):
                n, t = CHUNK["heads"] + 4 * g + 2, TILE["heads"] + 8 * g + 4
                sc.wait_ge(chunks_used, plus(n + 1, i, BODY))
                sc.wait_ge(evacuated, plus(t, i, 16))
                nc.scalar.activation(cross[:, 0, :], ps[:, t % 4, SEQ:], ACT.Copy).then_inc(cross_ready, 1)
                swap_halves(g + 2, i, 2)
                sc.wait_ge(rope_done, plus(g + 2, i, 2))
                nc.scalar.activation(qpe_buf[:, g % 2, 0:SEQ], gate_act[:, :], ACT.Copy).then_inc(proj_hi, 1)

            def probT_hi_half(g, hh, i):
                sc.wait_ge(probT_ready, plus(2 * g + hh + 1, i, 4))
                nc.scalar.activation(probT[:, 0, :], ps[:, PROBT, 0:3 * P], ACT.Copy).then_inc(probT_hi, 1)

            def head_hi_half(g, hh, i):
                sc.wait_ge(head_ready, plus(2 * g + hh + 1, i, 4))
                nc.scalar.activation(heads[:, plus(2 * g + hh, i, 4), 0:SEQ], ps[:, STATS, 0:SEQ],
                                     ACT.Copy).then_inc(head_hi, 1)

            def exps(g, hh, i):
                sc.wait_ge(max_ready, plus(2 * g + hh + 1, i, 4))
                nc.scalar.activation(prob[:, hh, 0:P], prob[:, hh, 0:P], ACT.Exp, bias=stat[:, hh, 2:3],
                                     accum_out=stat[:, hh, 4:5]).then_inc(exp_ready, 1)
                nc.scalar.activation(prob[:, hh, P:], prob[:, hh, P:], ACT.Exp, bias=stat[:, hh, 3:4],
                                     accum_out=stat[:, hh, 5:6]).then_inc(exp_ready, 1)

            def slot(g, i=None):
                n = CHUNK["heads"] + 4 * g
                own = g < HG
                if own:
                    pair_hi(g, 0, k_buf, i)
                if g >= 2:
                    head_hi_half(g - 2, 0, i)
                    probT_hi_half(g - 2, 1, i)
                if own:
                    split(n + SPLIT_SLOTS, i)
                    value_hi(g, i)
                if g >= 2:
                    head_hi_half(g - 2, 1, i)
                if own:
                    split(n + 1 + SPLIT_SLOTS, i)
                if 1 <= g <= HG:
                    exps(g - 1, 0, i)
                    exps(g - 1, 1, i)
                if g == 0:
                    root_of(5, LATENT)
                    lat_split(1, G_LQ)
                if own:
                    rope_hi(g, i)
                    split(n + 2 + SPLIT_SLOTS, i)
                    pair_hi(g, 3, q_buf, i)
                if 1 <= g <= HG:
                    probT_hi_half(g - 1, 0, i)
                if own:
                    split(n + 3 + SPLIT_SLOTS, i)

            slot(0)
            slot(1)
            with sc.Fori(0, HG // 2 - 2) as i:
                slot(2, i)
                slot(3, i)
            for g in range(HG - 2, HG + 2):
                slot(g)

            n1, t1 = CHUNK["wo"], TILE["wo"]

            def wo(d, i=None):
                split(n1 + 2 * d + SPLIT_SLOTS, i)
                gained(d, t1 + d + 1, G_FFN1, xg, i, 4)
                split(n1 + 2 * d + 1 + SPLIT_SLOTS, i)

            with sc.Fori(0, DT // 4) as i:
                for d in range(4):
                    wo(d, i)
            ffn(1, 0, 6)
            ffn(1, 1, None)
            root_of(7, D_MODEL)

        @block.vector
        def _(ve):
            steps = [0, None, 0]

            def step(ins):
                steps[0] += 1
                ins.then_inc(v_step, 1)
                ve.wait_ge(v_step, plus(steps[0], steps[1], steps[2]))

            def loop(count, per, body):
                with ve.Fori(0, count) as i:
                    start = steps[0]
                    steps[1:] = [i, per]
                    body(i)
                    assert steps[0] - start == per, (steps[0] - start, per)
                steps[:] = [start + per * count, None, 0]

            crossed = [0]

            def split(n, i=None):
                if n >= CHUNK["end"]:
                    return
                e = chunk_elems(n)
                src, hi, lo = raw[:, n % WEIGHT_SLOTS, 0:e], w_hi[:, n % SPLIT_SLOTS, 0:e], w_lo[:, n % SPLIT_SLOTS, 0:e]
                if CHUNK["kpe"] <= n < CHUNK["kpe"] + 2:
                    src = raw[:, n % WEIGHT_SLOTS, 0:TILES * ROPE].rearrange("p (k o c) -> p k o c", k=TILES, o=1)
                    src = src.broadcast_to([P, TILES, 2, ROPE])
                    hi = hi.rearrange("p (k o c) -> p k o c", k=TILES, o=2)
                    lo = lo.rearrange("p (k o c) -> p k o c", k=TILES, o=2)
                ve.wait_ge(hi_ready, plus(n + 1, i, BODY))
                nc.vector.tensor_tensor(lo, src, hi.bitcast(F32), ALU.subtract).then_inc(lo_ready, 1)

            def rstd_of(k):
                ve.wait_ge(root_ready, k)
                nc.vector.reciprocal(rstd[:, :], root[:, :]).then_inc(rstd_ready, 1)
                ve.wait_ge(rstd_ready, k)

            xgs = [0]

            def gained(t, col, dst, number, i=None, per=0):
                ve.wait_ge(xg_hi, plus(number, i, per))
                nc.vector.scalar_tensor_tensor(
                    dst[:, plus(t, i, per), SEQ:], x[:, plus(t, i, per), :], gain[:, plus(col + t, i, per), :],
                    dst[:, plus(t, i, per), 0:SEQ].bitcast(F32), ALU.mult, ALU.subtract).then_inc(xg_ready, 1)

            def rope_angles():
                step(nc.vector.tensor_copy(turns[:, :], pos_i[:, :]))
                step(nc.vector.tensor_scalar(angle[:, :], turns[:, :], const[:, C_FREQ:C_FREQ + 1], None, ALU.mult))
                magic = 1.5 * 2.0 ** 23
                step(nc.vector.tensor_scalar(turns[:, :], angle[:, :], 1.0 / (2.0 * np.pi), None, ALU.mult))
                step(nc.vector.tensor_scalar(turns[:, :], turns[:, :], magic, None, ALU.add))
                step(nc.vector.tensor_scalar(turns[:, :], turns[:, :], -magic, None, ALU.add))
                rest = 2.0 * np.pi
                for part in range(5):
                    e = np.floor(np.log2(rest)) - 7
                    c = float(np.floor(rest / 2.0 ** e) * 2.0 ** e) if part < 4 else float(np.float32(rest))
                    rest -= c
                    step(nc.vector.scalar_tensor_tensor(angle[:, :], turns[:, :], -c, angle[:, :], ALU.mult, ALU.add))
                pi_low = 3.1415925
                step(nc.vector.tensor_scalar(angle[:, :], angle[:, :], pi_low, -pi_low, ALU.min, ALU.max))
                step(nc.vector.scalar_tensor_tensor(turns[:, :], angle[:, :], -1.0, angle[:, :], ALU.mult, ALU.max))
                nc.vector.tensor_scalar(turns[:, :], turns[:, :], -1.0, float(np.pi / 2), ALU.mult,
                                        ALU.add).then_inc(angle_ready, 1)

            ve.wait_ge(init_ready, INIT)
            ve.wait_ge(const_landed, 32)
            rstd_of(1)
            for t in range(DT):
                ins = nc.vector.scalar_tensor_tensor(normed[:, t, PAD:], x[:, t, :], gain[:, G_POOL + t, :],
                                                     rstd[:, :], ALU.mult, ALU.mult)
                ins.then_inc(normed_ready, 1)

            def window_sum(dst, src, reach):
                return nc.vector.tensor_tensor(dst[:, :, PAD:], src[:, :, PAD:], src[:, :, PAD - reach:PAD + SEQ - reach],
                                               ALU.add)

            def pool_diff(g, win, dst):
                corr = const[:, C_CORR + g * PAD:C_CORR + (g + 1) * PAD].rearrange("p (o t) -> p o t", o=1)
                corr = corr.broadcast_to([P, GT, PAD])
                step(nc.vector.tensor_tensor(win[:, :, PAD:2 * PAD], win[:, :, PAD:2 * PAD], corr, ALU.mult))
                nc.vector.scalar_tensor_tensor(dst[:, :, PAD:], win[:, :, PAD:], 1.0 / WINDOWS[g],
                                               normed[:, g * GT:(g + 1) * GT, PAD:], ALU.mult,
                                               ALU.subtract).then_inc(diff_ready, 1)
                ve.wait_ge(diff_ready, g + 1)

            def pooled_lo(g, diff):
                ve.wait_ge(pooled_hi, g + 1)
                nc.vector.tensor_tensor(pooled[:, g % 2, :, SEQ:], diff[:, :, PAD:],
                                        pooled[:, g % 2, :, 0:SEQ].bitcast(F32),
                                        ALU.subtract).then_inc(pooled_ready, 1)

            ve.wait_ge(normed_ready, DT)
            split(0)
            split(1)
            step(window_sum(win_v, normed[:, 0:GT, :], 1))
            pool_diff(0, win_v, win_v)
            pooled_lo(0, win_v)
            split(2)
            split(3)
            ve.wait_ge(pooled_ready, 1)
            step(window_sum(win_v, normed[:, GT:2 * GT, :], 1))
            step(window_sum(win_v2, win_v, 2))
            pool_diff(1, win_v2, win_v2)
            pooled_lo(1, win_v2)

            for c in range(CHUNK["up0"]):
                ve.wait_ge(chunks_used, c + 1)
                for m in range(2):
                    t = 2 * c + m
                    b = t % 4
                    s = gain[:, G_SCALE + t, :]
                    step(nc.vector.scalar_tensor_tensor(x[:, t, :], ps[:, b, 0:SEQ], s, x[:, t, :], ALU.mult, ALU.add))
                    nc.vector.scalar_tensor_tensor(x[:, t, :], ps[:, b, SEQ:], s, x[:, t, :], ALU.mult,
                                                   ALU.add).then_inc(evacuated, 1)
                for m in range(2):
                    gained(2 * c + m, G_FFN0, xg, 2 * c + m + 1)
                if c in (1, 3):
                    g = 2 + c // 2
                    ve.wait_ge(windows_ready, g - 1)
                    ve.wait_ge(pooled_ready, g - 1)
                    diff = (win_v, win_v2)[g % 2]
                    pool_diff(g, win_p, diff)
                    pooled_lo(g, diff)
                split(c + SPLIT_SLOTS)

            def ffn_tile(p, f, splits, i=None):
                t = TILE[UPS[p]] + 2 * f
                bank = t % 4
                ve.wait_ge(cross_ready, plus(crossed[0] + f + 1, i, 2))
                nc.vector.tensor_tensor(sums[:, :, :], ps[:, bank:bank + 2, 0:SEQ], cross[:, :, :],
                                        ALU.add).then_inc(evacuated, 2)
                ve.wait_ge(evacuated, plus(t + 2, i, 4))
                r = rstd[:, :].rearrange("p (o t) -> p o t", o=1).broadcast_to([P, 2, SEQ])
                nc.vector.tensor_tensor(sums[:, :, :], sums[:, :, :], r, ALU.mult).then_inc(sums_ready, 1)
                splits[0]()
                ve.wait_ge(gate_ready, plus(p * FH + f + 1, i, 2))
                nc.vector.tensor_tensor(product[:, :], gate_act[:, :], sums[:, 1, :], ALU.mult).then_inc(product_ready, 1)
                splits[1]()
                ve.wait_ge(act_hi, plus(p * FH + f + 1, i, 2))
                nc.vector.tensor_tensor(act[:, plus(f, i, 2), SEQ:], product[:, :],
                                        act[:, plus(f, i, 2), 0:SEQ].bitcast(F32),
                                        ALU.subtract).then_inc(act_ready, 1)
                splits[2]()

            def into_x(t, d, used, i=None, per=0):
                b = t % 4
                xd = x[:, plus(d, i, per), :]
                ve.wait_ge(chunks_used, plus(used, i, BODY))
                step(nc.vector.tensor_tensor(xd, ps[:, b, 0:SEQ], xd, ALU.add))
                nc.vector.tensor_tensor(xd, ps[:, b, SEQ:], xd, ALU.add).then_inc(evacuated, 1)

            def ffn(layer, half, stats, xg_before):
                p = 2 * layer + half
                n0 = CHUNK[UPS[p]]
                for w in range(3):
                    split(n0 + w + SPLIT_SLOTS)
                if stats is not None:
                    rstd_of(stats)

                def tile(f, i=None):
                    n = n0 + 4 * f + 3 + SPLIT_SLOTS
                    ffn_tile(p, f, (lambda: split(n, i), lambda: split(n + 1, i),
                                    lambda: (split(n + 2, i), split(n + 3, i))), i)

                with ve.Fori(0, FH // 2 - 1) as i:
                    tile(0, i)
                    tile(1, i)
                tile(FH - 2)
                nothing = lambda: None
                ffn_tile(p, FH - 1, (nothing, nothing, lambda: split(n0 + 4 * FH - 1 + SPLIT_SLOTS)))
                crossed[0] += FH

                n1, t1 = CHUNK[DOWNS[p]], TILE[DOWNS[p]]

                def down(d, i=None):
                    split(n1 + 2 * d + SPLIT_SLOTS, i)
                    into_x(t1 + d, d, n1 + 2 * d + 2, i, 4)
                    if half == 1 and layer == 0:
                        gained(d, G_KV, xg, xg_before + d + 1, i, 4)
                    split(n1 + 2 * d + 1 + SPLIT_SLOTS, i)

                loop(DT // 4 - 1, 4, lambda i: [down(d, i) for d in range(4)])
                for d in range(DT - 4, DT):
                    down(d)

            ffn(0, 0, 2, None)
            ve.wait_ge(pos_landed, 16)
            rope_angles()
            ffn(0, 1, None, DT)

            xq_tiles = iter(range(DT))

            def xq_some(k):
                for _ in range(k):
                    t = next(xq_tiles)
                    gained(t, G_ATTN, xq, 2 * DT + t + 1)

            def lat_add(name, m):
                t = TILE[name] + m
                crossed[0] += 1
                ve.wait_ge(cross_ready, crossed[0])
                if m > 0:
                    ve.wait_ge(lat_sum, 1 if name == "kva" else 3)
                nc.vector.tensor_tensor(sums[:, :, :], ps[:, t % 4:t % 4 + 2, 0:SEQ], cross[:, :, :],
                                        ALU.add).then_inc(evacuated, 2)
                ve.wait_ge(evacuated, t + 2)

            def lat_scale(m):
                r = rstd[:, :].rearrange("p (o t) -> p o t", o=1).broadcast_to([P, 2, SEQ])
                nc.vector.tensor_tensor(lat_raw[:, m:m + 2, :], sums[:, :, :], r, ALU.mult).then_inc(lat_sum, 1)

            def lat_norm(which, col):
                ve.wait_ge(root_ready, 4 + which)
                nc.vector.reciprocal(product[:, :], root[:, :]).then_inc(rstd_ready, 1)
                ve.wait_ge(rstd_ready, 4 + which)
                r = product[:, :].rearrange("p (o t) -> p o t", o=1).broadcast_to([P, LT, SEQ])
                nc.vector.tensor_tensor(lat_raw[:, :, :], lat_raw[:, :, :], r, ALU.mult).then_inc(lat_scaled, 1)
                for t in range(LT):
                    ve.wait_ge(lat_hi, which * LT + t + 1)
                    nc.vector.scalar_tensor_tensor(
                        latent[:, which, t, SEQ:], lat_raw[:, t, :], gain[:, col + t, :],
                        latent[:, which, t, 0:SEQ].bitcast(F32), ALU.mult, ALU.subtract).then_inc(lat_ready, 1)

            n0 = CHUNK["kva"]
            for w in range(3):
                split(n0 + w + SPLIT_SLOTS)
                xq_some(2)
                if w == 1:
                    rstd_of(3)
            lat_add("kva", 0)
            lat_scale(0)
            for w in range(3, 7):
                split(n0 + w + SPLIT_SLOTS)
                xq_some(2)
            lat_add("kva", 2)
            lat_scale(2)
            split(n0 + 7 + SPLIT_SLOTS)
            xq_some(2)
            split(n0 + 8 + SPLIT_SLOTS)

            def rotate(t, crossed_at, k, i=None, scaled=False):
                ve.wait_ge(cross_ready, plus(crossed_at, i, 6))
                nc.vector.tensor_tensor(gate_act[:, :], ps[:, t % 4, 0:SEQ], cross[:, 0, :],
                                        ALU.add).then_inc(evacuated, 2)
                ve.wait_ge(evacuated, plus(t + 2, i, 16))
                if scaled:
                    step(nc.vector.tensor_tensor(gate_act[:, :], gate_act[:, :], rstd[:, :], ALU.mult))
                nc.vector.tensor_tensor(sums[:, 0, :], gate_act[:, :], cos[:, :], ALU.mult).then_inc(rope_sum, 1)
                ve.wait_ge(rope_swapped, plus(4 * k, i, 8))
                step(nc.vector.tensor_tensor(sums[:, 1, :], product[:, :], sin[:, :], ALU.mult))
                nc.vector.tensor_tensor(gate_act[:, :], sums[:, 0, :], sums[:, 1, :], ALU.add).then_inc(rope_done, 1)
                ve.wait_ge(rope_done, plus(k, i, 2))

            ve.wait_ge(table_ready, 2)
            step(nc.vector.tensor_scalar(sin[:, :], sin[:, :], const[:, C_SIGN:C_SIGN + 1], None, ALU.mult))
            crossed[0] += 1
            split(n0 + 9 + SPLIT_SLOTS)
            rotate(TILE["kpe"], crossed[0], 1, scaled=True)
            nc.vector.memset(kpe_buf[64:P, 0, :].bitcast(F32), 0.0).then_inc(kpe_ready, 1)
            nc.vector.memset(kpe_buf[0:64, 1, :].bitcast(F32), 0.0).then_inc(kpe_ready, 1)
            for hh in range(2):
                rows = slice(64 * hh, 64 * hh + 64)
                ve.wait_ge(proj_hi, hh + 1)
                nc.vector.tensor_tensor(kpe_buf[rows, hh, SEQ:], gate_act[rows, :],
                                        kpe_buf[rows, hh, 0:SEQ].bitcast(F32), ALU.subtract).then_inc(kpe_ready, 1)
            split(n0 + 10 + SPLIT_SLOTS)
            split(n0 + 11 + SPLIT_SLOTS)
            split(n0 + 12 + SPLIT_SLOTS)
            lat_add("qa", 0)
            split(n0 + 13 + SPLIT_SLOTS)
            lat_norm(KV, G_LKV)
            ve.wait_ge(lat_ready, LT)
            lat_scale(0)
            split(n0 + 14 + SPLIT_SLOTS)
            split(n0 + 15 + SPLIT_SLOTS)
            split(n0 + 16 + SPLIT_SLOTS)
            lat_add("qa", 2)
            lat_scale(2)
            split(n0 + 17 + SPLIT_SLOTS)

            def pair_lo(g, part, dst, ready, crossed_at, i):
                t = TILE["heads"] + 8 * g + 2 * part
                if part == 0:
                    if g == 0:
                        ve.wait_ge(lat_sum, 4)
                    else:
                        ve.wait_ge(q_ready, plus(g, i, 2))
                ve.wait_ge(cross_ready, plus(crossed_at, i, 6))
                nc.vector.tensor_tensor(sums[:, :, :], ps[:, t % 4:t % 4 + 2, 0:SEQ], cross[:, :, :],
                                        ALU.add).then_inc(evacuated, 2)
                ve.wait_ge(proj_hi, plus(2 + 4 * g + part + 1, i, 8))
                nc.vector.tensor_tensor(dst[:, g % 2, :, SEQ:], sums[:, :, :], dst[:, g % 2, :, 0:SEQ].bitcast(F32),
                                        ALU.subtract).then_inc(ready, 1)

            def value_lo(g, i):
                t = TILE["heads"] + 8 * g + 2
                ve.wait_ge(proj_hi, plus(2 + 4 * g + 2, i, 8))
                nc.vector.tensor_tensor(v_buf[:, g % 2, :, 1, :], ps[:, t % 4:t % 4 + 2, 0:2 * V_DIM],
                                        v_buf[:, g % 2, :, 0, :].bitcast(F32), ALU.subtract).then_inc(evacuated, 2)

            def rope_lo(g, crossed_at, i):
                rotate(TILE["heads"] + 8 * g + 4, crossed_at, g + 2, i)
                ve.wait_ge(proj_hi, plus(2 + 4 * g + 3, i, 8))
                nc.vector.tensor_tensor(qpe_buf[:, g % 2, SEQ:], gate_act[:, :], qpe_buf[:, g % 2, 0:SEQ].bitcast(F32),
                                        ALU.subtract).then_inc(qpe_ready, 1)

            def probT_lo_half(g, hh, i):
                ve.wait_ge(probT_hi, plus(2 * g + hh + 1, i, 4))
                nc.vector.tensor_tensor(probT[:, 1, :], ps[:, PROBT, 0:3 * P], probT[:, 0, :].bitcast(F32),
                                        ALU.subtract).then_inc(probT_split, 1)

            def head_lo_half(g, hh, i):
                h = plus(2 * g + hh, i, 4)
                ve.wait_ge(head_hi, plus(2 * g + hh + 1, i, 4))
                nc.vector.tensor_tensor(heads[:, h, SEQ:], ps[:, STATS, 0:SEQ], heads[:, h, 0:SEQ].bitcast(F32),
                                        ALU.subtract).then_inc(head_split, 1)

            def row_max(g, hh, i):
                ve.wait_ge(scores_ready, plus(2 * g + hh + 1, i, 4))
                nc.vector.tensor_copy(stat[:, hh, 7:8], eps[:, :])
                for qt in range(2):
                    nk = (qt + 1) * P
                    mask = const[:, C_MASK + 2 * P - nk:C_MASK + 2 * P]
                    ins = nc.vector.tensor_tensor_reduce(
                        prob[:, hh, qt * P:qt * P + nk], ps[:, SCORES + hh, qt * P:qt * P + nk], mask, ATTN_SCALE,
                        -3.0e38, ALU.add, ALU.max, stat[:, hh, qt:qt + 1])
                step(ins)
                nc.vector.tensor_scalar(stat[:, hh, 2:4], stat[:, hh, 0:2], -1.0, None, ALU.mult).then_inc(max_ready, 1)

            def normalise(g, hh, i):
                ve.wait_ge(exp_ready, plus(2 * (2 * g + hh + 1), i, 8))
                step(nc.vector.reciprocal(stat[:, hh, 6:8], stat[:, hh, 4:6]))
                step(nc.vector.tensor_scalar(prob[:, hh, 0:P], prob[:, hh, 0:P], stat[:, hh, 6:7], None, ALU.mult))
                nc.vector.tensor_scalar(prob[:, hh, P:], prob[:, hh, P:], stat[:, hh, 7:8], None,
                                        ALU.mult).then_inc(prob_ready, 1)

            crossed_heads = crossed[0]

            def slot(g, i=None):
                n, cr = CHUNK["heads"] + 4 * g, crossed_heads + 3 * g
                own = g < HG
                if own:
                    pair_lo(g, 0, k_buf, k_ready, cr + 1, i)
                if g >= 2:
                    head_lo_half(g - 2, 0, i)
                    probT_lo_half(g - 2, 1, i)
                if own:
                    split(n + SPLIT_SLOTS, i)
                    value_lo(g, i)
                if g >= 2:
                    head_lo_half(g - 2, 1, i)
                if own:
                    split(n + 1 + SPLIT_SLOTS, i)
                if 1 <= g <= HG:
                    row_max(g - 1, 0, i)
                    row_max(g - 1, 1, i)
                    normalise(g - 1, 0, i)
                    normalise(g - 1, 1, i)
                if g == 0:
                    lat_norm(Q, G_LQ)
                if own:
                    rope_lo(g, cr + 2, i)
                    split(n + 2 + SPLIT_SLOTS, i)
                    pair_lo(g, 3, q_buf, q_ready, cr + 3, i)
                if 1 <= g <= HG:
                    probT_lo_half(g - 1, 0, i)
                if own:
                    split(n + 3 + SPLIT_SLOTS, i)

            slot(0)
            slot(1)
            loop(HG // 2 - 2, 2 * 7, lambda i: (slot(2, i), slot(3, i)))
            for g in range(HG - 2, HG + 2):
                slot(g)
            crossed[0] += 3 * HG

            n1, t1 = CHUNK["wo"], TILE["wo"]

            def wo(d, i):
                split(n1 + 2 * d + SPLIT_SLOTS, i)
                into_x(t1 + d, d, n1 + 2 * d + 2, i, 4)
                gained(d, G_FFN1, xg, 3 * DT + d + 1, i, 4)
                split(n1 + 2 * d + 1 + SPLIT_SLOTS, i)

            loop(DT // 4, 4, lambda i: [wo(d, i) for d in range(4)])
            ffn(1, 0, 6, None)
            ffn(1, 1, None, None)

            rstd_of(7)
            for q in range(3):
                ve.wait_ge(y_gained, 4 * q + 4)
                r = rstd[:, :].rearrange("p (o t) -> p o t", o=1).broadcast_to([P, 4, SEQ])
                nc.vector.tensor_tensor(y[:, 4 * q:4 * q + 4, :], y[:, 4 * q:4 * q + 4, :], r,
                                        ALU.mult).then_inc(y_done_v, 1)

        @block.gpsimd
        def _(gp):
            steps = [0, None, 0]

            def step(ins):
                steps[0] += 1
                ins.then_inc(p_step, 1)
                gp.wait_ge(p_step, plus(steps[0], steps[1], steps[2]))

            for ap, value in ((ones[:, :], 1.0), (eps[:, :], EPS), (normed[:, :, 0:PAD], 0.0),
                              (win_v[:, :, 0:PAD], 0.0), (win_v2[:, :, 0:PAD], 0.0), (win_p[:, :, 0:PAD], 0.0),
                              (win_p2[:, :, 0:PAD], 0.0)):
                nc.gpsimd.memset(ap, value).then_inc(init_ready, 1)
            gp.wait_ge(init_ready, INIT)

            def window_sum(dst, src, reach):
                return nc.gpsimd.tensor_tensor(dst[:, :, PAD:], src[:, :, PAD:],
                                               src[:, :, PAD - reach:PAD + SEQ - reach], ALU.add)

            gp.wait_ge(normed_ready, 3 * GT)
            step(window_sum(win_p, normed[:, 2 * GT:3 * GT, :], 1))
            step(window_sum(win_p2, win_p, 2))
            window_sum(win_p, win_p2, 4).then_inc(windows_ready, 1)
            gp.wait_ge(normed_ready, 4 * GT)
            gp.wait_ge(windows_ready, 1)
            step(window_sum(win_p2, normed[:, 3 * GT:4 * GT, :], 1))
            gp.wait_ge(diff_ready, 3)
            step(window_sum(win_p, win_p2, 2))
            step(window_sum(win_p2, win_p, 4))
            window_sum(win_p, win_p2, 8).then_inc(windows_ready, 1)

            def add_square(k, src, d, i=None):
                step(nc.gpsimd.tensor_tensor(square[:, :], src, src, ALU.mult))
                nc.gpsimd.tensor_tensor(square_sum[:, :], square_sum[:, :], square[:, :],
                                        ALU.add).then_inc(squares_added, 1)
                gp.wait_ge(squares_added, plus(squares_before(k) + d + 1, i, 4))

            def start_sum(k):
                gp.wait_ge(stats_summed, k)
                step(nc.gpsimd.memset(square_sum[:, :], 0.0))

            def stream_squares(k, phase):
                start_sum(k)
                start = steps[0]
                with gp.Fori(0, DT // 4) as i:
                    steps[1:] = [i, 4]
                    for d in range(4):
                        gp.wait_ge(evacuated, plus(TILE[phase] + d + 1, i, 4))
                        add_square(k, x[:, plus(d, i, 4), :], d, i)
                steps[:] = [start + DT, None, 0]

            def latent_squares(k, which):
                start_sum(k)
                for d in range(LT):
                    gp.wait_ge(lat_sum, 2 * which + d // 2 + 1)
                    add_square(k, lat_raw[:, d, :], d)

            stream_squares(1, "pool")
            stream_squares(2, "down1")
            latent_squares(3, KV)
            latent_squares(4, Q)
            stream_squares(5, "wo")
            stream_squares(6, "down3")

            gp.wait_ge(rstd_ready, 7)
            gp.wait_ge(y_gained, DT)
            r = rstd[:, :].rearrange("p (o t) -> p o t", o=1).broadcast_to([P, 4, SEQ])
            nc.gpsimd.tensor_tensor(y[:, 12:16, :], y[:, 12:16, :], r, ALU.mult).then_inc(y_done_p, 1)


def shape_constants():
    c = np.zeros((P, C_COLS), np.float32)
    c[:, C_IDENT:C_IDENT + P] = np.eye(P)
    row, col = np.arange(P)[:, None], np.arange(P)[None, :]
    c[:, C_MASK + P:C_MASK + 2 * P] = np.where(col <= row, 0.0, -1.0e30)
    for g, w in enumerate(WINDOWS):
        c[:, C_CORR + g * PAD:C_CORR + (g + 1) * PAD] = w / np.minimum(np.arange(PAD) + 1.0, w)
    half = ROPE // 2
    freq = np.float32(10000.0) ** (-np.arange(half, dtype=np.float32) / np.float32(half))
    c[:, C_FREQ] = np.tile(freq, P // half)
    c[:, C_SIGN] = np.tile(np.repeat([-1.0, 1.0], half), P // ROPE)
    return c


def by_tiles(w, k_per_chunk, tiles_per_chunk):
    k, m = w.shape[0] // P, w.shape[1] // P
    w = w.reshape(k // k_per_chunk, k_per_chunk, P, m // tiles_per_chunk, tiles_per_chunk, P)
    return w.transpose(3, 0, 2, 4, 1, 5).reshape(-1, P, tiles_per_chunk * k_per_chunk * P)


def kernel(**inputs):
    import concourse.bacc as bacc
    from concourse.bass_utils import run_bass_kernel_spmd

    a = {k: np.asarray(v) for k, v in inputs.items()}
    feature_tiles = lambda v: v.reshape(-1, P).T
    qb = a["w_q_b"][0].reshape(LATENT, HEADS, NOPE + ROPE)
    kvb = a["w_kv_b"].reshape(LATENT, HEADS, NOPE + V_DIM)
    values = kvb[:, :, NOPE:].reshape(LT, P, HG, 2 * V_DIM)
    rope_keys = a["w_kv_a"][:, LATENT:].reshape(2, TILES, P, ROPE)
    down = a["w_down"].reshape(4 * FH * P, D_MODEL)
    arrays = {
        "xT": a["x"][0].T.reshape(DT, P, SEQ).transpose(1, 0, 2),
        "positions": a["positions"].reshape(SEQ),
        "consts": shape_constants(),
        "gains": np.concatenate([feature_tiles(v.reshape(-1)) for v in (
            a["pool_norm"], a["pool_scale"], a["kv_in_norm"], a["attn_norm"], a["ffn_norm"][0], a["ffn_norm"][1],
            a["final_norm"], a["kv_latent_norm"], a["q_latent_norm"])], axis=1)[:, :, None],
        "pool_w": np.concatenate([by_tiles(w, GT, 2) for w in a["pool_w"][0]]),
        "w_kv_a": by_tiles(a["w_kv_a"][:, :LATENT], TILES, 1),
        "w_k_pe": rope_keys.transpose(0, 2, 1, 3).reshape(2, P, TILES * ROPE),
        "w_q_a": by_tiles(a["w_q_a"][0], TILES, 1),
        "w_kv_k": by_tiles(kvb[:, :, :NOPE].reshape(LATENT, -1), LT, 2),
        "w_kv_v": values.transpose(2, 1, 0, 3).reshape(HG, P, LT * 2 * V_DIM),
        "w_q_nope": by_tiles(qb[:, :, :NOPE].reshape(LATENT, -1), LT, 2),
        "w_q_pe": by_tiles(qb[:, :, NOPE:].reshape(LATENT, -1), LT, 1),
        "w_o": by_tiles(a["w_o"][0], TILES, 1),
        "w_gate": np.concatenate([by_tiles(w, TILES, 1) for w in a["w_gate"]]),
        "w_up": np.concatenate([by_tiles(w, TILES, 1) for w in a["w_up"]]),
        "w_down": np.concatenate([by_tiles(w, DTILES, 1) for w in np.split(down, 4)]),
    }
    arrays = {k: np.ascontiguousarray(v) for k, v in arrays.items()}

    nc = bacc.Bacc("TRN2", target_bir_lowering=False, num_devices=1)
    args = [nc.dram_tensor(k, v.shape, mybir.dt.from_np(v.dtype), kind="ExternalInput").ap()
            for k, v in arrays.items()]
    out = nc.dram_tensor("out", (P, DT, SEQ), F32, kind="ExternalOutput").ap()
    trunk(nc, *args, out)
    got = run_bass_kernel_spmd(nc, [arrays], core_ids=[0]).results[0]["out"]
    return got.transpose(1, 0, 2).reshape(D_MODEL, SEQ).T.reshape(1, SEQ, D_MODEL)
```

```python
from contextlib import ExitStack

import numpy as np
import concourse.bass as bass
from concourse import mybir

F32 = mybir.dt.float32
F32R = mybir.dt.float32r
I32 = mybir.dt.int32
ALU = mybir.AluOpType
ACT = mybir.ActivationFunctionType

P = 128
SEQ = 256
D_MODEL = 2048
D_FF = 5632
WINDOWS = (2, 4, 8, 16)
HEADS = 16
NOPE, ROPE, V_DIM = 128, 64, 128
LATENT = 512
ATTN_SCALE = 1.0 / float(np.sqrt(NOPE + ROPE))
EPS = 1e-6

DT = D_MODEL // P
LT = LATENT // P
FH = D_FF // P // 2
GROUPS = len(WINDOWS)
GT = DT // GROUPS
PAD = max(WINDOWS)
HG = HEADS // 2
WARM_UP = 16

WEIGHT_SLOTS = 8
SPLIT_SLOTS = 4
TILES = 8
DTILES = FH // 2
BODY = WEIGHT_SLOTS

C_IDENT = 0
C_MASK = C_IDENT + P
C_CORR = C_MASK + 2 * P
C_FREQ = C_CORR + GROUPS * PAD
C_SIGN = C_FREQ + 1
C_COLS = C_SIGN + 1

G_POOL, G_SCALE, G_KV, G_ATTN, G_FFN0, G_FFN1, G_FINAL, G_LKV, G_LQ, G_COLS = (
    0, DT, 2 * DT, 3 * DT, 4 * DT, 5 * DT, 6 * DT, 7 * DT, 7 * DT + LT, 7 * DT + 2 * LT)


def chunk_plan():
    chunks, tiles, c, t = {}, {}, 0, 0
    for name, nc_, nt in (
        ("pool", DT * GT // TILES, DT),
        ("up0", 4 * FH, 2 * FH), ("down0", 2 * DT, DT), ("up1", 4 * FH, 2 * FH), ("down1", 2 * DT, DT),
        ("qa", 2 * LT, LT), ("kva", 2 * LT, LT), ("kpe", 2, 2),
        ("heads", 4 * HG, 8 * HG), ("wo", 2 * DT, DT),
        ("up2", 4 * FH, 2 * FH), ("down2", 2 * DT, DT), ("up3", 4 * FH, 2 * FH), ("down3", 2 * DT, DT),
    ):
        chunks[name], tiles[name] = c, t
        c, t = c + nc_, t + nt
    chunks["end"] = c
    return chunks, tiles


CHUNK, TILE = chunk_plan()

SQUARED = (DT, DT, LT, LT, DT, DT)


def squares_before(k):
    return sum(SQUARED[:k - 1])


def chunk_elems(n):
    for ph in ("down0", "down1", "down2", "down3"):
        if CHUNK[ph] <= n < CHUNK[ph] + 2 * DT:
            return DTILES * P
    if CHUNK["heads"] <= n < CHUNK["wo"] and (n - CHUNK["heads"]) % 4 == 0:
        return TILES * P // 2
    return TILES * P


def made(n):
    return n + 1 - CHUNK["up0"]


def plus(n, i, per):
    return n if i is None else i * per + n


def trunk(nc, xT, positions, consts, gains, pool_w, w_kv_a, w_k_pe, w_q_a, w_kv_k, w_kv_v, w_q_nope, w_q_pe,
          w_o, w_gate, w_up, w_down, out):
    with ExitStack() as ctx:
        def sem(name):
            return ctx.enter_context(nc.semaphore(name))

        def sb(name, shape, dt=F32):
            return ctx.enter_context(nc.sbuf_tensor(name, shape, dt))

        x = sb("x", [P, DT, SEQ])
        raw = sb("raw", [P, WEIGHT_SLOTS, DTILES * P])
        w_hi = sb("w_hi", [P, SPLIT_SLOTS, DTILES * P], F32R)
        w_lo = sb("w_lo", [P, SPLIT_SLOTS, DTILES * P], F32R)
        const = sb("const", [P, C_COLS])
        gain = sb("gain", [P, G_COLS, 1])
        ones = sb("ones", [P, P])
        eps = sb("eps", [P, 1])
        cos = sb("cos", [P, SEQ])
        sin = sb("sin", [P, SEQ])
        root = sb("root", [P, SEQ])
        rstd = sb("rstd", [P, SEQ])
        square = sb("square", [P, SEQ])
        square_sum = sb("square_sum", [P, SEQ])
        cross = sb("cross", [P, 2, SEQ])
        sums = sb("sums", [P, 2, SEQ])
        gate_act = sb("gate_act", [P, SEQ])
        product = sb("product", [P, SEQ])

        KB = 1024
        region_at = nc.sbuf_base
        sb("region", [P, 80 * KB // 4])
        scratch_at = nc.sbuf_base
        sb("scratch", [P, (9 * KB + 64) // 4])

        def at(name, shape, dt, offset):
            return nc.alloc_sbuf_tensor_at(name, shape, dt, offset=offset)

        xg = at("xg", [P, DT, 2 * SEQ], F32R, region_at)
        act = at("act", [P, FH, 2 * SEQ], F32R, region_at + 32 * KB)
        PR = PAD + SEQ
        grp = GT * PR * 4
        pool_at = region_at + 32 * KB
        x_square = at("x_square", [P, DT, SEQ], F32, pool_at)
        pooled = at("pooled", [P, DT, SEQ], F32, pool_at)
        normed = at("normed", [P, DT, PR], F32, pool_at + 16 * KB)
        win_v = at("win_v", [P, GT, PR], F32, pool_at + 16 * KB + 4 * grp)
        win_v2 = at("win_v2", [P, GT, PR], F32, pool_at + 16 * KB + 5 * grp)
        win_p = at("win_p", [P, GT, PR], F32, pool_at + 16 * KB + 6 * grp)
        win_p2 = at("win_p2", [P, GT, PR], F32, scratch_at)
        xk = at("xk", [P, DT, 2 * SEQ], F32R, region_at + 32 * KB)
        latent = at("latent", [P, 2, LT, 2 * SEQ], F32R, region_at + 64 * KB)
        lat_raw = at("lat_raw", [P, LT, SEQ], F32, scratch_at)
        lat_rstd = at("lat_rstd", [P, SEQ], F32, scratch_at + 6 * KB)
        k_buf = at("k_buf", [P, 2, 2, 2 * SEQ], F32R, region_at)
        q_buf = at("q_buf", [P, 2, 2, 2 * SEQ], F32R, region_at + 8 * KB)
        v_buf = at("v_buf", [P, 2, 2, 2, 2 * V_DIM], F32R, region_at + 16 * KB)
        qpe_buf = at("qpe_buf", [P, 2, 2 * SEQ], F32R, region_at + 24 * KB)
        kpe_buf = at("kpe_buf", [P, 2, 2 * SEQ], F32R, region_at + 28 * KB)
        heads = at("heads", [P, HEADS, 2 * SEQ], F32R, region_at + 32 * KB)
        prob = at("prob", [P, 2, 3 * P], F32, scratch_at)
        probT = at("probT", [P, 2, 2, 3 * P], F32R, scratch_at + 3 * KB)
        stat = at("stat", [P, 2, 8], F32, scratch_at + 9 * KB)
        y = at("y", [P, DT, SEQ], F32, region_at)
        pos_i = at("pos_i", [P, SEQ], I32, scratch_at + 4 * KB + KB // 2)
        angle = at("angle", [P, SEQ], F32, scratch_at)
        turns = at("turns", [P, SEQ], F32, scratch_at + KB)

        ps = ctx.enter_context(nc.psum_tensor("ps", [P, 8, 512], F32))
        SCORES, HEADS_OUT, STATS = 4, 6, 7

        x_landed = [sem(f"x_landed{q}") for q in range(4)]
        const_landed = sem("const_landed")
        landed = [sem(f"landed{s}") for s in range(WEIGHT_SLOTS)]
        hi_ready = sem("hi_ready")
        lo_ready = sem("lo_ready")
        chunks_used = sem("chunks_used")
        evacuated = sem("evacuated")
        xg_hi = sem("xg_hi")
        xg_ready = sem("xg_ready")
        cross_ready = sem("cross_ready")
        sums_ready = sem("sums_ready")
        gate_ready = sem("gate_ready")
        product_ready = sem("product_ready")
        act_hi = sem("act_hi")
        act_ready = sem("act_ready")
        squares_added = sem("squares_added")
        stats_summed = sem("stats_summed")
        root_ready = sem("root_ready")
        rstd_ready = sem("rstd_ready")
        squares_ready = sem("squares_ready")
        init_ready = sem("init_ready")
        windows_ready = sem("windows_ready")
        normed_ready = sem("normed_ready")
        diff_ready = sem("diff_ready")
        angle_ready = sem("angle_ready")
        table_ready = sem("table_ready")
        pos_landed = sem("pos_landed")
        lat_sum = sem("lat_sum")
        lat_scaled = sem("lat_scaled")
        lat_hi = sem("lat_hi")
        lat_ready = sem("lat_ready")
        proj_hi = sem("proj_hi")
        rope_sum = sem("rope_sum")
        rope_swapped = sem("rope_swapped")
        rope_done = sem("rope_done")
        k_ready = sem("k_ready")
        q_ready = sem("q_ready")
        qpe_ready = sem("qpe_ready")
        kpe_ready = sem("kpe_ready")
        scores_ready = sem("scores_ready")
        max_ready = sem("max_ready")
        exp_ready = sem("exp_ready")
        prob_ready = sem("prob_ready")
        probT_ready = sem("probT_ready")
        probT_hi = sem("probT_hi")
        probT_split = sem("probT_split")
        head_ready = sem("head_ready")
        head_hi = sem("head_hi")
        head_split = sem("head_split")
        y_gained = sem("y_gained")
        y_done_v = sem("y_done_v")
        y_done_p = sem("y_done_p")
        stored = sem("stored")
        v_step = sem("v_step")
        p_step = sem("p_step")

        block = ctx.enter_context(nc.Block())

        KV, Q = 0, 1
        INIT = 8
        UPS = ("up0", "up1", "up2", "up3")
        DOWNS = ("down0", "down1", "down2", "down3")

        @block.sync
        def _(sp):
            def load(n, src, i=None):
                before = n - WEIGHT_SLOTS
                if before >= CHUNK["up0"]:
                    sp.wait_ge(lo_ready, plus(made(before), i, BODY))
                elif before >= 0:
                    sp.wait_ge(chunks_used, before + 1)
                sp.dma_start(raw[:, n % WEIGHT_SLOTS, 0:chunk_elems(n)], src).then_inc(landed[n % WEIGHT_SLOTS], 16)

            for q in range(4):
                sp.dma_start(x[:, 4 * q:4 * q + 4, :], xT[:, 4 * q:4 * q + 4, :]).then_inc(x_landed[q], 16)
            sp.dma_start(const[:, :], consts).then_inc(const_landed, 16)
            sp.dma_start(gain[:, :, :], gains).then_inc(const_landed, 16)
            sp.dma_start(pos_i[:, :], positions.partition_broadcast(P)).then_inc(pos_landed, 16)
            for c in range(CHUNK["up0"]):
                load(CHUNK["pool"] + c, pool_w[c])

            def ffn(layer, half):
                up, down = UPS[2 * layer + half], DOWNS[2 * layer + half]

                def up_body(b, i=None):
                    for c in range(BODY * b, BODY * (b + 1)):
                        w = w_gate if c % 4 < 2 else w_up
                        row = ((layer * 2 + half) * FH + c // 4) * 2 + c % 2
                        load(CHUNK[up] + c, w[plus(row, i, 4)], i)

                peel = 1 if up == "up0" else 0
                for b in range(peel):
                    up_body(b)
                with sp.Fori(0, FH // 2 - peel) as i:
                    up_body(peel, i)
                with sp.Fori(0, DT // 4) as i:
                    for c in range(BODY):
                        load(CHUNK[down] + c, w_down[plus((layer * 2 + half) * DT * 2 + c, i, BODY)], i)

            ffn(0, 0)
            ffn(0, 1)
            for c in range(2 * LT):
                load(CHUNK["qa"] + c, w_q_a[c])
            for c in range(2 * LT):
                load(CHUNK["kva"] + c, w_kv_a[c])
            for c in range(2):
                n = CHUNK["kpe"] + c
                sp.wait_ge(lo_ready, made(n - WEIGHT_SLOTS))
                sp.dma_start(raw[:, n % WEIGHT_SLOTS, 0:TILES * ROPE], w_k_pe[c]).then_inc(
                    landed[n % WEIGHT_SLOTS], 16)
            with sp.Fori(0, HG // 2) as i:
                for g in range(2):
                    for c, w in enumerate((w_q_pe, w_q_nope, w_kv_k, w_kv_v)):
                        load(CHUNK["heads"] + 4 * g + c, w[plus(g, i, 2)], i)
            with sp.Fori(0, DT // 4) as i:
                for c in range(BODY):
                    load(CHUNK["wo"] + c, w_o[plus(2 * (c % 4) + c // 4, i, BODY)], i)
            ffn(1, 0)
            ffn(1, 1)

            for q in range(4):
                if q < 3:
                    sp.wait_ge(y_done_v, q + 1)
                else:
                    sp.wait_ge(y_done_p, 1)
                sp.dma_start(out[:, 4 * q:4 * q + 4, :], y[:, 4 * q:4 * q + 4, :]).then_inc(stored, 16)
            sp.wait_ge(stored, 64)

        @block.tensor
        def _(pe):
            def product3(n, j, bank, moving, start, stop):
                s = n % SPLIT_SLOTS
                pe.matmul(ps[:, bank, :], w_hi[:, s, j * P:(j + 1) * P], moving, start=start, stop=False)
                return pe.matmul(ps[:, bank, 0:SEQ], w_lo[:, s, j * P:(j + 1) * P], moving[:, 0:SEQ],
                                 start=False, stop=stop)

            def bank_free(t, i=None, per=0):
                if t >= 4:
                    pe.wait_ge(evacuated, plus(t - 3, i, per))

            def long_tile(n, t, operand, kts, i=None, per=0, each=None):
                for c in range(2):
                    pe.wait_ge(lo_ready, plus(made(n + c), i, BODY))
                    if c == 0:
                        bank_free(t, i, per)
                    for j in range(kts):
                        kt = c * kts + j
                        if each is not None:
                            each(kt)
                        mm = product3(n + c, j, t % 4, operand[:, kt, :], kt == 0, kt == 2 * kts - 1)
                    mm.then_inc(chunks_used, 1)

            def sum_over_partitions(k):
                pe.wait_ge(squares_added, squares_before(k + 1))
                pe.wait_ge(root_ready, k)
                pe.matmul(ps[:, STATS, 0:SEQ], ones[:, :], square_sum[:, :], start=True,
                          stop=True).then_inc(stats_summed, 1)

            pe.wait_ge(init_ready, INIT)
            for _ in range(WARM_UP):
                pe.matmul(ps[:, SCORES, 0:P], ones[:, :], ones[:, :], start=True, stop=True)
            for t in range(DT):
                if t % 4 == 0:
                    pe.wait_ge(squares_ready, t // 4 + 1)
                mm = pe.matmul(ps[:, STATS, 0:SEQ], ones[:, :], x_square[:, t, :], start=(t == 0),
                               stop=(t == DT - 1))
            mm.then_inc(stats_summed, 1)

            for c in range(CHUNK["up0"]):
                if c % 2 == 0:
                    pe.wait_ge(diff_ready, c // 2 + 1)
                pe.wait_ge(landed[c], 16)
                for m in range(2):
                    t = TILE["pool"] + 2 * c + m
                    bank_free(t)
                    for kt in range(GT):
                        j = m * GT + kt
                        mm = pe.matmul(ps[:, t % 4, 0:SEQ], raw[:, c, j * P:(j + 1) * P],
                                       pooled[:, c // 2 * GT + kt, :], start=(kt == 0), stop=(kt == GT - 1))
                mm.then_inc(chunks_used, 1)

            def ffn(layer, half, xg_before, stats):
                p = 2 * layer + half
                n0, t0 = CHUNK[UPS[p]], TILE[UPS[p]]
                peel = 0
                if half == 0:
                    peel = 1
                    long_tile(n0, t0, xg, TILES, each=lambda kt: pe.wait_ge(xg_ready, xg_before + kt + 1))
                    long_tile(n0 + 2, t0 + 1, xg, TILES)
                    sum_over_partitions(stats)
                    long_tile(n0 + 4, t0 + 2, xg, TILES)
                    long_tile(n0 + 6, t0 + 3, xg, TILES)
                with pe.Fori(0, FH // 2 - peel) as i:
                    for f in range(4):
                        long_tile(n0 + BODY * peel + 2 * f, t0 + 4 * peel + f, xg, TILES, i, 4)
                n0, t0 = CHUNK[DOWNS[p]], TILE[DOWNS[p]]
                long_tile(n0, t0, act, DTILES, each=lambda kt: pe.wait_ge(act_ready, p * FH + kt + 1))
                for d in range(1, 4):
                    long_tile(n0 + 2 * d, t0 + d, act, DTILES)
                with pe.Fori(0, DT // 4 - 1) as i:
                    for d in range(4):
                        long_tile(n0 + BODY + 2 * d, t0 + 4 + d, act, DTILES, i, 4)

            ffn(0, 0, 0, 1)
            ffn(0, 1, None, None)

            for m in range(LT):
                long_tile(CHUNK["qa"] + 2 * m, TILE["qa"] + m, xg, TILES,
                          each=(lambda kt: pe.wait_ge(xg_ready, DT + kt + 1)) if m == 0 else None)
                if m == 0:
                    sum_over_partitions(2)
            for m in range(LT):
                long_tile(CHUNK["kva"] + 2 * m, TILE["kva"] + m, xk, TILES,
                          each=(lambda kt: pe.wait_ge(xg_ready, 2 * DT + kt + 1)) if m == 0 else None)
                if m == 1:
                    sum_over_partitions(3)
            long_tile(CHUNK["kpe"], TILE["kpe"], xk, TILES)

            def key_part(g, i=None):
                n, t = CHUNK["heads"] + 4 * g + 2, TILE["heads"] + 8 * g + 4
                pe.wait_ge(lo_ready, plus(made(n), i, BODY))
                for m in range(2):
                    bank_free(t + m, i, 16)
                    for kt in range(LT):
                        mm = product3(n, m * LT + kt, (t + m) % 4, latent[:, KV, kt, :], kt == 0, kt == LT - 1)
                mm.then_inc(chunks_used, 1)

            def value_part(g, i=None):
                n, t = CHUNK["heads"] + 4 * g + 3, TILE["heads"] + 8 * g + 6
                s = n % SPLIT_SLOTS
                pe.wait_ge(lo_ready, plus(made(n), i, BODY))
                for m in range(2):
                    bank_free(t + m, i, 16)
                    dst = ps[:, (t + m) % 4, 0:2 * V_DIM]
                    for kt in range(LT):
                        wh = w_hi[:, s, kt * 2 * V_DIM:(kt + 1) * 2 * V_DIM]
                        wl = w_lo[:, s, kt * 2 * V_DIM:(kt + 1) * 2 * V_DIM]
                        c_hi = latent[:, KV, kt, m * P:(m + 1) * P]
                        c_lo = latent[:, KV, kt, SEQ + m * P:SEQ + (m + 1) * P]
                        pe.matmul(dst, c_hi, wh, start=(kt == 0), stop=False)
                        pe.matmul(dst, c_hi, wl, start=False, stop=False)
                        mm = pe.matmul(dst, c_lo, wh, start=False, stop=(kt == LT - 1))
                mm.then_inc(chunks_used, 1)

            def query_rope_part(g, i=None):
                n, t = CHUNK["heads"] + 4 * g, TILE["heads"] + 8 * g
                pe.wait_ge(lo_ready, plus(made(n), i, BODY))
                bank_free(t, i, 16)
                for kt in range(LT):
                    mm = product3(n, kt, t % 4, latent[:, Q, kt, :], kt == 0, kt == LT - 1)
                mm.then_inc(chunks_used, 1)

            def query_part(g, i=None):
                n, t = CHUNK["heads"] + 4 * g + 1, TILE["heads"] + 8 * g + 2
                pe.wait_ge(lo_ready, plus(made(n), i, BODY))
                for m in range(2):
                    bank_free(t + m, i, 16)
                    for kt in range(LT):
                        mm = product3(n, m * LT + kt, (t + m) % 4, latent[:, Q, kt, :], kt == 0, kt == LT - 1)
                mm.then_inc(chunks_used, 1)

            def scores(g, hh, i=None):
                b = g % 2
                if hh == 0:
                    pe.wait_ge(k_ready, plus(g + 1, i, 2))
                    pe.wait_ge(qpe_ready, plus(g + 1, i, 2))
                    pe.wait_ge(q_ready, plus(g + 1, i, 2))
                    if g >= 1:
                        pe.wait_ge(probT_split, plus(g, i, 2))
                for qt in range(2):
                    nk = (qt + 1) * P
                    dst = ps[:, SCORES + hh, qt * P:qt * P + nk]
                    pairs = ((q_buf[:, b, hh, :], k_buf[:, b, hh, :]), (qpe_buf[:, b, :], kpe_buf[:, hh, :]))
                    for part, (q, k) in enumerate(pairs):
                        q_hi, q_lo = q[:, qt * P:(qt + 1) * P], q[:, SEQ + qt * P:SEQ + (qt + 1) * P]
                        k_hi, k_lo = k[:, 0:nk], k[:, SEQ:SEQ + nk]
                        pe.matmul(dst, q_hi, k_hi, start=(part == 0), stop=False)
                        pe.matmul(dst, q_hi, k_lo, start=False, stop=False)
                        mm = pe.matmul(dst, q_lo, k_hi, start=False, stop=(part == 1))
                mm.then_inc(scores_ready, 1)

            def turn_probs(g, hh, i=None):
                pe.wait_ge(prob_ready, plus(2 * g + hh + 1, i, 4))
                for c in range(3):
                    mm = pe.transpose(ps[:, SCORES + hh, c * P:(c + 1) * P], prob[:, hh, c * P:(c + 1) * P],
                                      const[:, C_IDENT:C_IDENT + P])
                mm.then_inc(probT_ready, 1)

            def head_output(g, hh, i=None):
                b = g % 2
                if hh == 0:
                    pe.wait_ge(evacuated, plus(TILE["heads"] + 8 * g + 8, i, 16))
                    pe.wait_ge(probT_split, plus(g + 1, i, 2))
                    if g >= 1:
                        pe.wait_ge(head_split, plus(g, i, 2))
                for kt in range(2):
                    v_hi = v_buf[:, b, kt, 0, hh * V_DIM:(hh + 1) * V_DIM]
                    v_lo = v_buf[:, b, kt, 1, hh * V_DIM:(hh + 1) * V_DIM]
                    cols = slice(0, 2 * P) if kt == 0 else slice(2 * P, 3 * P)
                    dst = ps[:, HEADS_OUT + hh, kt * P:SEQ]
                    pe.matmul(dst, v_hi, probT[:, hh, 0, cols], start=(kt == 0), stop=False)
                    pe.matmul(dst, v_hi, probT[:, hh, 1, cols], start=False, stop=False)
                    mm = pe.matmul(dst, v_lo, probT[:, hh, 0, cols], start=False, stop=(kt == 1))
                mm.then_inc(head_ready, 1)

            def wo_part(c, i=None, each=None):
                n, t = CHUNK["wo"] + c, TILE["wo"] + 4 * (c // BODY) + c % 4
                half = c // 4 % 2
                pe.wait_ge(lo_ready, plus(made(n), i, BODY))
                if half == 0:
                    bank_free(t, i, 4)
                for j in range(TILES):
                    kt = half * TILES + j
                    if each is not None:
                        each(kt)
                    mm = product3(n, j, t % 4, heads[:, kt, :], kt == 0, kt == DT - 1)
                mm.then_inc(chunks_used, 1)

            def slot(g, i=None):
                own = g < HG
                if own:
                    query_rope_part(g, i)
                if g >= 1:
                    scores(g - 1, 0, i)
                    scores(g - 1, 1, i)
                if own:
                    query_part(g, i)
                    if g == 0:
                        pe.wait_ge(lat_ready, 2 * LT)
                    key_part(g, i)
                else:
                    wo_part(0)
                    wo_part(1)
                if g >= 1:
                    turn_probs(g - 1, 0, i)
                    turn_probs(g - 1, 1, i)
                if own:
                    value_part(g, i)
                else:
                    wo_part(2)
                if g >= 1:
                    head_output(g - 1, 0, i)
                    head_output(g - 1, 1, i)

            sum_over_partitions(4)
            pe.wait_ge(lat_ready, LT)
            slot(0)
            slot(1)
            with pe.Fori(0, HG // 2 - 1) as i:
                slot(2, i)
                slot(3, i)
            slot(HG)

            wo_part(3)
            wo_part(4, each=lambda kt: pe.wait_ge(head_split, kt // 2 + 1))
            for c in range(5, BODY):
                wo_part(c)
            with pe.Fori(0, DT // 4 - 1) as i:
                for c in range(BODY, 2 * BODY):
                    wo_part(c, i)

            ffn(1, 0, 3 * DT, 5)
            ffn(1, 1, None, None)
            sum_over_partitions(6)

        @block.scalar
        def _(sc):
            def split(n, i=None):
                if n >= CHUNK["end"]:
                    return
                e = chunk_elems(n)
                src = raw[:, n % WEIGHT_SLOTS, 0:e]
                if CHUNK["kpe"] <= n < CHUNK["kpe"] + 2:
                    src = raw[:, n % WEIGHT_SLOTS, 0:TILES * ROPE].rearrange("p (k o c) -> p k o c", k=TILES, o=1)
                    src = src.broadcast_to([P, TILES, 2, ROPE])
                sc.wait_ge(landed[n % WEIGHT_SLOTS], plus(16 * (n // WEIGHT_SLOTS + 1), i, 16))
                if n >= CHUNK["up0"] + SPLIT_SLOTS:
                    sc.wait_ge(chunks_used, plus(n - SPLIT_SLOTS + 1, i, BODY))
                dst = w_hi[:, n % SPLIT_SLOTS, 0:e]
                if CHUNK["kpe"] <= n < CHUNK["kpe"] + 2:
                    dst = dst.rearrange("p (k o c) -> p k o c", k=TILES, o=2)
                nc.scalar.activation(dst, src, ACT.Copy).then_inc(hi_ready, 1)

            def root_of(k, features):
                sc.wait_ge(stats_summed, k)
                if k >= 2:
                    sc.wait_ge(rstd_ready, k - 1)
                nc.scalar.activation(root[:, :], ps[:, STATS, 0:SEQ], ACT.Sqrt, bias=eps[:, :],
                                     scale=1.0 / features).then_inc(root_ready, 1)

            def gained(t, tile_count, col, dst, i=None, per=0):
                sc.wait_ge(evacuated, plus(tile_count, i, per))
                nc.scalar.activation(dst[:, plus(t, i, per), 0:SEQ], x[:, plus(t, i, per), :], ACT.Identity,
                                     scale=gain[:, plus(col + t, i, per), :]).then_inc(xg_hi, 1)

            for q in range(4):
                sc.wait_ge(x_landed[q], 16)
                nc.scalar.activation(x_square[:, 4 * q:4 * q + 4, :], x[:, 4 * q:4 * q + 4, :],
                                     ACT.Square).then_inc(squares_ready, 1)
            sc.wait_ge(init_ready, INIT)
            root_of(1, D_MODEL)
            sc.wait_ge(const_landed, 32)

            for t in range(DT):
                gained(t, TILE["pool"] + t + 1, G_FFN0, xg)
                if t >= DT - SPLIT_SLOTS:
                    split(CHUNK["up0"] + t - (DT - SPLIT_SLOTS))

            def ffn_tile(p, f, splits, i=None):
                n, t = CHUNK[UPS[p]] + 4 * f, TILE[UPS[p]] + 2 * f
                bank = t % 4
                sc.wait_ge(chunks_used, plus(n + 4, i, BODY))
                nc.scalar.activation(cross[:, :, :], ps[:, bank:bank + 2, SEQ:], ACT.Copy).then_inc(cross_ready, 1)
                splits[0]()
                sc.wait_ge(sums_ready, plus(p * FH + f + 1, i, 2))
                nc.scalar.activation(gate_act[:, :], sums[:, 0, :], ACT.Silu).then_inc(gate_ready, 1)
                splits[1]()
                sc.wait_ge(product_ready, plus(p * FH + f + 1, i, 2))
                nc.scalar.activation(act[:, plus(f, i, 2), 0:SEQ], product[:, :], ACT.Copy).then_inc(act_hi, 1)
                splits[2]()

            def ffn(layer, half, stats):
                p = 2 * layer + half
                n0 = CHUNK[UPS[p]]
                for w in range(3):
                    split(n0 + w + SPLIT_SLOTS)
                if stats is not None:
                    root_of(stats, D_MODEL)

                def tile(f, i=None):
                    n = n0 + 4 * f + 3 + SPLIT_SLOTS
                    ffn_tile(p, f, (lambda: split(n, i), lambda: split(n + 1, i),
                                    lambda: (split(n + 2, i), split(n + 3, i))), i)

                with sc.Fori(0, FH // 2 - 1) as i:
                    tile(0, i)
                    tile(1, i)
                tile(FH - 2)
                nothing = lambda: None
                ffn_tile(p, FH - 1, (nothing, nothing, lambda: split(n0 + 4 * FH - 1 + SPLIT_SLOTS)))

                n1, t1 = CHUNK[DOWNS[p]], TILE[DOWNS[p]]

                def down(d, i=None):
                    split(n1 + 2 * d + SPLIT_SLOTS, i)
                    if half == 1 and layer == 0:
                        gained(d, t1 + d + 1, G_ATTN, xg, i, 4)
                    if half == 1 and layer == 1:
                        sc.wait_ge(evacuated, plus(t1 + d + 1, i, 4))
                        nc.scalar.activation(y[:, plus(d, i, 4), :], x[:, plus(d, i, 4), :], ACT.Identity,
                                             scale=gain[:, plus(G_FINAL + d, i, 4), :]).then_inc(y_gained, 1)
                    split(n1 + 2 * d + 1 + SPLIT_SLOTS, i)

                with sc.Fori(0, DT // 4 - 1) as i:
                    for d in range(4):
                        down(d, i)
                for d in range(DT - 4, DT):
                    down(d)

            ffn(0, 0, 2)
            sc.wait_ge(angle_ready, 1)
            nc.scalar.activation(sin[:, :], angle[:, :], ACT.Sin).then_inc(table_ready, 1)
            nc.scalar.activation(cos[:, :], turns[:, :], ACT.Sin).then_inc(table_ready, 1)
            ffn(0, 1, None)

            xk_tiles = iter(range(DT))

            def xk_some(k):
                for _ in range(k):
                    gained(next(xk_tiles), TILE["qa"], G_KV, xk)

            def lat_pair(name, m):
                n, t = CHUNK[name] + 2 * m, TILE[name] + m
                sc.wait_ge(chunks_used, n + 4)
                sc.wait_ge(evacuated, t)
                nc.scalar.activation(cross[:, :, :], ps[:, t % 4:t % 4 + 2, SEQ:], ACT.Copy).then_inc(cross_ready, 1)

            def lat_split(which, number, col):
                sc.wait_ge(lat_scaled, number + 1)
                for t in range(LT):
                    nc.scalar.activation(latent[:, which, t, 0:SEQ], lat_raw[:, t, :], ACT.Identity,
                                         scale=gain[:, col + t, :]).then_inc(lat_hi, 1)

            n0 = CHUNK["qa"]
            for w in range(3):
                split(n0 + w + SPLIT_SLOTS)
                xk_some(2)
                if w == 1:
                    root_of(3, D_MODEL)
            lat_pair("qa", 0)
            for w in range(3, 7):
                split(n0 + w + SPLIT_SLOTS)
                xk_some(2)
            lat_pair("qa", 2)
            split(n0 + 7 + SPLIT_SLOTS)
            xk_some(2)
            for w in range(8, 11):
                split(n0 + w + SPLIT_SLOTS)
            lat_pair("kva", 0)
            split(n0 + 11 + SPLIT_SLOTS)
            root_of(4, LATENT)
            lat_split(Q, 0, G_LQ)
            split(n0 + 12 + SPLIT_SLOTS)
            split(n0 + 13 + SPLIT_SLOTS)
            split(n0 + 14 + SPLIT_SLOTS)
            lat_pair("kva", 2)
            split(n0 + 15 + SPLIT_SLOTS)
            split(n0 + 16 + SPLIT_SLOTS)

            def swap_halves():
                for q in range(4):
                    nc.scalar.activation(product[32 * q:32 * q + 32, :], gate_act[32 * (q ^ 1):32 * (q ^ 1) + 32, :],
                                         ACT.Copy).then_inc(rope_swapped, 1)

            sc.wait_ge(chunks_used, CHUNK["kpe"] + 2)
            sc.wait_ge(evacuated, TILE["kpe"])
            b = TILE["kpe"] % 4
            nc.scalar.activation(cross[:, 0, :], ps[:, b, SEQ:], ACT.Copy).then_inc(cross_ready, 1)
            split(n0 + 17 + SPLIT_SLOTS)
            sc.wait_ge(rope_sum, 1)
            swap_halves()
            root_of(5, LATENT)
            lat_split(KV, 1, G_LKV)
            sc.wait_ge(rope_done, 1)
            for hh in range(2):
                rows = slice(64 * hh, 64 * hh + 64)
                nc.scalar.activation(kpe_buf[rows, hh, 0:SEQ], gate_act[rows, :], ACT.Copy).then_inc(proj_hi, 1)

            def pair_hi(g, part, dst, i):
                n, t = CHUNK["heads"] + 4 * g + part, TILE["heads"] + 8 * g + 2 * part
                sc.wait_ge(chunks_used, plus(n + 1, i, BODY))
                sc.wait_ge(evacuated, plus(t, i, 16))
                nc.scalar.activation(cross[:, :, :], ps[:, t % 4:t % 4 + 2, SEQ:], ACT.Copy).then_inc(cross_ready, 1)
                sc.wait_ge(evacuated, plus(t + 2, i, 16))
                nc.scalar.activation(dst[:, g % 2, :, 0:SEQ], sums[:, :, :], ACT.Copy).then_inc(proj_hi, 1)

            def value_hi(g, i):
                n, t = CHUNK["heads"] + 4 * g + 3, TILE["heads"] + 8 * g + 6
                sc.wait_ge(chunks_used, plus(n + 1, i, BODY))
                nc.scalar.activation(v_buf[:, g % 2, :, 0, :], ps[:, t % 4:t % 4 + 2, 0:2 * V_DIM],
                                     ACT.Copy).then_inc(proj_hi, 1)

            def rope_cross(g, i):
                n, t = CHUNK["heads"] + 4 * g, TILE["heads"] + 8 * g
                sc.wait_ge(chunks_used, plus(n + 1, i, BODY))
                sc.wait_ge(evacuated, plus(t, i, 16))
                nc.scalar.activation(cross[:, 0, :], ps[:, t % 4, SEQ:], ACT.Copy).then_inc(cross_ready, 1)

            def rope_hi(g, i):
                sc.wait_ge(rope_done, plus(g + 2, i, 2))
                nc.scalar.activation(qpe_buf[:, g % 2, 0:SEQ], gate_act[:, :], ACT.Copy).then_inc(proj_hi, 1)

            def probT_hi_half(g, i):
                sc.wait_ge(probT_ready, plus(2 * g + 2, i, 4))
                nc.scalar.activation(probT[:, :, 0, :], ps[:, SCORES:SCORES + 2, 0:3 * P],
                                     ACT.Copy).then_inc(probT_hi, 1)

            def heads_hi_half(g, i):
                sc.wait_ge(head_ready, plus(2 * g + 2, i, 4))
                for hh in range(2):
                    nc.scalar.activation(heads[:, plus(2 * g + hh, i, 4), 0:SEQ], ps[:, HEADS_OUT + hh, 0:SEQ],
                                         ACT.Copy).then_inc(head_hi, 1)

            def exps(g, hh, i):
                sc.wait_ge(max_ready, plus(2 * g + hh + 1, i, 4))
                nc.scalar.activation(prob[:, hh, 0:P], prob[:, hh, 0:P], ACT.Exp, bias=stat[:, hh, 2:3],
                                     accum_out=stat[:, hh, 4:5]).then_inc(exp_ready, 1)
                nc.scalar.activation(prob[:, hh, P:], prob[:, hh, P:], ACT.Exp, bias=stat[:, hh, 3:4],
                                     accum_out=stat[:, hh, 5:6]).then_inc(exp_ready, 1)

            def slot(g, i=None):
                n = CHUNK["heads"] + 4 * g
                if g >= 2:
                    heads_hi_half(g - 2, i)
                rope_cross(g, i)
                split(n + SPLIT_SLOTS, i)
                sc.wait_ge(evacuated, plus(TILE["heads"] + 8 * g + 2, i, 16))
                swap_halves()
                if g >= 1:
                    exps(g - 1, 0, i)
                    exps(g - 1, 1, i)
                pair_hi(g, 1, q_buf, i)
                split(n + 1 + SPLIT_SLOTS, i)
                if g >= 1:
                    probT_hi_half(g - 1, i)
                pair_hi(g, 2, k_buf, i)
                split(n + 2 + SPLIT_SLOTS, i)
                value_hi(g, i)
                split(n + 3 + SPLIT_SLOTS, i)
                rope_hi(g, i)

            slot(0)
            slot(1)
            with sc.Fori(0, HG // 2 - 2) as i:
                slot(2, i)
                slot(3, i)
            slot(HG - 2)
            slot(HG - 1)

            n1, t1 = CHUNK["wo"], TILE["wo"]
            heads_hi_half(HG - 2, None)
            exps(HG - 1, 0, None)
            exps(HG - 1, 1, None)
            split(n1 + SPLIT_SLOTS)
            split(n1 + 1 + SPLIT_SLOTS)
            probT_hi_half(HG - 1, None)
            split(n1 + 2 + SPLIT_SLOTS)
            heads_hi_half(HG - 1, None)
            split(n1 + 3 + SPLIT_SLOTS)

            def wo(c, i=None):
                if c // 4 % 2:
                    d = 4 * (c // BODY) + c % 4
                    gained(d, t1 + d + 1, G_FFN1, xg, i, 4)
                split(n1 + c + SPLIT_SLOTS, i)

            for c in range(4, BODY):
                wo(c)
            with sc.Fori(0, DT // 4 - 1) as i:
                for c in range(BODY, 2 * BODY):
                    wo(c, i)
            ffn(1, 0, 6)
            ffn(1, 1, None)
            root_of(7, D_MODEL)

        @block.vector
        def _(ve):
            steps = [0, None, 0]

            def step(ins):
                steps[0] += 1
                ins.then_inc(v_step, 1)
                ve.wait_ge(v_step, plus(steps[0], steps[1], steps[2]))

            def loop(count, per, body):
                with ve.Fori(0, count) as i:
                    start = steps[0]
                    steps[1:] = [i, per]
                    body(i)
                    assert steps[0] - start == per, (steps[0] - start, per)
                steps[:] = [start + per * count, None, 0]

            crossed = [0]

            def split(n, i=None):
                if n >= CHUNK["end"]:
                    return
                e = chunk_elems(n)
                src, hi, lo = raw[:, n % WEIGHT_SLOTS, 0:e], w_hi[:, n % SPLIT_SLOTS, 0:e], w_lo[:, n % SPLIT_SLOTS, 0:e]
                if CHUNK["kpe"] <= n < CHUNK["kpe"] + 2:
                    src = raw[:, n % WEIGHT_SLOTS, 0:TILES * ROPE].rearrange("p (k o c) -> p k o c", k=TILES, o=1)
                    src = src.broadcast_to([P, TILES, 2, ROPE])
                    hi = hi.rearrange("p (k o c) -> p k o c", k=TILES, o=2)
                    lo = lo.rearrange("p (k o c) -> p k o c", k=TILES, o=2)
                ve.wait_ge(hi_ready, plus(made(n), i, BODY))
                nc.vector.tensor_tensor(lo, src, hi.bitcast(F32), ALU.subtract).then_inc(lo_ready, 1)

            def rstd_of(k):
                ve.wait_ge(root_ready, k)
                nc.vector.reciprocal(rstd[:, :], root[:, :]).then_inc(rstd_ready, 1)
                ve.wait_ge(rstd_ready, k)

            xgs = [0]

            def gained(t, col, dst, number, i=None, per=0):
                ve.wait_ge(xg_hi, plus(number, i, per))
                nc.vector.scalar_tensor_tensor(
                    dst[:, plus(t, i, per), SEQ:], x[:, plus(t, i, per), :], gain[:, plus(col + t, i, per), :],
                    dst[:, plus(t, i, per), 0:SEQ].bitcast(F32), ALU.mult, ALU.subtract).then_inc(xg_ready, 1)

            def rope_angles():
                step(nc.vector.tensor_copy(turns[:, :], pos_i[:, :]))
                step(nc.vector.tensor_scalar(angle[:, :], turns[:, :], const[:, C_FREQ:C_FREQ + 1], None, ALU.mult))
                magic = 1.5 * 2.0 ** 23
                step(nc.vector.tensor_scalar(turns[:, :], angle[:, :], 1.0 / (2.0 * np.pi), None, ALU.mult))
                step(nc.vector.tensor_scalar(turns[:, :], turns[:, :], magic, None, ALU.add))
                step(nc.vector.tensor_scalar(turns[:, :], turns[:, :], -magic, None, ALU.add))
                rest = 2.0 * np.pi
                for part in range(5):
                    e = np.floor(np.log2(rest)) - 7
                    c = float(np.floor(rest / 2.0 ** e) * 2.0 ** e) if part < 4 else float(np.float32(rest))
                    rest -= c
                    step(nc.vector.scalar_tensor_tensor(angle[:, :], turns[:, :], -c, angle[:, :], ALU.mult, ALU.add))
                pi_low = 3.1415925
                step(nc.vector.tensor_scalar(angle[:, :], angle[:, :], pi_low, -pi_low, ALU.min, ALU.max))
                step(nc.vector.scalar_tensor_tensor(turns[:, :], angle[:, :], -1.0, angle[:, :], ALU.mult, ALU.max))
                nc.vector.tensor_scalar(turns[:, :], turns[:, :], -1.0, float(np.pi / 2), ALU.mult,
                                        ALU.add).then_inc(angle_ready, 1)

            ve.wait_ge(init_ready, INIT)
            ve.wait_ge(const_landed, 32)
            rstd_of(1)

            def norm_group(g):
                for t in range(g * GT, (g + 1) * GT):
                    nc.vector.scalar_tensor_tensor(normed[:, t, PAD:], x[:, t, :], gain[:, G_POOL + t, :],
                                                   rstd[:, :], ALU.mult, ALU.mult).then_inc(normed_ready, 1)

            def window_sums(g):
                src, dst, other = normed[:, g * GT:(g + 1) * GT, :], win_v, win_v2
                for k in range(g + 1):
                    reach = 1 << k
                    step(nc.vector.tensor_tensor(dst[:, :, PAD:], src[:, :, PAD:],
                                                 src[:, :, PAD - reach:PAD + SEQ - reach], ALU.add))
                    src, dst, other = dst, other, dst
                return src

            def pool_diff(g, win, number):
                corr = const[:, C_CORR + g * PAD:C_CORR + (g + 1) * PAD].rearrange("p (o t) -> p o t", o=1)
                corr = corr.broadcast_to([P, GT, PAD])
                step(nc.vector.tensor_tensor(win[:, :, PAD:2 * PAD], win[:, :, PAD:2 * PAD], corr, ALU.mult))
                nc.vector.scalar_tensor_tensor(pooled[:, g * GT:(g + 1) * GT, :], win[:, :, PAD:], 1.0 / WINDOWS[g],
                                               normed[:, g * GT:(g + 1) * GT, PAD:], ALU.mult,
                                               ALU.subtract).then_inc(diff_ready, 1)
                ve.wait_ge(diff_ready, number)

            def pool_out(*tiles):
                for t in tiles:
                    if t % 2 == 0:
                        ve.wait_ge(chunks_used, t // 2 + 1)
                    nc.vector.scalar_tensor_tensor(x[:, t, :], ps[:, t % 4, 0:SEQ], gain[:, G_SCALE + t, :],
                                                   x[:, t, :], ALU.mult, ALU.add).then_inc(evacuated, 1)

            LAST = GROUPS - 1
            norm_group(0)
            ve.wait_ge(normed_ready, GT)
            pool_diff(0, window_sums(0), 1)
            norm_group(LAST)
            norm_group(1)
            ve.wait_ge(normed_ready, 3 * GT)
            win = window_sums(1)
            pool_out(0, 1)
            pool_diff(1, win, 2)
            pool_out(2, 3)
            norm_group(2)
            ve.wait_ge(normed_ready, 4 * GT)
            win = window_sums(2)
            pool_out(4, 5)
            pool_diff(2, win, 3)
            pool_out(6, 7)
            ve.wait_ge(windows_ready, 1)
            pool_diff(LAST, win_p2, 4)
            for t in range(DT // 2):
                gained(t, G_FFN0, xg, t + 1)
            for t in range(DT // 2, DT):
                pool_out(t)
                gained(t, G_FFN0, xg, t + 1)
                if t >= DT - SPLIT_SLOTS:
                    split(CHUNK["up0"] + t - (DT - SPLIT_SLOTS))

            def ffn_tile(p, f, splits, i=None):
                t = TILE[UPS[p]] + 2 * f
                bank = t % 4
                ve.wait_ge(cross_ready, plus(crossed[0] + f + 1, i, 2))
                nc.vector.tensor_tensor(sums[:, :, :], ps[:, bank:bank + 2, 0:SEQ], cross[:, :, :],
                                        ALU.add).then_inc(evacuated, 2)
                ve.wait_ge(evacuated, plus(t + 2, i, 4))
                r = rstd[:, :].rearrange("p (o t) -> p o t", o=1).broadcast_to([P, 2, SEQ])
                nc.vector.tensor_tensor(sums[:, :, :], sums[:, :, :], r, ALU.mult).then_inc(sums_ready, 1)
                splits[0]()
                ve.wait_ge(gate_ready, plus(p * FH + f + 1, i, 2))
                nc.vector.tensor_tensor(product[:, :], gate_act[:, :], sums[:, 1, :], ALU.mult).then_inc(product_ready, 1)
                splits[1]()
                ve.wait_ge(act_hi, plus(p * FH + f + 1, i, 2))
                nc.vector.tensor_tensor(act[:, plus(f, i, 2), SEQ:], product[:, :],
                                        act[:, plus(f, i, 2), 0:SEQ].bitcast(F32),
                                        ALU.subtract).then_inc(act_ready, 1)
                splits[2]()

            def into_x(t, d, used, i=None, per=0):
                b = t % 4
                xd = x[:, plus(d, i, per), :]
                ve.wait_ge(chunks_used, plus(used, i, BODY))
                step(nc.vector.tensor_tensor(xd, ps[:, b, 0:SEQ], xd, ALU.add))
                nc.vector.tensor_tensor(xd, ps[:, b, SEQ:], xd, ALU.add).then_inc(evacuated, 1)

            def ffn(layer, half, stats, xg_before):
                p = 2 * layer + half
                n0 = CHUNK[UPS[p]]
                for w in range(3):
                    split(n0 + w + SPLIT_SLOTS)
                if stats is not None:
                    rstd_of(stats)

                def tile(f, i=None):
                    n = n0 + 4 * f + 3 + SPLIT_SLOTS
                    ffn_tile(p, f, (lambda: split(n, i), lambda: split(n + 1, i),
                                    lambda: (split(n + 2, i), split(n + 3, i))), i)

                with ve.Fori(0, FH // 2 - 1) as i:
                    tile(0, i)
                    tile(1, i)
                tile(FH - 2)
                nothing = lambda: None
                ffn_tile(p, FH - 1, (nothing, nothing, lambda: split(n0 + 4 * FH - 1 + SPLIT_SLOTS)))
                crossed[0] += FH

                n1, t1 = CHUNK[DOWNS[p]], TILE[DOWNS[p]]

                def down(d, i=None):
                    split(n1 + 2 * d + SPLIT_SLOTS, i)
                    into_x(t1 + d, d, n1 + 2 * d + 2, i, 4)
                    if half == 1 and layer == 0:
                        gained(d, G_ATTN, xg, xg_before + d + 1, i, 4)
                    split(n1 + 2 * d + 1 + SPLIT_SLOTS, i)

                loop(DT // 4 - 1, 4, lambda i: [down(d, i) for d in range(4)])
                for d in range(DT - 4, DT):
                    down(d)

            ffn(0, 0, 2, None)
            ve.wait_ge(pos_landed, 16)
            rope_angles()
            ffn(0, 1, None, DT)

            xk_tiles = iter(range(DT))

            def xk_some(k):
                for _ in range(k):
                    t = next(xk_tiles)
                    gained(t, G_KV, xk, 2 * DT + t + 1)

            def lat_add(name, m):
                t = TILE[name] + m
                crossed[0] += 1
                ve.wait_ge(cross_ready, crossed[0])
                if m > 0:
                    ve.wait_ge(lat_sum, 1 if name == "qa" else 3)
                nc.vector.tensor_tensor(sums[:, :, :], ps[:, t % 4:t % 4 + 2, 0:SEQ], cross[:, :, :],
                                        ALU.add).then_inc(evacuated, 2)
                ve.wait_ge(evacuated, t + 2)

            def lat_scale(m):
                r = rstd[:, :].rearrange("p (o t) -> p o t", o=1).broadcast_to([P, 2, SEQ])
                nc.vector.tensor_tensor(lat_raw[:, m:m + 2, :], sums[:, :, :], r, ALU.mult).then_inc(lat_sum, 1)

            def lat_norm(which, number, col):
                ve.wait_ge(root_ready, 4 + number)
                nc.vector.reciprocal(lat_rstd[:, :], root[:, :]).then_inc(rstd_ready, 1)
                ve.wait_ge(rstd_ready, 4 + number)
                r = lat_rstd[:, :].rearrange("p (o t) -> p o t", o=1).broadcast_to([P, LT, SEQ])
                nc.vector.tensor_tensor(lat_raw[:, :, :], lat_raw[:, :, :], r, ALU.mult).then_inc(lat_scaled, 1)
                for t in range(LT):
                    ve.wait_ge(lat_hi, number * LT + t + 1)
                    nc.vector.scalar_tensor_tensor(
                        latent[:, which, t, SEQ:], lat_raw[:, t, :], gain[:, col + t, :],
                        latent[:, which, t, 0:SEQ].bitcast(F32), ALU.mult, ALU.subtract).then_inc(lat_ready, 1)

            n0 = CHUNK["qa"]
            for w in range(3):
                split(n0 + w + SPLIT_SLOTS)
                xk_some(2)
                if w == 1:
                    rstd_of(3)
            lat_add("qa", 0)
            lat_scale(0)
            for w in range(3, 7):
                split(n0 + w + SPLIT_SLOTS)
                xk_some(2)
            lat_add("qa", 2)
            lat_scale(2)
            split(n0 + 7 + SPLIT_SLOTS)
            xk_some(2)
            for w in range(8, 11):
                split(n0 + w + SPLIT_SLOTS)
            lat_add("kva", 0)
            split(n0 + 11 + SPLIT_SLOTS)
            lat_norm(Q, 0, G_LQ)
            ve.wait_ge(lat_ready, LT)
            lat_scale(0)
            split(n0 + 12 + SPLIT_SLOTS)
            split(n0 + 13 + SPLIT_SLOTS)
            split(n0 + 14 + SPLIT_SLOTS)
            lat_add("kva", 2)
            lat_scale(2)
            split(n0 + 15 + SPLIT_SLOTS)
            split(n0 + 16 + SPLIT_SLOTS)
            ve.wait_ge(table_ready, 2)
            step(nc.vector.tensor_scalar(sin[:, :], sin[:, :], const[:, C_SIGN:C_SIGN + 1], None, ALU.mult))

            crossed[0] += 1
            ve.wait_ge(cross_ready, crossed[0])
            nc.vector.tensor_tensor(gate_act[:, :], ps[:, TILE["kpe"] % 4, 0:SEQ], cross[:, 0, :],
                                    ALU.add).then_inc(evacuated, 2)
            ve.wait_ge(evacuated, TILE["kpe"] + 2)
            nc.vector.tensor_tensor(gate_act[:, :], gate_act[:, :], rstd[:, :], ALU.mult).then_inc(rope_sum, 1)
            split(n0 + 17 + SPLIT_SLOTS)
            nc.vector.memset(kpe_buf[64:P, 0, :].bitcast(F32), 0.0).then_inc(kpe_ready, 1)
            nc.vector.memset(kpe_buf[0:64, 1, :].bitcast(F32), 0.0).then_inc(kpe_ready, 1)
            lat_norm(KV, 1, G_LKV)
            for hh in range(2):
                rows = slice(64 * hh, 64 * hh + 64)
                ve.wait_ge(proj_hi, hh + 1)
                nc.vector.tensor_tensor(kpe_buf[rows, hh, SEQ:], gate_act[rows, :],
                                        kpe_buf[rows, hh, 0:SEQ].bitcast(F32), ALU.subtract).then_inc(kpe_ready, 1)

            def pair_add(g, part, crossed_at, i):
                t = TILE["heads"] + 8 * g + 2 * part
                if part == 2:
                    ve.wait_ge(q_ready, plus(g + 1, i, 2))
                elif g >= 1:
                    ve.wait_ge(k_ready, plus(g, i, 2))
                ve.wait_ge(cross_ready, plus(crossed_at, i, 6))
                nc.vector.tensor_tensor(sums[:, :, :], ps[:, t % 4:t % 4 + 2, 0:SEQ], cross[:, :, :],
                                        ALU.add).then_inc(evacuated, 2)

            def value_lo(g, i):
                t = TILE["heads"] + 8 * g + 6
                ve.wait_ge(proj_hi, plus(2 + 4 * g + 3, i, 8))
                nc.vector.tensor_tensor(v_buf[:, g % 2, :, 1, :], ps[:, t % 4:t % 4 + 2, 0:2 * V_DIM],
                                        v_buf[:, g % 2, :, 0, :].bitcast(F32), ALU.subtract).then_inc(evacuated, 2)

            def rope_add(g, crossed_at, i):
                t = TILE["heads"] + 8 * g
                if g == 0:
                    ve.wait_ge(kpe_ready, 4)
                else:
                    ve.wait_ge(qpe_ready, plus(g, i, 2))
                ve.wait_ge(cross_ready, plus(crossed_at, i, 6))
                nc.vector.tensor_tensor(gate_act[:, :], ps[:, t % 4, 0:SEQ], cross[:, 0, :],
                                        ALU.add).then_inc(evacuated, 2)

            def rope_lo(g, i):
                ve.wait_ge(proj_hi, plus(2 + 4 * g + 4, i, 8))
                nc.vector.tensor_tensor(qpe_buf[:, g % 2, SEQ:], gate_act[:, :], qpe_buf[:, g % 2, 0:SEQ].bitcast(F32),
                                        ALU.subtract).then_inc(qpe_ready, 1)

            def probT_lo_half(g, i):
                ve.wait_ge(probT_hi, plus(g + 1, i, 2))
                nc.vector.tensor_tensor(probT[:, :, 1, :], ps[:, SCORES:SCORES + 2, 0:3 * P],
                                        probT[:, :, 0, :].bitcast(F32), ALU.subtract).then_inc(probT_split, 1)

            def heads_lo_half(g, i):
                ve.wait_ge(head_hi, plus(2 * g + 2, i, 4))
                step(nc.vector.tensor_tensor(heads[:, plus(2 * g, i, 4), SEQ:], ps[:, HEADS_OUT, 0:SEQ],
                                             heads[:, plus(2 * g, i, 4), 0:SEQ].bitcast(F32), ALU.subtract))
                nc.vector.tensor_tensor(heads[:, plus(2 * g + 1, i, 4), SEQ:], ps[:, HEADS_OUT + 1, 0:SEQ],
                                        heads[:, plus(2 * g + 1, i, 4), 0:SEQ].bitcast(F32),
                                        ALU.subtract).then_inc(head_split, 1)

            def row_max(g, hh, i):
                ve.wait_ge(scores_ready, plus(2 * g + hh + 1, i, 4))
                nc.vector.tensor_copy(stat[:, hh, 7:8], eps[:, :])
                for qt in range(2):
                    nk = (qt + 1) * P
                    mask = const[:, C_MASK + 2 * P - nk:C_MASK + 2 * P]
                    ins = nc.vector.tensor_tensor_reduce(
                        prob[:, hh, qt * P:qt * P + nk], ps[:, SCORES + hh, qt * P:qt * P + nk], mask, ATTN_SCALE,
                        -3.0e38, ALU.add, ALU.max, stat[:, hh, qt:qt + 1])
                step(ins)
                nc.vector.tensor_scalar(stat[:, hh, 2:4], stat[:, hh, 0:2], -1.0, None, ALU.mult).then_inc(max_ready, 1)

            def normalise(g, hh, i):
                ve.wait_ge(exp_ready, plus(2 * (2 * g + hh + 1), i, 8))
                step(nc.vector.reciprocal(stat[:, hh, 6:8], stat[:, hh, 4:6]))
                step(nc.vector.tensor_scalar(prob[:, hh, 0:P], prob[:, hh, 0:P], stat[:, hh, 6:7], None, ALU.mult))
                nc.vector.tensor_scalar(prob[:, hh, P:], prob[:, hh, P:], stat[:, hh, 7:8], None,
                                        ALU.mult).then_inc(prob_ready, 1)

            crossed_heads = crossed[0]

            def slot(g, i=None):
                n, cr = CHUNK["heads"] + 4 * g, crossed_heads + 3 * g
                if g >= 2:
                    heads_lo_half(g - 2, i)
                rope_add(g, cr + 1, i)
                split(n + SPLIT_SLOTS, i)
                if g >= 1:
                    row_max(g - 1, 0, i)
                    row_max(g - 1, 1, i)
                    normalise(g - 1, 0, i)
                    normalise(g - 1, 1, i)
                pair_add(g, 1, cr + 2, i)
                split(n + 1 + SPLIT_SLOTS, i)
                if g >= 1:
                    probT_lo_half(g - 1, i)
                pair_add(g, 2, cr + 3, i)
                split(n + 2 + SPLIT_SLOTS, i)
                value_lo(g, i)
                split(n + 3 + SPLIT_SLOTS, i)
                rope_lo(g, i)

            slot(0)
            slot(1)
            loop(HG // 2 - 2, 2 * 7, lambda i: (slot(2, i), slot(3, i)))
            slot(HG - 2)
            slot(HG - 1)
            crossed[0] += 3 * HG

            n1, t1 = CHUNK["wo"], TILE["wo"]
            heads_lo_half(HG - 2, None)
            row_max(HG - 1, 0, None)
            row_max(HG - 1, 1, None)
            normalise(HG - 1, 0, None)
            normalise(HG - 1, 1, None)
            split(n1 + SPLIT_SLOTS)
            split(n1 + 1 + SPLIT_SLOTS)
            probT_lo_half(HG - 1, None)
            split(n1 + 2 + SPLIT_SLOTS)
            heads_lo_half(HG - 1, None)
            split(n1 + 3 + SPLIT_SLOTS)

            def wo(c, i=None):
                if c // 4 % 2:
                    d = 4 * (c // BODY) + c % 4
                    into_x(t1 + d, d, n1 + c + 1, i, 4)
                    gained(d, G_FFN1, xg, 3 * DT + d + 1, i, 4)
                split(n1 + c + SPLIT_SLOTS, i)

            for c in range(4, BODY):
                wo(c)
            loop(DT // 4 - 1, 4, lambda i: [wo(c, i) for c in range(BODY, 2 * BODY)])
            ffn(1, 0, 6, None)
            ffn(1, 1, None, None)

            rstd_of(7)
            for q in range(3):
                ve.wait_ge(y_gained, 4 * q + 4)
                r = rstd[:, :].rearrange("p (o t) -> p o t", o=1).broadcast_to([P, 4, SEQ])
                nc.vector.tensor_tensor(y[:, 4 * q:4 * q + 4, :], y[:, 4 * q:4 * q + 4, :], r,
                                        ALU.mult).then_inc(y_done_v, 1)

        @block.gpsimd
        def _(gp):
            steps = [0, None, 0]

            def step(ins):
                steps[0] += 1
                ins.then_inc(p_step, 1)
                gp.wait_ge(p_step, plus(steps[0], steps[1], steps[2]))

            for ap, value in ((ones[:, :], 1.0), (eps[:, :], EPS), (normed[:, :, 0:PAD], 0.0),
                              (win_v[:, :, 0:PAD], 0.0), (win_v2[:, :, 0:PAD], 0.0), (win_p[:, :, 0:PAD], 0.0),
                              (win_p2[:, :, 0:PAD], 0.0), (stat[:, :, :], 0.0)):
                nc.gpsimd.memset(ap, value).then_inc(init_ready, 1)
            gp.wait_ge(init_ready, INIT)

            def window_sum(dst, src, reach):
                return nc.gpsimd.tensor_tensor(dst[:, :, PAD:], src[:, :, PAD:],
                                               src[:, :, PAD - reach:PAD + SEQ - reach], ALU.add)

            gp.wait_ge(normed_ready, 2 * GT)
            step(window_sum(win_p, normed[:, 3 * GT:4 * GT, :], 1))
            step(window_sum(win_p2, win_p, 2))
            step(window_sum(win_p, win_p2, 4))
            window_sum(win_p2, win_p, 8).then_inc(windows_ready, 1)

            def add_square(k, src, d, i=None):
                step(nc.gpsimd.tensor_tensor(square[:, :], src, src, ALU.mult))
                nc.gpsimd.tensor_tensor(square_sum[:, :], square_sum[:, :], square[:, :],
                                        ALU.add).then_inc(squares_added, 1)
                gp.wait_ge(squares_added, plus(squares_before(k) + d + 1, i, 4))

            def start_sum(k):
                gp.wait_ge(stats_summed, k)
                step(nc.gpsimd.memset(square_sum[:, :], 0.0))

            def stream_squares(k, phase):
                start_sum(k)
                start = steps[0]
                with gp.Fori(0, DT // 4) as i:
                    steps[1:] = [i, 4]
                    for d in range(4):
                        gp.wait_ge(evacuated, plus(TILE[phase] + d + 1, i, 4))
                        add_square(k, x[:, plus(d, i, 4), :], d, i)
                steps[:] = [start + DT, None, 0]

            def latent_squares(k, number):
                start_sum(k)
                for d in range(LT):
                    gp.wait_ge(lat_sum, 2 * number + d // 2 + 1)
                    add_square(k, lat_raw[:, d, :], d)

            stream_squares(1, "pool")
            stream_squares(2, "down1")
            latent_squares(3, 0)
            latent_squares(4, 1)

            def rotate(k, i=None):
                gp.wait_ge(rope_swapped, plus(4 * k, i, 8))
                nc.gpsimd.tensor_tensor(gate_act[:, :], gate_act[:, :], cos[:, :], ALU.mult)
                step(nc.gpsimd.tensor_tensor(product[:, :], product[:, :], sin[:, :], ALU.mult))
                nc.gpsimd.tensor_tensor(gate_act[:, :], gate_act[:, :], product[:, :], ALU.add).then_inc(rope_done, 1)

            def pair_lo(g, part, dst, ready, i):
                gp.wait_ge(proj_hi, plus(2 + 4 * g + part, i, 8))
                nc.gpsimd.tensor_tensor(dst[:, g % 2, :, SEQ:], sums[:, :, :], dst[:, g % 2, :, 0:SEQ].bitcast(F32),
                                        ALU.subtract).then_inc(ready, 1)

            rotate(1)
            start = steps[0]
            with gp.Fori(0, HG // 2) as i:
                steps[1:] = [i, 2]
                for g in range(2):
                    rotate(g + 2, i)
                    pair_lo(g, 1, q_buf, q_ready, i)
                    pair_lo(g, 2, k_buf, k_ready, i)
            steps[:] = [start + HG, None, 0]

            stream_squares(5, "wo")
            stream_squares(6, "down3")

            gp.wait_ge(rstd_ready, 7)
            gp.wait_ge(y_gained, DT)
            r = rstd[:, :].rearrange("p (o t) -> p o t", o=1).broadcast_to([P, 4, SEQ])
            nc.gpsimd.tensor_tensor(y[:, 12:16, :], y[:, 12:16, :], r, ALU.mult).then_inc(y_done_p, 1)


def shape_constants():
    c = np.zeros((P, C_COLS), np.float32)
    c[:, C_IDENT:C_IDENT + P] = np.eye(P)
    row, col = np.arange(P)[:, None], np.arange(P)[None, :]
    c[:, C_MASK + P:C_MASK + 2 * P] = np.where(col <= row, 0.0, -1.0e30)
    for g, w in enumerate(WINDOWS):
        c[:, C_CORR + g * PAD:C_CORR + (g + 1) * PAD] = w / np.minimum(np.arange(PAD) + 1.0, w)
    half = ROPE // 2
    freq = np.float32(10000.0) ** (-np.arange(half, dtype=np.float32) / np.float32(half))
    c[:, C_FREQ] = np.tile(freq, P // half)
    c[:, C_SIGN] = np.tile(np.repeat([-1.0, 1.0], half), P // ROPE)
    return c


def by_tiles(w, k_per_chunk, tiles_per_chunk):
    k, m = w.shape[0] // P, w.shape[1] // P
    w = w.reshape(k // k_per_chunk, k_per_chunk, P, m // tiles_per_chunk, tiles_per_chunk, P)
    return w.transpose(3, 0, 2, 4, 1, 5).reshape(-1, P, tiles_per_chunk * k_per_chunk * P)


def kernel(**inputs):
    import concourse.bacc as bacc
    from concourse.bass_utils import run_bass_kernel_spmd

    a = {k: np.asarray(v) for k, v in inputs.items()}
    feature_tiles = lambda v: v.reshape(-1, P).T
    qb = a["w_q_b"][0].reshape(LATENT, HEADS, NOPE + ROPE)
    kvb = a["w_kv_b"].reshape(LATENT, HEADS, NOPE + V_DIM)
    values = kvb[:, :, NOPE:].reshape(LT, P, HG, 2 * V_DIM)
    rope_keys = a["w_kv_a"][:, LATENT:].reshape(2, TILES, P, ROPE)
    down = a["w_down"].reshape(4 * FH * P, D_MODEL)
    arrays = {
        "xT": a["x"][0].T.reshape(DT, P, SEQ).transpose(1, 0, 2),
        "positions": a["positions"].reshape(SEQ),
        "consts": shape_constants(),
        "gains": np.concatenate([feature_tiles(v.reshape(-1)) for v in (
            a["pool_norm"], a["pool_scale"], a["kv_in_norm"], a["attn_norm"], a["ffn_norm"][0], a["ffn_norm"][1],
            a["final_norm"], a["kv_latent_norm"], a["q_latent_norm"])], axis=1)[:, :, None],
        "pool_w": np.concatenate([by_tiles(w, GT, 2) for w in a["pool_w"][0]]),
        "w_kv_a": by_tiles(a["w_kv_a"][:, :LATENT], TILES, 1),
        "w_k_pe": rope_keys.transpose(0, 2, 1, 3).reshape(2, P, TILES * ROPE),
        "w_q_a": by_tiles(a["w_q_a"][0], TILES, 1),
        "w_kv_k": by_tiles(kvb[:, :, :NOPE].reshape(LATENT, -1), LT, 2),
        "w_kv_v": values.transpose(2, 1, 0, 3).reshape(HG, P, LT * 2 * V_DIM),
        "w_q_nope": by_tiles(qb[:, :, :NOPE].reshape(LATENT, -1), LT, 2),
        "w_q_pe": by_tiles(qb[:, :, NOPE:].reshape(LATENT, -1), LT, 1),
        "w_o": by_tiles(a["w_o"][0], TILES, 1),
        "w_gate": np.concatenate([by_tiles(w, TILES, 1) for w in a["w_gate"]]),
        "w_up": np.concatenate([by_tiles(w, TILES, 1) for w in a["w_up"]]),
        "w_down": np.concatenate([by_tiles(w, DTILES, 1) for w in np.split(down, 4)]),
    }
    arrays = {k: np.ascontiguousarray(v) for k, v in arrays.items()}

    nc = bacc.Bacc("TRN2", target_bir_lowering=False, num_devices=1)
    args = [nc.dram_tensor(k, v.shape, mybir.dt.from_np(v.dtype), kind="ExternalInput").ap()
            for k, v in arrays.items()]
    out = nc.dram_tensor("out", (P, DT, SEQ), F32, kind="ExternalOutput").ap()
    trunk(nc, *args, out)
    got = run_bass_kernel_spmd(nc, [arrays], core_ids=[0]).results[0]["out"]
    return got.transpose(1, 0, 2).reshape(D_MODEL, SEQ).T.reshape(1, SEQ, D_MODEL)
```

```python
from contextlib import ExitStack

import numpy as np
import concourse.bass as bass
from concourse import mybir

F32 = mybir.dt.float32
F32R = mybir.dt.float32r
I32 = mybir.dt.int32
ALU = mybir.AluOpType
ACT = mybir.ActivationFunctionType

P = 128
SEQ = 256
D_MODEL = 2048
D_FF = 5632
WINDOWS = (2, 4, 8, 16)
HEADS = 16
NOPE, ROPE, V_DIM = 128, 64, 128
LATENT = 512
ATTN_SCALE = 1.0 / float(np.sqrt(NOPE + ROPE))
EPS = 1e-6

DT = D_MODEL // P
LT = LATENT // P
FH = D_FF // P // 2
GROUPS = len(WINDOWS)
GT = DT // GROUPS
PAD = max(WINDOWS)
HG = HEADS // 2
POOL_ORDER = (0, 2, 1, 3)
FIRST_SPLITS = (4, 6, 8, 10)
WARM_UP_POOL = 16
WARM_UP = 8

WEIGHT_SLOTS = 8
SPLIT_SLOTS = 4
TILES = 8
DTILES = FH // 2
Y_VECTOR, Y_GPSIMD = ((0, 2), (2, 4), (4, 8), (8, 11)), ((11, 13), (13, 16))
BODY = WEIGHT_SLOTS

C_IDENT = 0
C_MASK = C_IDENT + P
C_CORR = C_MASK + 2 * P
C_FREQ = C_CORR + GROUPS * PAD
C_SIGN = C_FREQ + 1
C_COLS = C_SIGN + 1

G_POOL, G_SCALE, G_KV, G_ATTN, G_FFN0, G_FFN1, G_FINAL, G_LKV, G_LQ, G_COLS = (
    0, DT, 2 * DT, 3 * DT, 4 * DT, 5 * DT, 6 * DT, 7 * DT, 7 * DT + LT, 7 * DT + 2 * LT)


def chunk_plan():
    chunks, tiles, c, t = {}, {}, 0, 0
    for name, nc_, nt in (
        ("pool", DT * GT // TILES, DT),
        ("up0", 4 * FH, 2 * FH), ("down0", 2 * DT, DT), ("up1", 4 * FH, 2 * FH), ("down1", 2 * DT, DT),
        ("qa", 2 * LT, LT), ("kva", 2 * LT, LT), ("kpe", 2, 2),
        ("heads", 4 * HG, 8 * HG), ("wo", 2 * DT, DT),
        ("up2", 4 * FH, 2 * FH), ("down2", 2 * DT, DT), ("up3", 4 * FH, 2 * FH), ("down3", 2 * DT, DT),
    ):
        chunks[name], tiles[name] = c, t
        c, t = c + nc_, t + nt
    chunks["end"] = c
    return chunks, tiles


CHUNK, TILE = chunk_plan()

SQUARED = (DT, DT, LT, LT, DT, DT - 1)


def squares_before(k):
    return sum(SQUARED[:k - 1])


def chunk_elems(n):
    for ph in ("down0", "down1", "down2", "down3"):
        if CHUNK[ph] <= n < CHUNK[ph] + 2 * DT:
            return DTILES * P
    if CHUNK["heads"] <= n < CHUNK["wo"] and (n - CHUNK["heads"]) % 4 == 0:
        return TILES * P // 2
    return TILES * P


def made(n):
    return n + 1 - CHUNK["up0"]


def plus(n, i, per):
    return n if i is None else i * per + n


def trunk(nc, xT, positions, consts, gains, pool_w, w_kv_a, w_k_pe, w_q_a, w_kv_k, w_kv_v, w_q_nope, w_q_pe,
          w_o, w_gate, w_up, w_down, out):
    with ExitStack() as ctx:
        def sem(name):
            return ctx.enter_context(nc.semaphore(name))

        def sb(name, shape, dt=F32):
            return ctx.enter_context(nc.sbuf_tensor(name, shape, dt))

        x = sb("x", [P, DT, SEQ])
        raw = sb("raw", [P, WEIGHT_SLOTS, DTILES * P])
        w_hi = sb("w_hi", [P, SPLIT_SLOTS, DTILES * P], F32R)
        w_lo = sb("w_lo", [P, SPLIT_SLOTS, DTILES * P], F32R)
        const = sb("const", [P, C_COLS])
        gain = sb("gain", [P, G_COLS, 1])
        ones = sb("ones", [P, P])
        eps = sb("eps", [P, 1])
        cos = sb("cos", [P, SEQ])
        sin = sb("sin", [P, SEQ])
        root = sb("root", [P, SEQ])
        rstd = sb("rstd", [P, SEQ])
        square = sb("square", [P, SEQ])
        square_sum = sb("square_sum", [P, SEQ])
        cross = sb("cross", [P, 2, SEQ])
        sums = sb("sums", [P, 2, SEQ])
        gate_act = sb("gate_act", [P, SEQ])
        product = sb("product", [P, SEQ])

        KB = 1024
        region_at = nc.sbuf_base
        sb("region", [P, 80 * KB // 4])
        scratch_at = nc.sbuf_base
        sb("scratch", [P, (9 * KB + 64) // 4])

        def at(name, shape, dt, offset):
            return nc.alloc_sbuf_tensor_at(name, shape, dt, offset=offset)

        xg = at("xg", [P, DT, 2 * SEQ], F32R, region_at)
        act = at("act", [P, FH, 2 * SEQ], F32R, region_at + 32 * KB)
        PR = PAD + SEQ
        grp = GT * PR * 4
        pool_at = region_at + 32 * KB
        x_square = at("x_square", [P, DT, SEQ], F32, pool_at)
        pooled = at("pooled", [P, DT, SEQ], F32, pool_at)
        normed = at("normed", [P, DT, PR], F32, pool_at + 16 * KB)
        win_v = at("win_v", [P, GT, PR], F32, pool_at + 16 * KB + 4 * grp)
        win_v2 = at("win_v2", [P, GT, PR], F32, pool_at + 16 * KB + 5 * grp)
        win_p = at("win_p", [P, GT, PR], F32, pool_at + 16 * KB + 6 * grp)
        win_p2 = at("win_p2", [P, GT, PR], F32, scratch_at)
        xk = at("xk", [P, DT, 2 * SEQ], F32R, region_at + 32 * KB)
        latent = at("latent", [P, 2, LT, 2 * SEQ], F32R, region_at + 64 * KB)
        lat_raw = at("lat_raw", [P, LT, SEQ], F32, scratch_at)
        lat_rstd = at("lat_rstd", [P, SEQ], F32, scratch_at + 6 * KB)
        key_raw = at("key_raw", [P, SEQ], F32, scratch_at + 7 * KB)
        k_buf = at("k_buf", [P, 2, 2, 2 * SEQ], F32R, region_at)
        q_buf = at("q_buf", [P, 2, 2, 2 * SEQ], F32R, region_at + 8 * KB)
        v_buf = at("v_buf", [P, 2, 2, 2, 2 * V_DIM], F32R, region_at + 16 * KB)
        qpe_buf = at("qpe_buf", [P, 2, 2 * SEQ], F32R, region_at + 24 * KB)
        kpe_buf = at("kpe_buf", [P, 2, 2 * SEQ], F32R, region_at + 28 * KB)
        heads = at("heads", [P, HEADS, 2 * SEQ], F32R, region_at + 32 * KB)
        prob = at("prob", [P, 2, 3 * P], F32, scratch_at)
        probT = at("probT", [P, 2, 2, 3 * P], F32R, scratch_at + 3 * KB)
        stat = at("stat", [P, 2, 8], F32, scratch_at + 9 * KB)
        y = at("y", [P, DT, SEQ], F32, region_at)
        pos_i = at("pos_i", [P, SEQ], I32, scratch_at + 4 * KB + KB // 2)
        angle = at("angle", [P, SEQ], F32, scratch_at)
        turns = at("turns", [P, SEQ], F32, scratch_at + KB)

        def square_of(t):
            return (cross, sums)[t % 4 // 2][:, t % 2, :]

        ps = ctx.enter_context(nc.psum_tensor("ps", [P, 8, 512], F32))
        SCORES, HEADS_OUT, STATS = 4, 6, 7

        x_landed = [sem(f"x_landed{q}") for q in range(4)]
        const_landed = sem("const_landed")
        gain_landed = sem("gain_landed")
        landed = [sem(f"landed{s}") for s in range(WEIGHT_SLOTS)]
        hi_ready = sem("hi_ready")
        lo_ready = sem("lo_ready")
        chunks_used = sem("chunks_used")
        evacuated = sem("evacuated")
        xg_hi = sem("xg_hi")
        xg_ready = sem("xg_ready")
        cross_ready = sem("cross_ready")
        sums_ready = sem("sums_ready")
        gate_ready = sem("gate_ready")
        product_ready = sem("product_ready")
        act_hi = sem("act_hi")
        act_ready = sem("act_ready")
        squares_added = sem("squares_added")
        stats_summed = sem("stats_summed")
        root_ready = sem("root_ready")
        rstd_ready = sem("rstd_ready")
        squares_ready = sem("squares_ready")
        quarter_ready = sem("quarter_ready")
        pool_gained = sem("pool_gained")
        square_made = sem("square_made")
        init_ready = sem("init_ready")
        windows_ready = sem("windows_ready")
        normed_ready = sem("normed_ready")
        diff_ready = sem("diff_ready")
        angle_ready = sem("angle_ready")
        table_ready = sem("table_ready")
        pos_landed = sem("pos_landed")
        lat_sum = sem("lat_sum")
        lat_scaled = sem("lat_scaled")
        lat_hi = sem("lat_hi")
        lat_ready = sem("lat_ready")
        key_rope_hi = sem("key_rope_hi")
        query_rope_hi = sem("query_rope_hi")
        pair_hi_ready = sem("pair_hi_ready")
        value_hi_ready = sem("value_hi_ready")
        rope_sum = sem("rope_sum")
        rope_swapped = sem("rope_swapped")
        rope_done = sem("rope_done")
        k_ready = sem("k_ready")
        q_ready = sem("q_ready")
        qpe_ready = sem("qpe_ready")
        kpe_ready = sem("kpe_ready")
        scores_ready = sem("scores_ready")
        max_ready = sem("max_ready")
        exp_ready = sem("exp_ready")
        prob_ready = sem("prob_ready")
        probT_ready = sem("probT_ready")
        probT_hi = sem("probT_hi")
        probT_split = sem("probT_split")
        head_ready = sem("head_ready")
        head_hi = sem("head_hi")
        head_split = sem("head_split")
        last_square = sem("last_square")
        y_gained = sem("y_gained")
        y_done_v = sem("y_done_v")
        y_done_p = sem("y_done_p")
        stored = sem("stored")
        v_step = sem("v_step")
        p_step = sem("p_step")

        block = ctx.enter_context(nc.Block())

        KV, Q = 0, 1
        INIT = 8
        UPS = ("up0", "up1", "up2", "up3")
        DOWNS = ("down0", "down1", "down2", "down3")

        @block.sync
        def _(sp):
            def load(n, src, i=None):
                before = n - WEIGHT_SLOTS
                if before >= CHUNK["up0"]:
                    sp.wait_ge(lo_ready, plus(made(before), i, BODY))
                elif before >= 0:
                    sp.wait_ge(chunks_used, before + 1)
                sp.dma_start(raw[:, n % WEIGHT_SLOTS, 0:chunk_elems(n)], src).then_inc(landed[n % WEIGHT_SLOTS], 16)

            for q in range(4):
                sp.dma_start(x[:, 4 * q:4 * q + 4, :], xT[:, 4 * q:4 * q + 4, :]).then_inc(x_landed[q], 16)
                if q == 1:
                    sp.dma_start(gain[:, :, :], gains).then_inc(gain_landed, 16)
            sp.dma_start(const[:, :], consts).then_inc(const_landed, 16)
            sp.dma_start(pos_i[:, :], positions.partition_broadcast(P)).then_inc(pos_landed, 16)
            for c in range(CHUNK["up0"]):
                load(CHUNK["pool"] + c, pool_w[c])

            def ffn(layer, half):
                up, down = UPS[2 * layer + half], DOWNS[2 * layer + half]

                def up_body(b, i=None):
                    for c in range(BODY * b, BODY * (b + 1)):
                        of_up, part = c % 4 // 2, c % 2
                        if half == 0 and c < 4:
                            of_up, part = part, of_up
                        w = w_up if of_up else w_gate
                        row = ((layer * 2 + half) * FH + c // 4) * 2 + part
                        load(CHUNK[up] + c, w[plus(row, i, 4)], i)

                peel = 1 - half
                for b in range(peel):
                    up_body(b)
                with sp.Fori(0, FH // 2 - peel) as i:
                    up_body(peel, i)
                with sp.Fori(0, DT // 4) as i:
                    for c in range(BODY):
                        load(CHUNK[down] + c, w_down[plus((layer * 2 + half) * DT * 2 + c, i, BODY)], i)

            ffn(0, 0)
            ffn(0, 1)
            for c in range(2 * LT):
                load(CHUNK["qa"] + c, w_q_a[c])
            for c in range(2 * LT):
                load(CHUNK["kva"] + c, w_kv_a[c])
            for c in range(2):
                n = CHUNK["kpe"] + c
                sp.wait_ge(lo_ready, made(n - WEIGHT_SLOTS))
                sp.dma_start(raw[:, n % WEIGHT_SLOTS, 0:TILES * ROPE], w_k_pe[c]).then_inc(
                    landed[n % WEIGHT_SLOTS], 16)
            with sp.Fori(0, HG // 2) as i:
                for g in range(2):
                    for c, w in enumerate((w_q_pe, w_q_nope, w_kv_k, w_kv_v)):
                        load(CHUNK["heads"] + 4 * g + c, w[plus(g, i, 2)], i)
            with sp.Fori(0, DT // 4) as i:
                for c in range(BODY):
                    load(CHUNK["wo"] + c, w_o[plus(2 * (c % 4) + c // 4, i, BODY)], i)
            ffn(1, 0)
            ffn(1, 1)

            for done, count, (a, b) in ((y_done_v, 1, Y_VECTOR[0]), (y_done_v, 2, Y_VECTOR[1]),
                                        (y_done_p, 1, Y_GPSIMD[0]), (y_done_v, 3, Y_VECTOR[2]),
                                        (y_done_p, 2, Y_GPSIMD[1]), (y_done_v, 4, Y_VECTOR[3])):
                sp.wait_ge(done, count)
                sp.dma_start(out[:, a:b, :], y[:, a:b, :]).then_inc(stored, 16)
            sp.wait_ge(stored, 16 * (len(Y_VECTOR) + len(Y_GPSIMD)))

        @block.tensor
        def _(pe):
            def product3(n, j, bank, moving, start, stop):
                s = n % SPLIT_SLOTS
                pe.matmul(ps[:, bank, :], w_hi[:, s, j * P:(j + 1) * P], moving, start=start, stop=False)
                return pe.matmul(ps[:, bank, 0:SEQ], w_lo[:, s, j * P:(j + 1) * P], moving[:, 0:SEQ],
                                 start=False, stop=stop)

            def bank_free(t, i=None, per=0):
                if t >= 4:
                    pe.wait_ge(evacuated, plus(t - 3, i, per))

            def long_tile(n, t, operand, kts, i=None, per=0, each=None):
                for c in range(2):
                    pe.wait_ge(lo_ready, plus(made(n + c), i, BODY))
                    if c == 0:
                        bank_free(t, i, per)
                    for j in range(kts):
                        kt = c * kts + j
                        if each is not None:
                            each(kt)
                        mm = product3(n + c, j, t % 4, operand[:, kt, :], kt == 0, kt == 2 * kts - 1)
                    mm.then_inc(chunks_used, 1)

            def first_tiles(n, t, xg_before):
                for c in range(4):
                    half, m = c // 2, c % 2
                    pe.wait_ge(lo_ready, made(n + c))
                    if half == 0:
                        bank_free(t + m)
                    for j in range(TILES):
                        kt = half * TILES + j
                        if m == 0:
                            pe.wait_ge(xg_ready, xg_before + kt + 1)
                        mm = product3(n + c, j, (t + m) % 4, xg[:, kt, :], kt == 0, kt == DT - 1)
                    mm.then_inc(chunks_used, 1)

            def sum_over_partitions(k):
                pe.wait_ge(squares_added, squares_before(k + 1))
                pe.wait_ge(root_ready, k)
                pe.matmul(ps[:, STATS, 0:SEQ], ones[:, :], square_sum[:, :], start=True,
                          stop=True).then_inc(stats_summed, 1)

            pe.wait_ge(init_ready, INIT)
            for _ in range(WARM_UP):
                pe.matmul(ps[:, SCORES, 0:P], ones[:, :], ones[:, :], start=True, stop=True)
            for q in range(4):
                pe.wait_ge(quarter_ready, q + 1)
                mm = pe.matmul(ps[:, STATS, 0:SEQ], ones[:, :], x_square[:, 4 * q, :], start=(q == 0), stop=(q == 3))
            mm.then_inc(stats_summed, 1)
            for _ in range(WARM_UP_POOL):
                pe.matmul(ps[:, SCORES, 0:P], ones[:, :], ones[:, :], start=True, stop=True)

            def pool_tile(t, kts):
                c = t // 2
                for kt in kts:
                    j = t % 2 * GT + kt
                    mm = pe.matmul(ps[:, t % 4, 0:SEQ], raw[:, c, j * P:(j + 1) * P], pooled[:, c // 2 * GT + kt, :],
                                   start=(kt == 0), stop=(kt == GT - 1))
                if t % 2 == 1 and kts[-1] == GT - 1:
                    mm.then_inc(chunks_used, 1)

            for part in range(2):
                pe.wait_ge(diff_ready, part + 1)
                for t in range(GT):
                    if part == 0 and t % 2 == 0:
                        pe.wait_ge(landed[t // 2], 16)
                    pool_tile(t, range(part * GT // 2, (part + 1) * GT // 2))
            for t in range(GT, DT):
                if t % GT == 0:
                    pe.wait_ge(diff_ready, t // GT + 2)
                if t % 2 == 0:
                    pe.wait_ge(landed[t // 2], 16)
                bank_free(t)
                pool_tile(t, range(GT))

            def ffn(layer, half, xg_before, stats):
                p = 2 * layer + half
                n0, t0 = CHUNK[UPS[p]], TILE[UPS[p]]
                peel = 0
                if half == 0:
                    peel = 1
                    first_tiles(n0, t0, xg_before)
                    sum_over_partitions(stats)
                    long_tile(n0 + 4, t0 + 2, xg, TILES)
                    long_tile(n0 + 6, t0 + 3, xg, TILES)
                with pe.Fori(0, FH // 2 - peel) as i:
                    for f in range(4):
                        long_tile(n0 + BODY * peel + 2 * f, t0 + 4 * peel + f, xg, TILES, i, 4)
                n0, t0 = CHUNK[DOWNS[p]], TILE[DOWNS[p]]
                long_tile(n0, t0, act, DTILES, each=lambda kt: pe.wait_ge(act_ready, p * FH + kt + 1))
                for d in range(1, 4):
                    long_tile(n0 + 2 * d, t0 + d, act, DTILES)
                with pe.Fori(0, DT // 4 - 1) as i:
                    for d in range(4):
                        long_tile(n0 + BODY + 2 * d, t0 + 4 + d, act, DTILES, i, 4)

            ffn(0, 0, 0, 1)
            ffn(0, 1, None, None)

            for m in range(LT):
                long_tile(CHUNK["qa"] + 2 * m, TILE["qa"] + m, xg, TILES,
                          each=(lambda kt: pe.wait_ge(xg_ready, DT + kt + 1)) if m == 0 else None)
                if m == 0:
                    sum_over_partitions(2)
            for m in range(LT):
                long_tile(CHUNK["kva"] + 2 * m, TILE["kva"] + m, xk, TILES,
                          each=(lambda kt: pe.wait_ge(xg_ready, 2 * DT + kt + 1)) if m == 0 else None)
                if m == 1:
                    sum_over_partitions(3)
            long_tile(CHUNK["kpe"], TILE["kpe"], xk, TILES)

            def key_part(g, i=None):
                n, t = CHUNK["heads"] + 4 * g + 2, TILE["heads"] + 8 * g + 4
                pe.wait_ge(lo_ready, plus(made(n), i, BODY))
                for m in range(2):
                    bank_free(t + m, i, 16)
                    for kt in range(LT):
                        mm = product3(n, m * LT + kt, (t + m) % 4, latent[:, KV, kt, :], kt == 0, kt == LT - 1)
                mm.then_inc(chunks_used, 1)

            def value_part(g, i=None):
                n, t = CHUNK["heads"] + 4 * g + 3, TILE["heads"] + 8 * g + 6
                s = n % SPLIT_SLOTS
                pe.wait_ge(lo_ready, plus(made(n), i, BODY))
                for m in range(2):
                    bank_free(t + m, i, 16)
                    dst = ps[:, (t + m) % 4, 0:2 * V_DIM]
                    for kt in range(LT):
                        wh = w_hi[:, s, kt * 2 * V_DIM:(kt + 1) * 2 * V_DIM]
                        wl = w_lo[:, s, kt * 2 * V_DIM:(kt + 1) * 2 * V_DIM]
                        c_hi = latent[:, KV, kt, m * P:(m + 1) * P]
                        c_lo = latent[:, KV, kt, SEQ + m * P:SEQ + (m + 1) * P]
                        pe.matmul(dst, c_hi, wh, start=(kt == 0), stop=False)
                        pe.matmul(dst, c_hi, wl, start=False, stop=False)
                        mm = pe.matmul(dst, c_lo, wh, start=False, stop=(kt == LT - 1))
                mm.then_inc(chunks_used, 1)

            def query_rope_part(g, i=None):
                n, t = CHUNK["heads"] + 4 * g, TILE["heads"] + 8 * g
                pe.wait_ge(lo_ready, plus(made(n), i, BODY))
                bank_free(t, i, 16)
                for kt in range(LT):
                    mm = product3(n, kt, t % 4, latent[:, Q, kt, :], kt == 0, kt == LT - 1)
                mm.then_inc(chunks_used, 1)

            def query_part(g, i=None):
                n, t = CHUNK["heads"] + 4 * g + 1, TILE["heads"] + 8 * g + 2
                pe.wait_ge(lo_ready, plus(made(n), i, BODY))
                for m in range(2):
                    bank_free(t + m, i, 16)
                    for kt in range(LT):
                        mm = product3(n, m * LT + kt, (t + m) % 4, latent[:, Q, kt, :], kt == 0, kt == LT - 1)
                mm.then_inc(chunks_used, 1)

            def scores(g, hh, i=None):
                b = g % 2
                if hh == 0:
                    pe.wait_ge(k_ready, plus(g + 1, i, 2))
                    pe.wait_ge(qpe_ready, plus(g + 1, i, 2))
                    pe.wait_ge(q_ready, plus(g + 1, i, 2))
                    if g == 0:
                        pe.wait_ge(kpe_ready, 2)
                    if g >= 1:
                        pe.wait_ge(probT_split, plus(g, i, 2))
                for qt in range(2):
                    nk = (qt + 1) * P
                    dst = ps[:, SCORES + hh, qt * P:qt * P + nk]
                    pairs = ((q_buf[:, b, hh, :], k_buf[:, b, hh, :]), (qpe_buf[:, b, :], kpe_buf[:, hh, :]))
                    for part, (q, k) in enumerate(pairs):
                        q_hi, q_lo = q[:, qt * P:(qt + 1) * P], q[:, SEQ + qt * P:SEQ + (qt + 1) * P]
                        k_hi, k_lo = k[:, 0:nk], k[:, SEQ:SEQ + nk]
                        pe.matmul(dst, q_hi, k_hi, start=(part == 0), stop=False)
                        pe.matmul(dst, q_hi, k_lo, start=False, stop=False)
                        mm = pe.matmul(dst, q_lo, k_hi, start=False, stop=(part == 1))
                mm.then_inc(scores_ready, 1)

            def turn_probs(g, hh, i=None):
                pe.wait_ge(prob_ready, plus(2 * (2 * g + hh + 1), i, 8))
                for c in range(3):
                    mm = pe.transpose(ps[:, SCORES + hh, c * P:(c + 1) * P], prob[:, hh, c * P:(c + 1) * P],
                                      const[:, C_IDENT:C_IDENT + P])
                mm.then_inc(probT_ready, 1)

            def head_output(g, hh, i=None):
                b = g % 2
                if hh == 0:
                    pe.wait_ge(evacuated, plus(TILE["heads"] + 8 * g + 8, i, 16))
                    pe.wait_ge(probT_split, plus(g + 1, i, 2))
                    if g >= 1:
                        pe.wait_ge(head_split, plus(g, i, 2))
                for kt in range(2):
                    v_hi = v_buf[:, b, kt, 0, hh * V_DIM:(hh + 1) * V_DIM]
                    v_lo = v_buf[:, b, kt, 1, hh * V_DIM:(hh + 1) * V_DIM]
                    cols = slice(0, 2 * P) if kt == 0 else slice(2 * P, 3 * P)
                    dst = ps[:, HEADS_OUT + hh, kt * P:SEQ]
                    pe.matmul(dst, v_hi, probT[:, hh, 0, cols], start=(kt == 0), stop=False)
                    pe.matmul(dst, v_hi, probT[:, hh, 1, cols], start=False, stop=False)
                    mm = pe.matmul(dst, v_lo, probT[:, hh, 0, cols], start=False, stop=(kt == 1))
                mm.then_inc(head_ready, 1)

            def wo_part(c, i=None, each=None):
                n, t = CHUNK["wo"] + c, TILE["wo"] + 4 * (c // BODY) + c % 4
                half = c // 4 % 2
                pe.wait_ge(lo_ready, plus(made(n), i, BODY))
                if half == 0:
                    bank_free(t, i, 4)
                for j in range(TILES):
                    kt = half * TILES + j
                    if each is not None:
                        each(kt)
                    mm = product3(n, j, t % 4, heads[:, kt, :], kt == 0, kt == DT - 1)
                mm.then_inc(chunks_used, 1)

            def slot(g, i=None):
                own = g < HG
                if own:
                    query_rope_part(g, i)
                if g >= 1:
                    scores(g - 1, 0, i)
                    scores(g - 1, 1, i)
                if own:
                    query_part(g, i)
                    if g == 0:
                        pe.wait_ge(lat_ready, 2 * LT)
                    key_part(g, i)
                else:
                    wo_part(0)
                    wo_part(1)
                if g >= 1:
                    turn_probs(g - 1, 0, i)
                    turn_probs(g - 1, 1, i)
                if own:
                    value_part(g, i)
                else:
                    wo_part(2)
                if g >= 1:
                    head_output(g - 1, 0, i)
                    head_output(g - 1, 1, i)

            sum_over_partitions(4)
            pe.wait_ge(lat_ready, LT)
            slot(0)
            slot(1)
            with pe.Fori(0, HG // 2 - 1) as i:
                slot(2, i)
                slot(3, i)
            slot(HG)

            wo_part(3)
            wo_part(4, each=lambda kt: pe.wait_ge(head_split, kt // 2 + 1))
            for c in range(5, BODY):
                wo_part(c)
            with pe.Fori(0, DT // 4 - 1) as i:
                for c in range(BODY, 2 * BODY):
                    wo_part(c, i)

            ffn(1, 0, 3 * DT, 5)
            ffn(1, 1, None, None)
            pe.wait_ge(squares_added, squares_before(7))
            pe.wait_ge(root_ready, 6)
            pe.matmul(ps[:, STATS, 0:SEQ], ones[:, :], square_sum[:, :], start=True, stop=False)
            pe.wait_ge(last_square, 1)
            pe.matmul(ps[:, STATS, 0:SEQ], ones[:, :], gate_act[:, :], start=False, stop=True).then_inc(stats_summed, 1)

        @block.scalar
        def _(sc):
            def split(n, i=None):
                if n >= CHUNK["end"]:
                    return
                e = chunk_elems(n)
                src = raw[:, n % WEIGHT_SLOTS, 0:e]
                if CHUNK["kpe"] <= n < CHUNK["kpe"] + 2:
                    src = raw[:, n % WEIGHT_SLOTS, 0:TILES * ROPE].rearrange("p (k o c) -> p k o c", k=TILES, o=1)
                    src = src.broadcast_to([P, TILES, 2, ROPE])
                sc.wait_ge(landed[n % WEIGHT_SLOTS], plus(16 * (n // WEIGHT_SLOTS + 1), i, 16))
                if n >= CHUNK["up0"] + SPLIT_SLOTS:
                    sc.wait_ge(chunks_used, plus(n - SPLIT_SLOTS + 1, i, BODY))
                dst = w_hi[:, n % SPLIT_SLOTS, 0:e]
                if CHUNK["kpe"] <= n < CHUNK["kpe"] + 2:
                    dst = dst.rearrange("p (k o c) -> p k o c", k=TILES, o=2)
                nc.scalar.activation(dst, src, ACT.Copy).then_inc(hi_ready, 1)

            def root_of(k, features):
                sc.wait_ge(stats_summed, k)
                if k >= 2:
                    sc.wait_ge(rstd_ready, k - 1)
                nc.scalar.activation(root[:, :], ps[:, STATS, 0:SEQ], ACT.Sqrt, bias=eps[:, :],
                                     scale=1.0 / features).then_inc(root_ready, 1)

            def gained(t, tile_count, col, dst, i=None, per=0):
                sc.wait_ge(evacuated, plus(tile_count, i, per))
                nc.scalar.activation(dst[:, plus(t, i, per), 0:SEQ], x[:, plus(t, i, per), :], ACT.Identity,
                                     scale=gain[:, plus(col + t, i, per), :]).then_inc(xg_hi, 1)

            sc.wait_ge(init_ready, INIT)
            nc.scalar.activation(stat[:, 0, 7:8], eps[:, :], ACT.Sqrt)
            for q in range(4):
                sc.wait_ge(x_landed[q], 16)
                nc.scalar.activation(x_square[:, 4 * q:4 * q + 4, :], x[:, 4 * q:4 * q + 4, :],
                                     ACT.Square).then_inc(squares_ready, 1)
            sc.wait_ge(gain_landed, 16)
            for number, g in enumerate(POOL_ORDER):
                for t in range(g * GT, (g + 1) * GT):
                    nc.scalar.activation(normed[:, t, PAD:], x[:, t, :], ACT.Identity,
                                         scale=gain[:, G_POOL + t, :]).then_inc(pool_gained, 1)
                if number == 0:
                    root_of(1, D_MODEL)

            for t in range(DT):
                gained(t, TILE["pool"] + t + 1, G_FFN0, xg)
                if t >= 4:
                    sc.wait_ge(squares_added, t - 3)
                nc.scalar.activation(square_of(t), x[:, t, :], ACT.Square).then_inc(square_made, 1)
                if t in FIRST_SPLITS:
                    split(CHUNK["up0"] + FIRST_SPLITS.index(t))

            def ffn_tile(p, f, splits, i=None):
                n, t = CHUNK[UPS[p]] + 4 * f, TILE[UPS[p]] + 2 * f
                bank = t % 4
                sc.wait_ge(chunks_used, plus(n + 4, i, BODY))
                nc.scalar.activation(cross[:, :, :], ps[:, bank:bank + 2, SEQ:], ACT.Copy).then_inc(cross_ready, 1)
                splits[0]()
                sc.wait_ge(sums_ready, plus(p * FH + f + 1, i, 2))
                nc.scalar.activation(gate_act[:, :], sums[:, 0, :], ACT.Silu).then_inc(gate_ready, 1)
                splits[1]()
                sc.wait_ge(product_ready, plus(p * FH + f + 1, i, 2))
                nc.scalar.activation(act[:, plus(f, i, 2), 0:SEQ], product[:, :], ACT.Copy).then_inc(act_hi, 1)
                splits[2]()

            def ffn(layer, half, stats):
                p = 2 * layer + half
                n0 = CHUNK[UPS[p]]
                for w in range(3):
                    split(n0 + w + SPLIT_SLOTS)
                if stats is not None:
                    root_of(stats, D_MODEL)

                def tile(f, i=None):
                    n = n0 + 4 * f + 3 + SPLIT_SLOTS
                    ffn_tile(p, f, (lambda: split(n, i), lambda: split(n + 1, i),
                                    lambda: (split(n + 2, i), split(n + 3, i))), i)

                with sc.Fori(0, FH // 2 - 1) as i:
                    tile(0, i)
                    tile(1, i)
                tile(FH - 2)
                nothing = lambda: None
                ffn_tile(p, FH - 1, (nothing, nothing, lambda: split(n0 + 4 * FH - 1 + SPLIT_SLOTS)))

                n1, t1 = CHUNK[DOWNS[p]], TILE[DOWNS[p]]

                def down(d, i=None):
                    split(n1 + 2 * d + SPLIT_SLOTS, i)
                    if half == 1 and layer == 0:
                        gained(d, t1 + d + 1, G_ATTN, xg, i, 4)
                    if half == 1 and layer == 1:
                        if d == DT - 1:
                            nc.scalar.activation(stat[:, 0, 7:8], eps[:, :], ACT.Sqrt)
                        sc.wait_ge(evacuated, plus(t1 + d + 1, i, 4))
                        if d == DT - 1:
                            nc.scalar.activation(gate_act[:, :], x[:, d, :], ACT.Square).then_inc(last_square, 1)
                        nc.scalar.activation(y[:, plus(d, i, 4), :], x[:, plus(d, i, 4), :], ACT.Identity,
                                             scale=gain[:, plus(G_FINAL + d, i, 4), :]).then_inc(y_gained, 1)
                    split(n1 + 2 * d + 1 + SPLIT_SLOTS, i)

                with sc.Fori(0, DT // 4 - 1) as i:
                    for d in range(4):
                        down(d, i)
                for d in range(DT - 4, DT):
                    down(d)

            ffn(0, 0, 2)
            sc.wait_ge(angle_ready, 1)
            nc.scalar.activation(sin[:, :], angle[:, :], ACT.Sin).then_inc(table_ready, 1)
            nc.scalar.activation(cos[:, :], turns[:, :], ACT.Sin).then_inc(table_ready, 1)
            ffn(0, 1, None)

            xk_tiles = iter(range(DT))

            def xk_some(k):
                for _ in range(k):
                    gained(next(xk_tiles), TILE["qa"], G_KV, xk)

            def lat_pair(name, m):
                n, t = CHUNK[name] + 2 * m, TILE[name] + m
                sc.wait_ge(chunks_used, n + 4)
                sc.wait_ge(evacuated, t)
                nc.scalar.activation(cross[:, :, :], ps[:, t % 4:t % 4 + 2, SEQ:], ACT.Copy).then_inc(cross_ready, 1)

            def lat_split(which, number, col):
                for t in range(LT):
                    if t % 2 == 0:
                        sc.wait_ge(lat_scaled, 2 * number + t // 2 + 1)
                    nc.scalar.activation(latent[:, which, t, 0:SEQ], lat_raw[:, t, :], ACT.Identity,
                                         scale=gain[:, col + t, :]).then_inc(lat_hi, 1)

            n0 = CHUNK["qa"]
            for w in range(3):
                split(n0 + w + SPLIT_SLOTS)
                xk_some(2)
                if w == 1:
                    root_of(3, D_MODEL)
            lat_pair("qa", 0)
            for w in range(3, 7):
                split(n0 + w + SPLIT_SLOTS)
                xk_some(2)
            lat_pair("qa", 2)
            split(n0 + 7 + SPLIT_SLOTS)
            xk_some(2)
            for w in range(8, 11):
                split(n0 + w + SPLIT_SLOTS)
            lat_pair("kva", 0)
            split(n0 + 11 + SPLIT_SLOTS)
            root_of(4, LATENT)
            lat_split(Q, 0, G_LQ)
            split(n0 + 12 + SPLIT_SLOTS)
            split(n0 + 13 + SPLIT_SLOTS)
            split(n0 + 14 + SPLIT_SLOTS)
            lat_pair("kva", 2)
            split(n0 + 15 + SPLIT_SLOTS)
            split(n0 + 16 + SPLIT_SLOTS)

            def swap_halves(src):
                for q in range(4):
                    nc.scalar.activation(product[32 * q:32 * q + 32, :], src[32 * (q ^ 1):32 * (q ^ 1) + 32, :],
                                         ACT.Copy).then_inc(rope_swapped, 1)

            sc.wait_ge(chunks_used, CHUNK["kpe"] + 2)
            sc.wait_ge(evacuated, TILE["kpe"])
            b = TILE["kpe"] % 4
            nc.scalar.activation(cross[:, 0, :], ps[:, b, SEQ:], ACT.Copy).then_inc(cross_ready, 1)
            root_of(5, LATENT)
            sc.wait_ge(rope_sum, 1)
            swap_halves(key_raw)
            split(n0 + 17 + SPLIT_SLOTS)

            def key_hi_halves():
                sc.wait_ge(rope_done, 1)
                for hh in range(2):
                    rows = slice(64 * hh, 64 * hh + 64)
                    nc.scalar.activation(kpe_buf[rows, hh, 0:SEQ], key_raw[rows, :],
                                         ACT.Copy).then_inc(key_rope_hi, 1)

            def pair_cross(g, part, i):
                n, t = CHUNK["heads"] + 4 * g + part, TILE["heads"] + 8 * g + 2 * part
                sc.wait_ge(chunks_used, plus(n + 1, i, BODY))
                sc.wait_ge(evacuated, plus(t, i, 16))
                nc.scalar.activation(cross[:, :, :], ps[:, t % 4:t % 4 + 2, SEQ:], ACT.Copy).then_inc(cross_ready, 1)

            def pair_hi(g, part, dst, i):
                sc.wait_ge(evacuated, plus(TILE["heads"] + 8 * g + 2 * part + 2, i, 16))
                nc.scalar.activation(dst[:, g % 2, :, 0:SEQ], sums[:, :, :], ACT.Copy).then_inc(pair_hi_ready, 1)

            def value_hi(g, i):
                n, t = CHUNK["heads"] + 4 * g + 3, TILE["heads"] + 8 * g + 6
                sc.wait_ge(chunks_used, plus(n + 1, i, BODY))
                nc.scalar.activation(v_buf[:, g % 2, :, 0, :], ps[:, t % 4:t % 4 + 2, 0:2 * V_DIM],
                                     ACT.Copy).then_inc(value_hi_ready, 1)

            def rope_cross(g, i):
                n, t = CHUNK["heads"] + 4 * g, TILE["heads"] + 8 * g
                sc.wait_ge(chunks_used, plus(n + 1, i, BODY))
                sc.wait_ge(evacuated, plus(t, i, 16))
                nc.scalar.activation(cross[:, 0, :], ps[:, t % 4, SEQ:], ACT.Copy).then_inc(cross_ready, 1)

            def rope_hi(g, i):
                sc.wait_ge(rope_done, plus(g + 2, i, 2))
                nc.scalar.activation(qpe_buf[:, g % 2, 0:SEQ], gate_act[:, :],
                                     ACT.Copy).then_inc(query_rope_hi, 1)

            def probT_hi_half(g, i):
                sc.wait_ge(probT_ready, plus(2 * g + 2, i, 4))
                nc.scalar.activation(probT[:, :, 0, :], ps[:, SCORES:SCORES + 2, 0:3 * P],
                                     ACT.Copy).then_inc(probT_hi, 1)

            def heads_hi_half(g, i):
                sc.wait_ge(head_ready, plus(2 * g + 2, i, 4))
                for hh in range(2):
                    nc.scalar.activation(heads[:, plus(2 * g + hh, i, 4), 0:SEQ], ps[:, HEADS_OUT + hh, 0:SEQ],
                                         ACT.Copy).then_inc(head_hi, 1)

            def exps(g, hh, i):
                sc.wait_ge(max_ready, plus(2 * g + hh + 1, i, 4))
                nc.scalar.activation(prob[:, hh, 0:P], prob[:, hh, 0:P], ACT.Exp, bias=stat[:, hh, 2:3],
                                     accum_out=stat[:, hh, 4:5]).then_inc(exp_ready, 1)
                nc.scalar.activation(prob[:, hh, P:], prob[:, hh, P:], ACT.Exp, bias=stat[:, hh, 3:4],
                                     accum_out=stat[:, hh, 5:6]).then_inc(exp_ready, 1)

            def slot(g, i=None):
                n = CHUNK["heads"] + 4 * g
                rope_cross(g, i)
                if g == 0:
                    lat_split(KV, 1, G_LKV)
                    pair_cross(0, 1, None)
                    pair_hi(0, 1, q_buf, None)
                    key_hi_halves()
                else:
                    split(n + SPLIT_SLOTS, i)
                sc.wait_ge(evacuated, plus(TILE["heads"] + 8 * g + 2, i, 16))
                swap_halves(gate_act)
                if g == 0:
                    split(n + SPLIT_SLOTS)
                else:
                    exps(g - 1, 0, i)
                    pair_cross(g, 1, i)
                    exps(g - 1, 1, i)
                    pair_hi(g, 1, q_buf, i)
                    if g >= 2:
                        heads_hi_half(g - 2, i)
                    probT_hi_half(g - 1, i)
                pair_cross(g, 2, i)
                rope_hi(g, i)
                pair_hi(g, 2, k_buf, i)
                split(n + 1 + SPLIT_SLOTS, i)
                split(n + 2 + SPLIT_SLOTS, i)
                value_hi(g, i)
                split(n + 3 + SPLIT_SLOTS, i)

            slot(0)
            slot(1)
            with sc.Fori(0, HG // 2 - 2) as i:
                slot(2, i)
                slot(3, i)
            slot(HG - 2)
            slot(HG - 1)

            n1, t1 = CHUNK["wo"], TILE["wo"]
            heads_hi_half(HG - 2, None)
            exps(HG - 1, 0, None)
            exps(HG - 1, 1, None)
            split(n1 + SPLIT_SLOTS)
            split(n1 + 1 + SPLIT_SLOTS)
            probT_hi_half(HG - 1, None)
            split(n1 + 2 + SPLIT_SLOTS)
            heads_hi_half(HG - 1, None)
            split(n1 + 3 + SPLIT_SLOTS)

            def wo(c, i=None):
                split(n1 + c + SPLIT_SLOTS, i)
                if c // 4 % 2:
                    d = 4 * (c // BODY) + c % 4
                    gained(d, t1 + d + 1, G_FFN1, xg, i, 4)

            for c in range(4, BODY):
                wo(c)
            with sc.Fori(0, DT // 4 - 1) as i:
                for c in range(BODY, 2 * BODY):
                    wo(c, i)
            ffn(1, 0, 6)
            ffn(1, 1, None)
            root_of(7, D_MODEL)

        @block.vector
        def _(ve):
            steps = [0, None, 0]

            def step(ins):
                steps[0] += 1
                ins.then_inc(v_step, 1)
                ve.wait_ge(v_step, plus(steps[0], steps[1], steps[2]))

            def loop(count, per, body):
                with ve.Fori(0, count) as i:
                    start = steps[0]
                    steps[1:] = [i, per]
                    body(i)
                    assert steps[0] - start == per, (steps[0] - start, per)
                steps[:] = [start + per * count, None, 0]

            crossed = [0]

            def split(n, i=None):
                if n >= CHUNK["end"]:
                    return
                e = chunk_elems(n)
                src, hi, lo = raw[:, n % WEIGHT_SLOTS, 0:e], w_hi[:, n % SPLIT_SLOTS, 0:e], w_lo[:, n % SPLIT_SLOTS, 0:e]
                if CHUNK["kpe"] <= n < CHUNK["kpe"] + 2:
                    src = raw[:, n % WEIGHT_SLOTS, 0:TILES * ROPE].rearrange("p (k o c) -> p k o c", k=TILES, o=1)
                    src = src.broadcast_to([P, TILES, 2, ROPE])
                    hi = hi.rearrange("p (k o c) -> p k o c", k=TILES, o=2)
                    lo = lo.rearrange("p (k o c) -> p k o c", k=TILES, o=2)
                ve.wait_ge(hi_ready, plus(made(n), i, BODY))
                nc.vector.tensor_tensor(lo, src, hi.bitcast(F32), ALU.subtract).then_inc(lo_ready, 1)

            def rstd_of(k):
                ve.wait_ge(root_ready, k)
                nc.vector.reciprocal(rstd[:, :], root[:, :]).then_inc(rstd_ready, 1)
                ve.wait_ge(rstd_ready, k)

            xgs = [0]

            def gained(t, col, dst, number, i=None, per=0):
                ve.wait_ge(xg_hi, plus(number, i, per))
                nc.vector.scalar_tensor_tensor(
                    dst[:, plus(t, i, per), SEQ:], x[:, plus(t, i, per), :], gain[:, plus(col + t, i, per), :],
                    dst[:, plus(t, i, per), 0:SEQ].bitcast(F32), ALU.mult, ALU.subtract).then_inc(xg_ready, 1)

            def rope_angles():
                step(nc.vector.tensor_copy(turns[:, :], pos_i[:, :]))
                step(nc.vector.tensor_scalar(angle[:, :], turns[:, :], const[:, C_FREQ:C_FREQ + 1], None, ALU.mult))
                magic = 1.5 * 2.0 ** 23
                step(nc.vector.tensor_scalar(turns[:, :], angle[:, :], 1.0 / (2.0 * np.pi), None, ALU.mult))
                step(nc.vector.tensor_scalar(turns[:, :], turns[:, :], magic, None, ALU.add))
                step(nc.vector.tensor_scalar(turns[:, :], turns[:, :], -magic, None, ALU.add))
                rest = 2.0 * np.pi
                for part in range(5):
                    e = np.floor(np.log2(rest)) - 7
                    c = float(np.floor(rest / 2.0 ** e) * 2.0 ** e) if part < 4 else float(np.float32(rest))
                    rest -= c
                    step(nc.vector.scalar_tensor_tensor(angle[:, :], turns[:, :], -c, angle[:, :], ALU.mult, ALU.add))
                pi_low = 3.1415925
                step(nc.vector.tensor_scalar(angle[:, :], angle[:, :], pi_low, -pi_low, ALU.min, ALU.max))
                step(nc.vector.scalar_tensor_tensor(turns[:, :], angle[:, :], -1.0, angle[:, :], ALU.mult, ALU.max))
                nc.vector.tensor_scalar(turns[:, :], turns[:, :], -1.0, float(np.pi / 2), ALU.mult,
                                        ALU.add).then_inc(angle_ready, 1)

            for q in range(4):
                ve.wait_ge(squares_ready, q + 1)
                a, b, c = x_square[:, 4 * q:4 * q + 2, :], x_square[:, 4 * q + 2:4 * q + 4, :], x_square[:, 4 * q, :]
                step(nc.vector.tensor_tensor(a, a, b, ALU.add))
                nc.vector.tensor_tensor(c, c, x_square[:, 4 * q + 1, :], ALU.add).then_inc(quarter_ready, 1)
            ve.wait_ge(init_ready, INIT)
            ve.wait_ge(const_landed, 16)
            ve.wait_ge(gain_landed, 16)
            rstd_of(1)

            def norm_tiles(a, b, number):
                ve.wait_ge(pool_gained, number)
                r = rstd[:, :].rearrange("p (o t) -> p o t", o=1).broadcast_to([P, b - a, SEQ])
                step(nc.vector.tensor_tensor(normed[:, a:b, PAD:], normed[:, a:b, PAD:], r, ALU.mult))

            def window_sums(g, a=0, b=GT):
                src, dst, other = normed[:, g * GT + a:g * GT + b, :], win_v[:, a:b, :], win_v2[:, a:b, :]
                for k in range(g + 1):
                    reach = 1 << k
                    step(nc.vector.tensor_tensor(dst[:, :, PAD:], src[:, :, PAD:],
                                                 src[:, :, PAD - reach:PAD + SEQ - reach], ALU.add))
                    src, dst, other = dst, other, dst
                return src

            def pool_diff(g, win, number, a=0, b=GT):
                corr = const[:, C_CORR + g * PAD:C_CORR + (g + 1) * PAD].rearrange("p (o t) -> p o t", o=1)
                corr = corr.broadcast_to([P, b - a, PAD])
                step(nc.vector.tensor_tensor(win[:, :, PAD:2 * PAD], win[:, :, PAD:2 * PAD], corr, ALU.mult))
                nc.vector.scalar_tensor_tensor(pooled[:, g * GT + a:g * GT + b, :], win[:, :, PAD:], 1.0 / WINDOWS[g],
                                               normed[:, g * GT + a:g * GT + b, PAD:], ALU.mult,
                                               ALU.subtract).then_inc(diff_ready, 1)
                ve.wait_ge(diff_ready, number)

            def pool_out(*tiles):
                for t in tiles:
                    if t % 2 == 0:
                        ve.wait_ge(chunks_used, t // 2 + 1)
                    nc.vector.scalar_tensor_tensor(x[:, t, :], ps[:, t % 4, 0:SEQ], gain[:, G_SCALE + t, :],
                                                   x[:, t, :], ALU.mult, ALU.add).then_inc(evacuated, 1)

            for a in (0, GT // 2):
                b = a + GT // 2
                norm_tiles(a, b, b)
                pool_diff(0, window_sums(0, a, b), a // (GT // 2) + 1, a, b)
            norm_tiles(GT, 2 * GT, 3 * GT)
            win = window_sums(1)
            pool_diff(1, win, 3)
            pool_out(0, 1)
            ve.wait_ge(normed_ready, 1)
            win = window_sums(2)
            pool_out(2, 3)
            pool_diff(2, win, 4)
            pool_out(4, 5, 6, 7)
            ve.wait_ge(windows_ready, 1)
            pool_diff(3, win_p2, 5)
            for t in range(DT // 2):
                gained(t, G_FFN0, xg, t + 1)
            for t in range(DT // 2, DT):
                pool_out(t)
                gained(t, G_FFN0, xg, t + 1)
            ve.wait_ge(lo_ready, SPLIT_SLOTS)

            def ffn_tile(p, f, splits, i=None):
                t = TILE[UPS[p]] + 2 * f
                bank = t % 4
                ve.wait_ge(cross_ready, plus(crossed[0] + f + 1, i, 2))
                nc.vector.tensor_tensor(sums[:, :, :], ps[:, bank:bank + 2, 0:SEQ], cross[:, :, :],
                                        ALU.add).then_inc(evacuated, 2)
                ve.wait_ge(evacuated, plus(t + 2, i, 4))
                r = rstd[:, :].rearrange("p (o t) -> p o t", o=1).broadcast_to([P, 2, SEQ])
                nc.vector.tensor_tensor(sums[:, :, :], sums[:, :, :], r, ALU.mult).then_inc(sums_ready, 1)
                splits[0]()
                ve.wait_ge(gate_ready, plus(p * FH + f + 1, i, 2))
                nc.vector.tensor_tensor(product[:, :], gate_act[:, :], sums[:, 1, :], ALU.mult).then_inc(product_ready, 1)
                splits[1]()
                ve.wait_ge(act_hi, plus(p * FH + f + 1, i, 2))
                nc.vector.tensor_tensor(act[:, plus(f, i, 2), SEQ:], product[:, :],
                                        act[:, plus(f, i, 2), 0:SEQ].bitcast(F32),
                                        ALU.subtract).then_inc(act_ready, 1)
                splits[2]()

            def into_x(t, d, used, i=None, per=0):
                b = t % 4
                xd = x[:, plus(d, i, per), :]
                ve.wait_ge(chunks_used, plus(used, i, BODY))
                step(nc.vector.tensor_tensor(xd, ps[:, b, 0:SEQ], xd, ALU.add))
                nc.vector.tensor_tensor(xd, ps[:, b, SEQ:], xd, ALU.add).then_inc(evacuated, 1)

            def ffn(layer, half, stats, xg_before):
                p = 2 * layer + half
                n0 = CHUNK[UPS[p]]
                for w in range(3):
                    split(n0 + w + SPLIT_SLOTS)
                if stats is not None:
                    rstd_of(stats)

                def tile(f, i=None):
                    n = n0 + 4 * f + 3 + SPLIT_SLOTS
                    ffn_tile(p, f, (lambda: split(n, i), lambda: split(n + 1, i),
                                    lambda: (split(n + 2, i), split(n + 3, i))), i)

                with ve.Fori(0, FH // 2 - 1) as i:
                    tile(0, i)
                    tile(1, i)
                tile(FH - 2)
                nothing = lambda: None
                ffn_tile(p, FH - 1, (nothing, nothing, lambda: split(n0 + 4 * FH - 1 + SPLIT_SLOTS)))
                crossed[0] += FH

                n1, t1 = CHUNK[DOWNS[p]], TILE[DOWNS[p]]

                def down(d, i=None):
                    split(n1 + 2 * d + SPLIT_SLOTS, i)
                    into_x(t1 + d, d, n1 + 2 * d + 2, i, 4)
                    if half == 1 and layer == 0:
                        gained(d, G_ATTN, xg, xg_before + d + 1, i, 4)
                    split(n1 + 2 * d + 1 + SPLIT_SLOTS, i)

                loop(DT // 4 - 1, 4, lambda i: [down(d, i) for d in range(4)])
                for d in range(DT - 4, DT):
                    down(d)

            ffn(0, 0, 2, None)
            ve.wait_ge(pos_landed, 16)
            rope_angles()
            ffn(0, 1, None, DT)

            xk_tiles = iter(range(DT))

            def xk_some(k):
                for _ in range(k):
                    t = next(xk_tiles)
                    gained(t, G_KV, xk, 2 * DT + t + 1)

            def lat_add(name, m):
                t = TILE[name] + m
                crossed[0] += 1
                ve.wait_ge(cross_ready, crossed[0])
                if m > 0:
                    ve.wait_ge(lat_sum, 1 if name == "qa" else 3)
                nc.vector.tensor_tensor(sums[:, :, :], ps[:, t % 4:t % 4 + 2, 0:SEQ], cross[:, :, :],
                                        ALU.add).then_inc(evacuated, 2)
                ve.wait_ge(evacuated, t + 2)

            def lat_scale(m):
                r = rstd[:, :].rearrange("p (o t) -> p o t", o=1).broadcast_to([P, 2, SEQ])
                nc.vector.tensor_tensor(lat_raw[:, m:m + 2, :], sums[:, :, :], r, ALU.mult).then_inc(lat_sum, 1)

            def lat_norm(which, number, col, beside=None):
                ve.wait_ge(root_ready, 4 + number)
                nc.vector.reciprocal(lat_rstd[:, :], root[:, :]).then_inc(rstd_ready, 1)
                ve.wait_ge(rstd_ready, 4 + number)
                r = lat_rstd[:, :].rearrange("p (o t) -> p o t", o=1).broadcast_to([P, 2, SEQ])
                for m in (0, 2):
                    nc.vector.tensor_tensor(lat_raw[:, m:m + 2, :], lat_raw[:, m:m + 2, :], r,
                                            ALU.mult).then_inc(lat_scaled, 1)
                if beside is not None:
                    beside()
                for t in range(LT):
                    ve.wait_ge(lat_hi, number * LT + t + 1)
                    nc.vector.scalar_tensor_tensor(
                        latent[:, which, t, SEQ:], lat_raw[:, t, :], gain[:, col + t, :],
                        latent[:, which, t, 0:SEQ].bitcast(F32), ALU.mult, ALU.subtract).then_inc(lat_ready, 1)

            n0 = CHUNK["qa"]
            for w in range(3):
                split(n0 + w + SPLIT_SLOTS)
                xk_some(2)
                if w == 1:
                    rstd_of(3)
            lat_add("qa", 0)
            lat_scale(0)
            for w in range(3, 7):
                split(n0 + w + SPLIT_SLOTS)
                xk_some(2)
            lat_add("qa", 2)
            lat_scale(2)
            split(n0 + 7 + SPLIT_SLOTS)
            xk_some(2)
            for w in range(8, 11):
                split(n0 + w + SPLIT_SLOTS)
            lat_add("kva", 0)
            split(n0 + 11 + SPLIT_SLOTS)
            lat_norm(Q, 0, G_LQ)
            ve.wait_ge(lat_ready, LT)
            lat_scale(0)
            split(n0 + 12 + SPLIT_SLOTS)
            split(n0 + 13 + SPLIT_SLOTS)
            split(n0 + 14 + SPLIT_SLOTS)
            lat_add("kva", 2)
            lat_scale(2)
            split(n0 + 15 + SPLIT_SLOTS)
            split(n0 + 16 + SPLIT_SLOTS)
            ve.wait_ge(table_ready, 2)
            step(nc.vector.tensor_scalar(sin[:, :], sin[:, :], const[:, C_SIGN:C_SIGN + 1], None, ALU.mult))

            crossed[0] += 1
            ve.wait_ge(cross_ready, crossed[0])
            nc.vector.tensor_tensor(key_raw[:, :], ps[:, TILE["kpe"] % 4, 0:SEQ], cross[:, 0, :],
                                    ALU.add).then_inc(evacuated, 2)
            ve.wait_ge(evacuated, TILE["kpe"] + 2)
            nc.vector.tensor_tensor(key_raw[:, :], key_raw[:, :], rstd[:, :], ALU.mult).then_inc(rope_sum, 1)

            def key_rope_lo():
                for hh in range(2):
                    rows = slice(64 * hh, 64 * hh + 64)
                    ve.wait_ge(key_rope_hi, hh + 1)
                    nc.vector.tensor_tensor(kpe_buf[rows, hh, SEQ:], key_raw[rows, :],
                                            kpe_buf[rows, hh, 0:SEQ].bitcast(F32),
                                            ALU.subtract).then_inc(kpe_ready, 1)

            def pair_add(g, part, crossed_at, i):
                t = TILE["heads"] + 8 * g + 2 * part
                if part == 2:
                    ve.wait_ge(q_ready, plus(g + 1, i, 2))
                elif g >= 1:
                    ve.wait_ge(k_ready, plus(g, i, 2))
                ve.wait_ge(cross_ready, plus(crossed_at, i, 6))
                nc.vector.tensor_tensor(sums[:, :, :], ps[:, t % 4:t % 4 + 2, 0:SEQ], cross[:, :, :],
                                        ALU.add).then_inc(evacuated, 2)

            def value_lo(g, i):
                t = TILE["heads"] + 8 * g + 6
                ve.wait_ge(value_hi_ready, plus(g + 1, i, 2))
                nc.vector.tensor_tensor(v_buf[:, g % 2, :, 1, :], ps[:, t % 4:t % 4 + 2, 0:2 * V_DIM],
                                        v_buf[:, g % 2, :, 0, :].bitcast(F32), ALU.subtract).then_inc(evacuated, 2)

            def rope_add(g, crossed_at, i):
                t = TILE["heads"] + 8 * g
                if g >= 1:
                    ve.wait_ge(qpe_ready, plus(g, i, 2))
                ve.wait_ge(cross_ready, plus(crossed_at, i, 6))
                nc.vector.tensor_tensor(gate_act[:, :], ps[:, t % 4, 0:SEQ], cross[:, 0, :],
                                        ALU.add).then_inc(evacuated, 2)

            def rope_lo(g, i):
                ve.wait_ge(query_rope_hi, plus(g + 1, i, 2))
                nc.vector.tensor_tensor(qpe_buf[:, g % 2, SEQ:], gate_act[:, :], qpe_buf[:, g % 2, 0:SEQ].bitcast(F32),
                                        ALU.subtract).then_inc(qpe_ready, 1)

            def probT_lo_half(g, i):
                ve.wait_ge(probT_hi, plus(g + 1, i, 2))
                nc.vector.tensor_tensor(probT[:, :, 1, :], ps[:, SCORES:SCORES + 2, 0:3 * P],
                                        probT[:, :, 0, :].bitcast(F32), ALU.subtract).then_inc(probT_split, 1)

            def heads_lo_half(g, i):
                ve.wait_ge(head_hi, plus(2 * g + 2, i, 4))
                step(nc.vector.tensor_tensor(heads[:, plus(2 * g, i, 4), SEQ:], ps[:, HEADS_OUT, 0:SEQ],
                                             heads[:, plus(2 * g, i, 4), 0:SEQ].bitcast(F32), ALU.subtract))
                nc.vector.tensor_tensor(heads[:, plus(2 * g + 1, i, 4), SEQ:], ps[:, HEADS_OUT + 1, 0:SEQ],
                                        heads[:, plus(2 * g + 1, i, 4), 0:SEQ].bitcast(F32),
                                        ALU.subtract).then_inc(head_split, 1)

            def row_max(g, hh, i):
                ve.wait_ge(scores_ready, plus(2 * g + hh + 1, i, 4))
                nc.vector.tensor_copy(stat[:, hh, 7:8], eps[:, :])
                for qt in range(2):
                    nk = (qt + 1) * P
                    mask = const[:, C_MASK + 2 * P - nk:C_MASK + 2 * P]
                    ins = nc.vector.tensor_tensor_reduce(
                        prob[:, hh, qt * P:qt * P + nk], ps[:, SCORES + hh, qt * P:qt * P + nk], mask, ATTN_SCALE,
                        -3.0e38, ALU.add, ALU.max, stat[:, hh, qt:qt + 1])
                step(ins)
                nc.vector.tensor_scalar(stat[:, hh, 2:4], stat[:, hh, 0:2], -1.0, None, ALU.mult).then_inc(max_ready, 1)

            def normalise(g, i):
                ve.wait_ge(exp_ready, plus(4 * g + 4, i, 8))
                step(nc.vector.reciprocal(stat[:, :, 6:8], stat[:, :, 4:6]))
                for hh in range(2):
                    nc.vector.tensor_scalar(prob[:, hh, 0:P], prob[:, hh, 0:P], stat[:, hh, 6:7], None,
                                            ALU.mult).then_inc(prob_ready, 1)
                    nc.vector.tensor_scalar(prob[:, hh, P:], prob[:, hh, P:], stat[:, hh, 7:8], None,
                                            ALU.mult).then_inc(prob_ready, 1)

            crossed_heads = crossed[0]

            def slot(g, i=None):
                n, cr = CHUNK["heads"] + 4 * g, crossed_heads + 3 * g
                if g == 0:
                    lat_norm(KV, 1, G_LKV, beside=lambda: rope_add(g, cr + 1, i))
                    pair_add(g, 1, cr + 2, i)
                    split(n - 1 + SPLIT_SLOTS)
                    key_rope_lo()
                    split(n + SPLIT_SLOTS)
                else:
                    rope_add(g, cr + 1, i)
                    row_max(g - 1, 0, i)
                    row_max(g - 1, 1, i)
                    pair_add(g, 1, cr + 2, i)
                    normalise(g - 1, i)
                    split(n + SPLIT_SLOTS, i)
                    if g >= 2:
                        heads_lo_half(g - 2, i)
                    probT_lo_half(g - 1, i)
                pair_add(g, 2, cr + 3, i)
                rope_lo(g, i)
                split(n + 1 + SPLIT_SLOTS, i)
                split(n + 2 + SPLIT_SLOTS, i)
                value_lo(g, i)
                split(n + 3 + SPLIT_SLOTS, i)

            slot(0)
            slot(1)
            loop(HG // 2 - 2, 2 * 4, lambda i: (slot(2, i), slot(3, i)))
            slot(HG - 2)
            slot(HG - 1)
            crossed[0] += 3 * HG

            n1, t1 = CHUNK["wo"], TILE["wo"]
            heads_lo_half(HG - 2, None)
            row_max(HG - 1, 0, None)
            row_max(HG - 1, 1, None)
            normalise(HG - 1, None)
            split(n1 + SPLIT_SLOTS)
            split(n1 + 1 + SPLIT_SLOTS)
            probT_lo_half(HG - 1, None)
            split(n1 + 2 + SPLIT_SLOTS)
            heads_lo_half(HG - 1, None)
            split(n1 + 3 + SPLIT_SLOTS)

            def wo(c, i=None):
                d = 4 * (c // BODY) + c % 4
                if c // 4 % 2:
                    into_x(t1 + d, d, n1 + c + 1, i, 4)
                split(n1 + c + SPLIT_SLOTS, i)
                if c // 4 % 2:
                    gained(d, G_FFN1, xg, 3 * DT + d + 1, i, 4)

            for c in range(4, BODY):
                wo(c)
            loop(DT // 4 - 1, 4, lambda i: [wo(c, i) for c in range(BODY, 2 * BODY)])
            ffn(1, 0, 6, None)
            ffn(1, 1, None, None)

            rstd_of(7)
            for a, b in Y_VECTOR:
                ve.wait_ge(y_gained, b)
                r = rstd[:, :].rearrange("p (o t) -> p o t", o=1).broadcast_to([P, b - a, SEQ])
                nc.vector.tensor_tensor(y[:, a:b, :], y[:, a:b, :], r, ALU.mult).then_inc(y_done_v, 1)

        @block.gpsimd
        def _(gp):
            steps = [0, None, 0]

            def step(ins):
                steps[0] += 1
                ins.then_inc(p_step, 1)
                gp.wait_ge(p_step, plus(steps[0], steps[1], steps[2]))

            for ap, value in ((ones[:, :], 1.0), (eps[:, :], EPS), (normed[:, :, 0:PAD], 0.0),
                              (win_v[:, :, 0:PAD], 0.0), (win_v2[:, :, 0:PAD], 0.0), (win_p[:, :, 0:PAD], 0.0),
                              (win_p2[:, :, 0:PAD], 0.0), (stat[:, :, :], 0.0)):
                nc.gpsimd.memset(ap, value).then_inc(init_ready, 1)
            gp.wait_ge(init_ready, INIT)

            def window_sum(dst, src, reach):
                return nc.gpsimd.tensor_tensor(dst[:, :, PAD:], src[:, :, PAD:],
                                               src[:, :, PAD - reach:PAD + SEQ - reach], ALU.add)

            gp.wait_ge(rstd_ready, 1)
            for g, number in ((2, 2 * GT), (3, 4 * GT)):
                gp.wait_ge(pool_gained, number)
                r = rstd[:, :].rearrange("p (o t) -> p o t", o=1).broadcast_to([P, GT, SEQ])
                own = normed[:, g * GT:(g + 1) * GT, PAD:]
                nc.gpsimd.tensor_tensor(own, own, r, ALU.mult).then_inc(normed_ready, 1)
            gp.wait_ge(normed_ready, 2)
            step(window_sum(win_p, normed[:, 3 * GT:4 * GT, :], 1))
            step(window_sum(win_p2, win_p, 2))
            step(window_sum(win_p, win_p2, 4))
            window_sum(win_p2, win_p, 8).then_inc(windows_ready, 1)

            def add_square(k, src, d, i=None):
                step(nc.gpsimd.tensor_tensor(square[:, :], src, src, ALU.mult))
                nc.gpsimd.tensor_tensor(square_sum[:, :], square_sum[:, :], square[:, :],
                                        ALU.add).then_inc(squares_added, 1)
                gp.wait_ge(squares_added, plus(squares_before(k) + d + 1, i, 4))

            def start_sum(k):
                gp.wait_ge(stats_summed, k)
                step(nc.gpsimd.memset(square_sum[:, :], 0.0))

            def stream_squares(k, phase):
                start_sum(k)
                def tile(d, i=None):
                    gp.wait_ge(evacuated, plus(TILE[phase] + d + 1, i, 4))
                    add_square(k, x[:, plus(d, i, 4), :], d, i)

                start = steps[0]
                with gp.Fori(0, DT // 4 - 1) as i:
                    steps[1:] = [i, 4]
                    for d in range(4):
                        tile(d, i)
                steps[:] = [start + DT - 4, None, 0]
                for d in range(DT - 4, SQUARED[k - 1]):
                    tile(d)

            def latent_squares(k, number):
                start_sum(k)
                for d in range(LT):
                    gp.wait_ge(lat_sum, 2 * number + d // 2 + 1)
                    add_square(k, lat_raw[:, d, :], d)

            start_sum(1)
            for t in range(DT):
                gp.wait_ge(square_made, t + 1)
                nc.gpsimd.tensor_tensor(square_sum[:, :], square_sum[:, :], square_of(t),
                                        ALU.add).then_inc(squares_added, 1)
                gp.wait_ge(squares_added, t + 1)
                if t in FIRST_SPLITS:
                    n = CHUNK["up0"] + FIRST_SPLITS.index(t)
                    gp.wait_ge(hi_ready, made(n))
                    e, slot_hi = chunk_elems(n), n % SPLIT_SLOTS
                    nc.gpsimd.tensor_tensor(w_lo[:, slot_hi, 0:e], raw[:, n % WEIGHT_SLOTS, 0:e],
                                            w_hi[:, slot_hi, 0:e].bitcast(F32), ALU.subtract).then_inc(lo_ready, 1)
            stream_squares(2, "down1")
            latent_squares(3, 0)
            gp.wait_ge(chunks_used, CHUNK["kva"])
            step(nc.gpsimd.memset(kpe_buf[:, :, :].bitcast(F32), 0.0))
            latent_squares(4, 1)

            def rotate(dst, k, i=None):
                gp.wait_ge(rope_swapped, plus(4 * k, i, 8))
                nc.gpsimd.tensor_tensor(dst[:, :], dst[:, :], cos[:, :], ALU.mult)
                step(nc.gpsimd.tensor_tensor(product[:, :], product[:, :], sin[:, :], ALU.mult))
                nc.gpsimd.tensor_tensor(dst[:, :], dst[:, :], product[:, :], ALU.add).then_inc(rope_done, 1)

            def pair_lo(g, part, dst, ready, i):
                gp.wait_ge(pair_hi_ready, plus(2 * g + part, i, 4))
                nc.gpsimd.tensor_tensor(dst[:, g % 2, :, SEQ:], sums[:, :, :], dst[:, g % 2, :, 0:SEQ].bitcast(F32),
                                        ALU.subtract).then_inc(ready, 1)

            rotate(key_raw, 1)

            def slot(g, i=None):
                if g == 0:
                    pair_lo(g, 1, q_buf, q_ready, i)
                rotate(gate_act, g + 2, i)
                if g >= 1:
                    pair_lo(g, 1, q_buf, q_ready, i)
                pair_lo(g, 2, k_buf, k_ready, i)

            slot(0)
            slot(1)
            start = steps[0]
            with gp.Fori(0, HG // 2 - 1) as i:
                steps[1:] = [i, 2]
                slot(2, i)
                slot(3, i)
            steps[:] = [start + HG - 2, None, 0]

            stream_squares(5, "wo")
            stream_squares(6, "down3")

            gp.wait_ge(rstd_ready, 7)
            for a, b in Y_GPSIMD:
                gp.wait_ge(y_gained, b)
                r = rstd[:, :].rearrange("p (o t) -> p o t", o=1).broadcast_to([P, b - a, SEQ])
                nc.gpsimd.tensor_tensor(y[:, a:b, :], y[:, a:b, :], r, ALU.mult).then_inc(y_done_p, 1)


def shape_constants():
    c = np.zeros((P, C_COLS), np.float32)
    c[:, C_IDENT:C_IDENT + P] = np.eye(P)
    row, col = np.arange(P)[:, None], np.arange(P)[None, :]
    c[:, C_MASK + P:C_MASK + 2 * P] = np.where(col <= row, 0.0, -1.0e30)
    for g, w in enumerate(WINDOWS):
        c[:, C_CORR + g * PAD:C_CORR + (g + 1) * PAD] = w / np.minimum(np.arange(PAD) + 1.0, w)
    half = ROPE // 2
    freq = np.float32(10000.0) ** (-np.arange(half, dtype=np.float32) / np.float32(half))
    c[:, C_FREQ] = np.tile(freq, P // half)
    c[:, C_SIGN] = np.tile(np.repeat([-1.0, 1.0], half), P // ROPE)
    return c


def by_tiles(w, k_per_chunk, tiles_per_chunk):
    k, m = w.shape[0] // P, w.shape[1] // P
    w = w.reshape(k // k_per_chunk, k_per_chunk, P, m // tiles_per_chunk, tiles_per_chunk, P)
    return w.transpose(3, 0, 2, 4, 1, 5).reshape(-1, P, tiles_per_chunk * k_per_chunk * P)


def kernel(**inputs):
    import concourse.bacc as bacc
    from concourse.bass_utils import run_bass_kernel_spmd

    a = {k: np.asarray(v) for k, v in inputs.items()}
    feature_tiles = lambda v: v.reshape(-1, P).T
    qb = a["w_q_b"][0].reshape(LATENT, HEADS, NOPE + ROPE)
    kvb = a["w_kv_b"].reshape(LATENT, HEADS, NOPE + V_DIM)
    values = kvb[:, :, NOPE:].reshape(LT, P, HG, 2 * V_DIM)
    rope_keys = a["w_kv_a"][:, LATENT:].reshape(2, TILES, P, ROPE)
    down = a["w_down"].reshape(4 * FH * P, D_MODEL)
    arrays = {
        "xT": a["x"][0].T.reshape(DT, P, SEQ).transpose(1, 0, 2),
        "positions": a["positions"].reshape(SEQ),
        "consts": shape_constants(),
        "gains": np.concatenate([feature_tiles(v.reshape(-1)) for v in (
            a["pool_norm"], a["pool_scale"], a["kv_in_norm"], a["attn_norm"], a["ffn_norm"][0], a["ffn_norm"][1],
            a["final_norm"], a["kv_latent_norm"], a["q_latent_norm"])], axis=1)[:, :, None],
        "pool_w": np.concatenate([by_tiles(w, GT, 2) for w in a["pool_w"][0]]),
        "w_kv_a": by_tiles(a["w_kv_a"][:, :LATENT], TILES, 1),
        "w_k_pe": rope_keys.transpose(0, 2, 1, 3).reshape(2, P, TILES * ROPE),
        "w_q_a": by_tiles(a["w_q_a"][0], TILES, 1),
        "w_kv_k": by_tiles(kvb[:, :, :NOPE].reshape(LATENT, -1), LT, 2),
        "w_kv_v": values.transpose(2, 1, 0, 3).reshape(HG, P, LT * 2 * V_DIM),
        "w_q_nope": by_tiles(qb[:, :, :NOPE].reshape(LATENT, -1), LT, 2),
        "w_q_pe": by_tiles(qb[:, :, NOPE:].reshape(LATENT, -1), LT, 1),
        "w_o": by_tiles(a["w_o"][0], TILES, 1),
        "w_gate": np.concatenate([by_tiles(w, TILES, 1) for w in a["w_gate"]]),
        "w_up": np.concatenate([by_tiles(w, TILES, 1) for w in a["w_up"]]),
        "w_down": np.concatenate([by_tiles(w, DTILES, 1) for w in np.split(down, 4)]),
    }
    arrays = {k: np.ascontiguousarray(v) for k, v in arrays.items()}

    nc = bacc.Bacc("TRN2", target_bir_lowering=False, num_devices=1)
    args = [nc.dram_tensor(k, v.shape, mybir.dt.from_np(v.dtype), kind="ExternalInput").ap()
            for k, v in arrays.items()]
    out = nc.dram_tensor("out", (P, DT, SEQ), F32, kind="ExternalOutput").ap()
    trunk(nc, *args, out)
    got = run_bass_kernel_spmd(nc, [arrays], core_ids=[0]).results[0]["out"]
    return got.transpose(1, 0, 2).reshape(D_MODEL, SEQ).T.reshape(1, SEQ, D_MODEL)
```
